# Optimizing a Trainium2 kernel written in Bass

```python
import jax, jax.numpy as jnp
from jax import lax
import numpy as np

D_MODEL = 1024
BATCH = 1
SEQ = 1024
DEPTH = 1
DEC_BATCH = 8
DEC_SEQ = 8
PAST_LEN = 8192
PAGE_SIZE = 128

D_MIX = D_MODEL
D_RG = D_MIX // 2
RG_BLOCKS = 8
RG_BW = D_RG // RG_BLOCKS
RG_C = 8.0
CONV_W = 4
GDN_HEADS = 4
GDN_DV = (D_MIX - D_RG) // GDN_HEADS
GDN_DK = GDN_DV
D_QK = GDN_HEADS * GDN_DK
D_V = GDN_HEADS * GDN_DV
D_GDN_CONV = 2 * D_QK + D_V
GDN_CHUNK = 64
D_FF = -(-8 * D_MODEL // (3 * 256)) * 256
EPS = 1e-6
D_IN = 2 * D_RG + D_GDN_CONV + D_V + 2 * GDN_HEADS
SPLITS = tuple(np.cumsum([D_RG, D_RG, D_GDN_CONV, D_V, GDN_HEADS]).tolist())

kernel_name = "hybrid_rglru_gdn_step"

def rmsnorm(x, w):
    xf = x.astype(jnp.float32)
    y = xf * lax.rsqrt(jnp.mean(xf * xf, axis=-1, keepdims=True) + EPS)
    return (y * w.astype(jnp.float32)).astype(x.dtype)

def l2norm(x):
    return x * lax.rsqrt(jnp.sum(x * x, axis=-1, keepdims=True) + EPS)

def causal_conv(x, buf, w):
    T = x.shape[1]
    xp = jnp.concatenate([buf.astype(x.dtype), x], axis=1)
    y = xp[:, 0:T] * w[0]
    for j in range(1, CONV_W):
        y = y + xp[:, j:j + T] * w[j]
    return y, xp[:, -(CONV_W - 1):]

def rglru(x, h0, w_a, b_a, w_i, b_i, lam):
    B, T, _ = x.shape
    xb = x.reshape(B, T, RG_BLOCKS, RG_BW)
    gate_r = jax.nn.sigmoid(jnp.einsum("bthi,hij->bthj", xb, w_a).reshape(B, T, D_RG) + b_a)
    gate_i = jax.nn.sigmoid(jnp.einsum("bthi,hij->bthj", xb, w_i).reshape(B, T, D_RG) + b_i)
    log_a = -RG_C * gate_r * jax.nn.softplus(-lam)
    a = jnp.exp(log_a)
    u = jnp.sqrt(-jnp.expm1(2.0 * log_a)) * (gate_i * x)
    u = u.at[:, 0].add(a[:, 0] * h0)

    def combine(left, right):
        a1, b1 = left
        a2, b2 = right
        return a1 * a2, a2 * b1 + b2

    _, h = lax.associative_scan(combine, (a, u), axis=1)
    return h, h[:, -1]

def gated_delta_chunked(q, k, v, g, beta, S0):
    B, T, H, DK = k.shape
    DV = v.shape[-1]
    C = min(GDN_CHUNK, T)
    pad = (-T) % C
    N = (T + pad) // C

    def to_chunks(z):
        z = jnp.pad(z, [(0, 0), (0, pad)] + [(0, 0)] * (z.ndim - 2))
        z = jnp.moveaxis(z, 2, 1)
        return z.reshape((B, H, N, C) + z.shape[3:])

    q, k, v, g, beta = (to_chunks(z) for z in (q, k, v, g, beta))
    gc = jnp.cumsum(g, axis=-1)
    tril = jnp.tril(jnp.ones((C, C), dtype=bool))
    strict = jnp.tril(jnp.ones((C, C), dtype=bool), -1)
    decay = jnp.exp(jnp.where(tril, gc[..., :, None] - gc[..., None, :], -jnp.inf))
    kb = k * beta[..., None]
    kkt = jnp.einsum("bhnid,bhnjd->bhnij", kb, k) * decay
    A = jnp.eye(C, dtype=k.dtype) + jnp.where(strict, kkt, 0.0)
    rhs = jnp.concatenate([v * beta[..., None], kb * jnp.exp(gc)[..., None]], axis=-1)
    sol = lax.linalg.triangular_solve(A, rhs, left_side=True, lower=True, unit_diagonal=True)
    u, w = sol[..., :DV], sol[..., DV:]
    qk = jnp.einsum("bhnid,bhnjd->bhnij", q, k) * decay
    q_dec = q * jnp.exp(gc)[..., None]
    k_tail = k * jnp.exp(gc[..., -1:] - gc)[..., None]
    g_last = jnp.exp(gc[..., -1])

    xs = tuple(jnp.moveaxis(z, 2, 0) for z in (qk, u, w, q_dec, k_tail, g_last))

    def step(S, inp):
        qk_n, u_n, w_n, qd_n, kt_n, gl_n = inp
        v_new = u_n - jnp.einsum("bhcd,bhde->bhce", w_n, S)
        o = jnp.einsum("bhcd,bhde->bhce", qd_n, S) + jnp.einsum("bhij,bhje->bhie", qk_n, v_new)
        S = S * gl_n[..., None, None] + jnp.einsum("bhcd,bhce->bhde", kt_n, v_new)
        return S, o

    S, o = lax.scan(step, S0, xs)
    o = jnp.transpose(o, (1, 0, 3, 2, 4)).reshape(B, N * C, H, DV)[:, :T]
    return o, S

def trunk(x, rg_conv_s, rg_h_s, gdn_conv_s, gdn_S_s,
          norm1, w_in, rg_conv_w, rg_conv_b, rg_wa, rg_ba, rg_wi, rg_bi, rg_lambda,
          gdn_conv_w, gdn_A_log, gdn_dt_bias, gdn_norm_w, w_out,
          norm2, w_gate, w_up, w_down, final_norm):
    B, T, _ = x.shape
    new_rc, new_rh, new_gc, new_gs = [], [], [], []
    for l in range(DEPTH):
        hn = rmsnorm(x, norm1[l])
        proj = hn @ w_in[l]
        xr, yr, qkv_raw, z, rest = jnp.split(proj, SPLITS[:4], axis=-1)
        b_raw, a_raw = rest[..., :GDN_HEADS], rest[..., GDN_HEADS:]

        xc, rc_new = causal_conv(xr, rg_conv_s[l], rg_conv_w[l])
        xc = (xc + rg_conv_b[l]).astype(jnp.float32)
        h, rh_new = rglru(xc, rg_h_s[l].astype(jnp.float32), rg_wa[l], rg_ba[l], rg_wi[l], rg_bi[l], rg_lambda[l])
        out_rg = (jax.nn.gelu(yr.astype(jnp.float32)) * h).astype(x.dtype)

        qkv, gc_new = causal_conv(qkv_raw, gdn_conv_s[l], gdn_conv_w[l])
        qkv = jax.nn.silu(qkv.astype(jnp.float32))
        q, k, v = jnp.split(qkv, [D_QK, 2 * D_QK], axis=-1)
        q = l2norm(q.reshape(B, T, GDN_HEADS, GDN_DK)) * (GDN_DK ** -0.5)
        k = l2norm(k.reshape(B, T, GDN_HEADS, GDN_DK))
        v = v.reshape(B, T, GDN_HEADS, GDN_DV)
        beta = jax.nn.sigmoid(b_raw.astype(jnp.float32))
        g = -jnp.exp(gdn_A_log[l].astype(jnp.float32)) * jax.nn.softplus(a_raw.astype(jnp.float32) + gdn_dt_bias[l])
        o, S_new = gated_delta_chunked(q, k, v, g, beta, gdn_S_s[l].astype(jnp.float32))
        zh = z.astype(jnp.float32).reshape(B, T, GDN_HEADS, GDN_DV)
        out_gdn = (rmsnorm(o, gdn_norm_w[l]) * jax.nn.silu(zh)).reshape(B, T, D_V).astype(x.dtype)

        x = x + jnp.concatenate([out_rg, out_gdn], axis=-1) @ w_out[l]

        hf = rmsnorm(x, norm2[l])
        x = x + (jax.nn.silu(hf @ w_gate[l]) * (hf @ w_up[l])) @ w_down[l]

        new_rc.append(rc_new)
        new_rh.append(rh_new)
        new_gc.append(gc_new)
        new_gs.append(S_new)
    y = rmsnorm(x, final_norm)
    return y, jnp.stack(new_rc), jnp.stack(new_rh), jnp.stack(new_gc), jnp.stack(new_gs)

def setup_inputs(seed: int = 0) -> dict:
    key = jax.random.key(seed)
    ks = iter(jax.random.split(key, 40))
    nrm = lambda shape, s: jax.random.normal(next(ks), shape, jnp.float32) * s
    L = DEPTH
    a0 = jax.random.uniform(next(ks), (L, D_RG), jnp.float32, 0.9, 0.999) ** (1.0 / RG_C)
    rg_lambda = jnp.log(a0) - jnp.log1p(-a0)
    A = jax.random.uniform(next(ks), (L, GDN_HEADS), jnp.float32, 1.0, 16.0)
    return {
        "x_prompt": nrm((BATCH, SEQ, D_MODEL), 1.0),
        "x_sample": nrm((DEC_BATCH, DEC_SEQ, D_MODEL), 1.0),
        "state_rglru_conv": nrm((L, DEC_BATCH, CONV_W - 1, D_RG), 1.0),
        "state_rglru_h": nrm((L, DEC_BATCH, D_RG), 0.5),
        "state_gdn_conv": nrm((L, DEC_BATCH, CONV_W - 1, D_GDN_CONV), 1.0),
        "state_gdn_S": nrm((L, DEC_BATCH, GDN_HEADS, GDN_DK, GDN_DV), GDN_DK ** -0.5),
        "norm1": 1.0 + nrm((L, D_MODEL), 0.02),
        "w_in": nrm((L, D_MODEL, D_IN), D_MODEL ** -0.5),
        "rg_conv_w": nrm((L, CONV_W, D_RG), CONV_W ** -0.5),
        "rg_conv_b": nrm((L, D_RG), 0.01),
        "rg_wa": nrm((L, RG_BLOCKS, RG_BW, RG_BW), RG_BW ** -0.5),
        "rg_ba": nrm((L, D_RG), 0.01),
        "rg_wi": nrm((L, RG_BLOCKS, RG_BW, RG_BW), RG_BW ** -0.5),
        "rg_bi": nrm((L, D_RG), 0.01),
        "rg_lambda": rg_lambda,
        "gdn_conv_w": nrm((L, CONV_W, D_GDN_CONV), CONV_W ** -0.5),
        "gdn_A_log": jnp.log(A),
        "gdn_dt_bias": nrm((L, GDN_HEADS), 0.1),
        "gdn_norm_w": 1.0 + nrm((L, GDN_DV), 0.02),
        "w_out": nrm((L, D_MIX, D_MODEL), D_MIX ** -0.5),
        "norm2": 1.0 + nrm((L, D_MODEL), 0.02),
        "w_gate": nrm((L, D_MODEL, D_FF), D_MODEL ** -0.5),
        "w_up": nrm((L, D_MODEL, D_FF), D_MODEL ** -0.5),
        "w_down": nrm((L, D_FF, D_MODEL), D_FF ** -0.5),
        "final_norm": 1.0 + nrm((D_MODEL,), 0.02),
    }

def reference(x_prompt, x_sample, state_rglru_conv, state_rglru_h, state_gdn_conv, state_gdn_S,
              norm1, w_in, rg_conv_w, rg_conv_b, rg_wa, rg_ba, rg_wi, rg_bi, rg_lambda,
              gdn_conv_w, gdn_A_log, gdn_dt_bias, gdn_norm_w, w_out,
              norm2, w_gate, w_up, w_down, final_norm):
    weights = (norm1, w_in, rg_conv_w, rg_conv_b, rg_wa, rg_ba, rg_wi, rg_bi, rg_lambda,
               gdn_conv_w, gdn_A_log, gdn_dt_bias, gdn_norm_w, w_out,
               norm2, w_gate, w_up, w_down, final_norm)
    Bp = x_prompt.shape[0]
    dt = x_prompt.dtype
    p0_rc = jnp.zeros((DEPTH, Bp, CONV_W - 1, D_RG), dt)
    p0_rh = jnp.zeros((DEPTH, Bp, D_RG), jnp.float32)
    p0_gc = jnp.zeros((DEPTH, Bp, CONV_W - 1, D_GDN_CONV), dt)
    p0_gs = jnp.zeros((DEPTH, Bp, GDN_HEADS, GDN_DK, GDN_DV), jnp.float32)
    y_prompt, p_rc, p_rh, p_gc, p_gs = trunk(x_prompt, p0_rc, p0_rh, p0_gc, p0_gs, *weights)
    y_sample, s_rc, s_rh, s_gc, s_gs = trunk(x_sample, state_rglru_conv, state_rglru_h,
                                             state_gdn_conv, state_gdn_S, *weights)
    return (y_prompt, y_sample, p_rc, p_rh, p_gc, p_gs, s_rc, s_rh, s_gc, s_gs)


_drawn_inputs = setup_inputs


def setup_inputs(seed=0):
    import zlib

    import numpy as np

    out = dict(_drawn_inputs(seed))
    spreads = {}
    factors = {'rg_ba': 25.387,
     'rg_bi': 8.0,
     'gdn_dt_bias': 3.615,
     'gdn_norm_w': 8.0,
     'norm2': 4.303,
     'final_norm': 8.087}
    for name, (base, spread) in spreads.items():
        noise = np.random.default_rng([zlib.crc32(name.encode()), seed]).standard_normal(out[name].shape)
        drawn = base * np.exp(spread * noise) if base else spread * noise
        out[name] = __import__('jax').numpy.asarray(drawn.astype(out[name].dtype))
    for name, factor in factors.items():
        out[name] = (out[name] * factor).astype(out[name].dtype)
    return out
```

```python
import numpy as np
import concourse.bass as bass
from concourse import mybir

F32 = mybir.dt.float32
F32R = mybir.dt.float32r
ACT = mybir.ActivationFunctionType
ALU = mybir.AluOpType
AX = mybir.AxisListType.X

P = 128
D = 1024
KT = D // P
SEQ = 1024
NS, LS = 8, 8
TS = NS * LS
T = SEQ + TS
NC = SEQ // P
MT = NC + 1
R = 4
H = 4
QKV = 3 * H
FF = 2816
FT = FF // P
EPS = 1e-6
GROUPS = [(0, 364), (364, 364), (728, 360)]
HIST = 3
SROW = HIST + LS
W = HIST + SEQ + NS * SROW
WC = W - HIST
S0 = SEQ + HIST
GATE_GROUPS = [(0, 372), (372, 370), (742, 370)]
NT = 2 * R + H + QKV
LEVELS = [1, 2, 4, 8, 16, 32, 64]
SAMPLE_LEVELS = 3
BANK = 512


class Plan:

    def __init__(self, nc, at):
        self.nc, self.at = nc, at

    def __call__(self, name, shape, dt=F32):
        n = 4 * int(np.prod(shape[1:]))
        t = self.nc.alloc_sbuf_tensor_at(name, shape, dt, offset=self.at)
        self.at += (n + 31) // 32 * 32
        assert self.at <= self.nc.sbuf_usable_end, (name, self.at)
        return t


def f32(ap):
    return ap.bitcast(F32)


def sample_rows(row):
    return row[:, S0:W].rearrange("p (b r) -> p b r", r=SROW)


def loop(eng, n, body):
    body(0)
    with eng.Fori(1, n) as j:
        body(j)


def mm3(pe, out, w_hi, w_lo, x_hi, x_lo, start, stop):
    pe.matmul(out, w_hi, x_hi, start=start, stop=False)
    pe.matmul(out, w_hi, x_lo, start=False, stop=False)
    return pe.matmul(out, w_lo, x_hi, start=False, stop=stop)


def build(nc, i, o, scratch):
    A = Plan(nc, (nc.sbuf_base + 31) // 32 * 32)
    psum = [nc.alloc_psum_tensor(f"bank{b}", [P, BANK], F32) for b in range(8)]
    expo = A("expo", [P, 3 * H])
    minus_half, eps_col = expo[:, 0:1], expo[:, 2 * H:2 * H + 1]
    stat = A("stat", [P, 2])
    normw = A("normw", [P, D])
    ht_hi = A("ht_hi", [P, KT, T], F32R)
    ht_lo = A("ht_lo", [P, KT, T], F32R)
    ffn_at = A.at
    cst = A("cst", [P, 12, P])
    ident, tle, ugt, strict, ones = (cst[:, n, :] for n in range(5))
    mlow = [cst[:, 5 + n, :] for n in range(len(LEVELS))]
    cs = A("cs", [TS, 3 * TS + NS])
    tle8, ugt8, strict8, blk = cs[:, 0:TS], cs[:, TS:2 * TS], cs[:, 2 * TS:3 * TS], cs[:, 3 * TS:]
    samp_qkv = A("samp_qkv", [P, QKV, TS])
    samp_z = A("samp_z", [P, H, TS])
    samp_rg = A("samp_rg", [P, R, TS])
    beta = A("beta", [P, MT, H])
    g = A("g", [P, MT, H])
    edec = A("edec", [P, 3, MT, H])
    esamp = A("esamp", [P, NS, H])
    gnw = A("gnw", [P, 1])
    base = A.at
    B = Plan(nc, base)
    wo_hi = B("wo_hi", [P, KT, D], F32R)
    wo_lo = B("wo_lo", [P, KT, D], F32R)
    after_wo = B.at

    input_block(nc, i, o, scratch, psum, Plan(nc, after_wo), locals())
    mixer_block(nc, i, o, scratch, psum, Plan(nc, after_wo), locals())
    ffn_block(nc, i, o, scratch, psum, Plan(nc, ffn_at), locals())



def input_block(nc, i, o, scratch, psum, B, k):
    cst, cs, ident, ht_hi, ht_lo, stat, normw = (k[n] for n in ("cst", "cs", "ident", "ht_hi", "ht_lo", "stat", "normw"))
    wo_hi, wo_lo, samp_qkv, samp_z, samp_rg = (k[n] for n in ("wo_hi", "wo_lo", "samp_qkv", "samp_z", "samp_rg"))
    beta, g, edec, esamp, minus_half, eps_col, gnw = (k[n] for n in ("beta", "g", "edec", "esamp", "minus_half", "eps_col", "gnw"))
    tle, ugt, ones, tle8, ugt8, blk = (k[n] for n in ("tle", "ugt", "ones", "tle8", "ugt8", "blk"))
    w_raw = [B(f"w_raw{s}", [P, KT, P]) for s in range(2)]
    w_hi = [B(f"w_hi{s}", [P, KT, P], F32R) for s in range(2)]
    w_lo = [B(f"w_lo{s}", [P, KT, P], F32R) for s in range(2)]
    rg_par = B("rg_par", [P, 8, R])
    rg_calc = B("rg_calc", [P, 3, R])
    rg_now = B("rg_now", [P, 3])
    rg_h0 = B("rg_h0", [P, R, NS])
    hist_rg = B("hist_rg", [P, R, NS * HIST])
    hist_g = B("hist_g", [P, QKV, NS * HIST])
    st_rg = B("st_rg", [P, R, (1 + NS) * HIST])
    st_h = B("st_h", [P, R, 1 + NS])
    st_g = B("st_g", [P, QKV, (1 + NS) * HIST])
    conv_w = B("conv_w", [P, QKV, 4])
    alog = B("alog", [P, 2 * H])
    rg_w = B("rg_w", [P, 2, P])
    NSP = MT * H + R
    sp = B("sp", [P, 5, NSP])
    graw = B("graw", [P, MT, 2 * H])
    gblk = B("gblk", [TS, NS, H])
    top = B.at
    B = Plan(nc, k["base"])
    xin = [B(f"xin{s}", [P, D]) for s in range(2)]
    xn = [B(f"xn{s}", [P, D]) for s in range(2)]
    gw_raw = B("gw_raw", [P, KT, 2 * H])
    gw_hi = B("gw_hi", [P, KT, 2 * H], F32R)
    gw_lo = B("gw_lo", [P, KT, 2 * H], F32R)
    gt = B("gt", [2 * H, T])
    B = Plan(nc, k["base"])
    rb_x, rb_xc, rb_gy, rb_r, rb_i, rb_t, rb_sq, rb_h = (
        B(f"rb_{n}", [P, W]) for n in ("x", "xc", "gy", "r", "i", "t", "sq", "h"))
    rb_tmp = B("rb_tmp", [P, NS])
    B = Plan(nc, top)
    cb_x = [B(f"cb_x{s}", [P, W]) for s in range(2)]
    cb_y = [B(f"cb_y{s}", [P, W]) for s in range(2)]
    wo_raw = [B(f"wo_raw{s}", [P, D]) for s in range(2)]

    S = nc.alloc_semaphore
    const_in, x_in = S("const_in"), [S(f"x_in{s}") for s in range(2)]
    ssq, rstd, xn_done = S("in_ssq"), S("in_rstd"), S("xn_done")
    xt_done, ht_hi_done, xt_free = S("xt_done"), S("ht_hi_done"), [S(f"xt_free{s}") for s in range(2)]
    gw_in, gw_hi_done, gw_lo_done = S("gw_in"), S("gw_hi_done"), S("gw_lo_done")
    gate_proj, gate_evac, gate_tok = S("gate_proj"), S("gate_evac"), S("gate_tok")
    graw_done, sp_arg, exp_done, beta_done = S("graw_done"), S("sp_arg"), S("exp_done"), S("beta_done")
    chain, pool_ms, g_done, decays, edec_done = S("dve_chain"), S("in_ms"), S("g_done"), S("decays"), S("edec_done")
    w_in, w_hi_done, w_lo_done = [S(f"w_in{s}") for s in range(2)], S("w_hi_done"), S("w_lo_done")
    proj, evac_done = S("proj_done"), S("evac_done")
    rg_init, rg_hist, rg_state = S("rg_init"), S("rg_hist"), S("rg_state")
    rg_conv, rg_w_in, gate_mm, rg_tanh = S("rg_conv"), S("rg_w_in"), S("gate_mm"), S("rg_tanh")
    rg_t, rg_sq, rg_vec, rg_out = S("rg_t"), S("rg_sq"), S("rg_vec"), S("rg_out")
    z_out, wo_in = [S(f"z_out{s}") for s in range(2)], [S(f"wo_in{s}") for s in range(2)]
    wo_hi_done, wo_lo_done = S("wo_hi_done"), S("wo_lo_done")
    cb_init, cb_hist, cb_state = S("cb_init"), S("cb_hist"), S("cb_state")
    cb_conv, cb_silu, cb_out = S("cb_conv"), S("cb_silu"), [S(f"cb_out{s}") for s in range(2)]
    st_out = S("st_out")
    consts = ((cst[:, :, :], "cst"), (cs[:, :], "cs"), (normw[:, :], "norm1"), (rg_par[:, :, :], "rg_par"),
              (rg_h0[:, :, :], "rg_h0"), (hist_rg[:, :, :], "hist_rg"), (hist_g[:, :, :], "hist_g"),
              (conv_w[:, :, :], "conv_w"), (alog[:, :], "alog"), (gnw[:, :], "gnw"), (k["expo"][:, :], "expo"))
    NCONST = 16 * len(consts)
    VEC = 14
    PAIRS = QKV // 2
    TZ, TQ = 2 * R, 2 * R + H

    def bank(s, n):
        return psum[3 * s + n]

    def sample_bank(s):
        a = GROUPS[-1][0]
        return bank(s, 2)[:, SEQ - a:T - a]

    def by_sample(ap):
        return ap.rearrange("p (b l) -> p b l", l=LS)

    with nc.Block() as block:

        @block.sync
        def _(eng):
            eng.dma_start(xin[0][:, :], i["x"][0:P, :]).then_inc(x_in[0], 16)
            for dst, name in consts:
                eng.dma_start(dst, i[name]).then_inc(const_in, 16)
            eng.dma_start(xin[1][:, :], i["x"][P:2 * P, :]).then_inc(x_in[1], 16)
            eng.dma_start(gw_raw[:, :, :], i["w_gates"]).then_inc(gw_in, 16)
            for s in range(2):
                eng.dma_start(w_raw[s][:, :, :], i["w_in"][s]).then_inc(w_in[s], 16)
            for m in range(2, MT):
                eng.wait_ge(xn_done, m - 1)
                n = P if m < NC else TS
                eng.dma_start(xin[m % 2][0:n, :], i["x"][m * P:m * P + n, :]).then_inc(x_in[m % 2], 16)

            def load_w(t, s):
                eng.wait_ge(w_hi_done, t + 1)
                eng.wait_ge(w_lo_done, t + 1)
                eng.dma_start(w_raw[s][:, :, :], i["w_in"][bass.ds(t + 2, 1)].squeeze(0)).then_inc(w_in[s], 16)

            def body1(j):
                eng.wait_ge(gate_mm, 6 * j)
                eng.dma_start(rg_w[:, :, :], i["rg_w"][bass.ds(j, 1)].squeeze(0)).then_inc(rg_w_in, 16)
                load_w(2 * j, 0)
                load_w(2 * j + 1, 1)
                eng.wait_ge(rg_vec, VEC * (j + 1))
                eng.dma_start(scratch["rg"][bass.ds(j, 1)].squeeze(0), rb_gy[:, 0:SEQ]).then_inc(rg_out, 16)

            loop(eng, R, body1)
            eng.wait_ge(rg_out, 16 * R)
            def body2(j):
                for s in range(2):
                    for n in range(2):
                        eng.wait_ge(wo_hi_done, 4 * j + 2 * s)
                        eng.wait_ge(wo_lo_done, 4 * j + 2 * s)
                        eng.dma_start(wo_raw[n][:, :],
                                      i["w_out"][bass.ds(4 * j + 2 * s + n, 1)].squeeze(0)).then_inc(wo_in[n], 16)
                    load_w(TZ + 2 * j + s, s)
                for s in range(2):
                    eng.wait_ge(evac_done, TZ + 2 * j + s + 2)
                    eng.dma_start(scratch["z"][bass.ds(2 * j + s, 1)].squeeze(0),
                                  cb_y[s][:, 0:SEQ]).then_inc(z_out[s], 16)

            loop(eng, H // 2, body2)

            def qkv(j, prefetch):
                for s in range(2):
                    if prefetch:
                        load_w(TQ + 2 * j + s, s)
                for s in range(2):
                    eng.wait_ge(cb_silu, 2 * j + s + 1)
                    eng.dma_start(scratch["qkv"][bass.ds(2 * j + s, 1)].squeeze(0),
                                  cb_y[s][:, 0:SEQ]).then_inc(cb_out[s], 16)

            loop(eng, PAIRS - 1, lambda j: qkv(j, True))
            qkv(PAIRS - 1, False)
            eng.wait_ge(rg_state, 2 * R)
            eng.wait_ge(rg_vec, VEC * R)
            eng.wait_ge(cb_state, 2 * QKV)
            for name, src in (("st_rg", st_rg), ("st_h", st_h), ("st_g", st_g)):
                eng.dma_start(o[name], src[:, :, :]).then_inc(st_out, 16)
            eng.wait_ge(st_out, 48)
            for s in range(2):
                eng.wait_ge(z_out[s], 16 * H // 2)
                eng.wait_ge(cb_out[s], 16 * PAIRS)

        @block.tensor
        def _(eng):
            eng.wait_ge(const_in, NCONST)

            def transposes(s, n):
                for half in range(2):
                    for kk in range(4):
                        f = 4 * half + kk
                        mm = eng.transpose(bank(s, half)[:, kk * P:kk * P + n],
                                           xn[s][0:n, f * P:(f + 1) * P], ident[0:n, 0:n])
                    mm.then_inc(xt_done, 1)

            def body4(j):
                for s in range(2):
                    eng.wait_ge(xn_done, 2 * j + s + 1)
                    eng.wait_ge(xt_free[s], j)
                    transposes(s, P)

            loop(eng, NC // 2, body4)
            eng.wait_ge(xn_done, MT)
            eng.wait_ge(xt_free[0], NC // 2)
            transposes(0, TS)
            for s in range(2):
                eng.wait_ge(xt_free[s], NC // 2 + 1 - s)
            eng.wait_ge(gw_hi_done, 1)
            eng.wait_ge(gw_lo_done, 1)
            for n, (a, m) in enumerate(GROUPS):
                for f in range(KT):
                    mm = mm3(eng, bank(1, n)[0:2 * H, 0:m], gw_hi[:, f, :], gw_lo[:, f, :],
                             ht_hi[:, f, a:a + m], ht_lo[:, f, a:a + m], f == 0, f == KT - 1)
                mm.then_inc(gate_proj, 1)
            eng.wait_ge(evac_done, 1)
            for m in range(MT):
                n = P if m < NC else TS
                mm = eng.transpose(psum[6][0:n, m * 2 * H:(m + 1) * 2 * H], gt[:, m * P:m * P + n],
                                   ident[0:2 * H, 0:2 * H])
            mm.then_inc(gate_tok, 1)

            def project(t, s):
                eng.wait_ge(w_hi_done, t + 1)
                eng.wait_ge(w_lo_done, t + 1)
                eng.wait_ge(evac_done, t)
                for n, (a, m) in enumerate(GROUPS):
                    for f in range(KT):
                        mm = mm3(eng, bank(s, n)[:, 0:m], w_hi[s][:, f, :], w_lo[s][:, f, :],
                                 ht_hi[:, f, a:a + m], ht_lo[:, f, a:a + m], f == 0, f == KT - 1)
                    mm.then_inc(proj, 1)

            eng.wait_ge(graw_done, 1)
            def body5(j):
                for s in range(2):
                    project(2 * j + s, s)
                eng.wait_ge(rg_conv, 4 * (j + 1))
                eng.wait_ge(rg_w_in, 16 * (j + 1))
                for n, (a, m) in enumerate(GATE_GROUPS):
                    for q in range(2):
                        eng.wait_ge(rg_tanh, 6 * j + max(0, 2 * n + q - 1))
                        eng.matmul(psum[6 + q][:, 0:m], rg_w[:, q, :], rb_xc[:, a:a + m],
                                   start=True, stop=True).then_inc(gate_mm, 1)

            loop(eng, R, body5)
            eng.wait_ge(g_done, 2)
            eng.wait_ge(rg_tanh, 6 * R)
            gp = g[:, 0:NC, :].rearrange("p c h -> p (c h)")
            n, full = NC * H, MT * H
            for q, m in enumerate((tle, ugt, ones)):
                eng.matmul(psum[6][:, q * full:q * full + n], m, gp, start=True, stop=True)
            for q, m in enumerate((tle8, ugt8)):
                eng.matmul(psum[6][0:TS, q * full + n:(q + 1) * full], m, g[0:TS, NC, :], start=True, stop=True)
            eng.matmul(psum[7][:, 0:NS * H], ones[0:TS, :], gblk[:, :, :].rearrange("p b h -> p (b h)"),
                       start=True, stop=True).then_inc(decays, 1)
            def body6(j):
                for s in range(2):
                    project(TZ + 2 * j + s, s)

            loop(eng, H // 2, body6)
            def body7(j):
                for s in range(2):
                    project(TQ + 2 * j + s, s)

            loop(eng, PAIRS, body7)

        @block.scalar
        def _(eng):
            eng.wait_ge(const_in, NCONST)

            def norm_tile(m, s, load, n, toks):
                eng.wait_ge(x_in[s], 16 * load)
                eng.wait_ge(xn_done, m)
                eng.activation(xn[s][0:n, :], xin[s][0:n, :], ACT.Square, scale=D ** -0.5,
                               accum_out=stat[0:n, 0:1]).then_inc(ssq, 1)
                for half in range(2):
                    eng.wait_ge(xt_done, 2 * m + half + 1)
                    eng.activation(ht_hi[:, 4 * half:4 * half + 4, toks],
                                   bank(s, half)[:, :].rearrange("p (f t) -> p f t", t=P)[:, :, 0:n],
                                   ACT.Copy).then_inc(ht_hi_done, 1)

            def body8(j):
                for s in range(2):
                    norm_tile(2 * j + s, s, j + 1, P, bass.ds(2 * P * j + s * P, P))

            loop(eng, NC // 2, body8)
            norm_tile(NC, 0, NC // 2 + 1, TS, slice(SEQ, T))
            eng.wait_ge(gw_in, 16)
            eng.activation(gw_hi[:, :, :], gw_raw[:, :, :], ACT.Copy).then_inc(gw_hi_done, 1)

            for s in range(2):
                eng.wait_ge(w_in[s], 16)
                eng.activation(w_hi[s][:, :, :], w_raw[s][:, :, :], ACT.Copy).then_inc(w_hi_done, 1)
            for n, (a, m) in enumerate(GROUPS):
                eng.wait_ge(gate_proj, n + 1)
                ins = eng.activation(gt[:, a:a + m], bank(1, n)[0:2 * H, 0:m], ACT.Copy)
            ins.then_inc(evac_done, 1)
            eng.wait_ge(sp_arg, 1)
            eng.activation(sp[:, 1, :], sp[:, 1, :], ACT.Exp, scale=-1.0)
            eng.activation(alog[:, 0:H], alog[:, 0:H], ACT.Exp).then_inc(exp_done, 1)
            eng.activation(beta[:, :, :], graw[:, :, 0:H], ACT.Sigmoid).then_inc(beta_done, 1)

            def split_next(t, s, load):
                eng.wait_ge(w_in[s], 16 * load)
                eng.activation(w_hi[s][:, :, :], w_raw[s][:, :, :], ACT.Copy).then_inc(w_hi_done, 1)

            eng.wait_ge(rg_init, 1)
            eng.wait_ge(g_done, 2)
            def body9(j):
                eng.wait_ge(rg_conv, 4 * j)
                eng.wait_ge(rg_state, 2 * j)
                for n, (a, m) in enumerate(GROUPS):
                    e = min(a + m, SEQ)
                    eng.wait_ge(proj, 6 * j + n + 1)
                    eng.activation(rb_x[:, HIST + a:HIST + e], bank(0, n)[:, 0:e - a], ACT.Copy)
                eng.activation(sample_rows(rb_x)[:, :, HIST:SROW], by_sample(sample_bank(0)),
                               ACT.Copy).then_inc(evac_done, 1)
                split_next(2 * j, 0, j + 2)
                eng.wait_ge(rg_out, 16 * j)
                eng.wait_ge(rg_vec, VEC * j)
                for n, (a, m) in enumerate(GROUPS):
                    e = min(a + m, SEQ)
                    eng.wait_ge(proj, 6 * j + n + 4)
                    eng.activation(rb_gy[:, a:e], bank(1, n)[:, 0:e - a], ACT.Gelu_apprx_tanh)
                eng.activation(sample_rows(rb_gy)[:, :, 0:LS], by_sample(sample_bank(1)),
                               ACT.Gelu_apprx_tanh).then_inc(evac_done, 1)
                split_next(2 * j + 1, 1, j + 2)
                for n, (a, m) in enumerate(GATE_GROUPS):
                    for q, row in enumerate((rb_r, rb_i)):
                        eng.wait_ge(gate_mm, 6 * j + 2 * n + q + 1)
                        eng.activation(row[:, a:a + m], psum[6 + q][:, 0:m], ACT.Tanh, scale=0.5,
                                       bias=rg_now[:, q:q + 1]).then_inc(rg_tanh, 1)
                eng.wait_ge(rg_tanh, 6 * j + 6)
                eng.activation(rb_t[:, 0:WC], rb_r[:, 0:WC], ACT.Tanh, scale=rg_now[:, 2:3], bias=rg_now[:, 2:3]).then_inc(rg_t, 1)
                eng.wait_ge(rg_t, j + 1)
                eng.activation(rb_sq[:, 0:WC], rb_t[:, 0:WC], ACT.Sqrt).then_inc(rg_sq, 1)

            loop(eng, R, body9)
            eng.wait_ge(decays, 1)
            n, full = NC * H, MT * H
            eng.activation(edec[:, :, 0:NC, :].rearrange("p q c h -> p q (c h)"),
                           psum[6][:, 0:3 * full].rearrange("p (q n) -> p q n", n=full)[:, :, 0:n], ACT.Exp)
            eng.activation(edec[0:TS, 0:2, NC, :],
                           psum[6][0:TS, 0:2 * full].rearrange("p (q n) -> p q n", n=full)[:, :, n:], ACT.Exp)
            eng.activation(esamp[:, :, :].rearrange("p b h -> p (b h)"), psum[7][:, 0:NS * H], ACT.Exp)
            eng.wait_ge(rg_vec, VEC * R)
            eng.wait_ge(rg_state, 2 * R)
            eng.wait_ge(rg_out, 16 * R)
            def body10(j):
                for s in range(2):
                    eng.wait_ge(z_out[s], 16 * j)
                    for n, (a, m) in enumerate(GROUPS):
                        e = min(a + m, SEQ)
                        eng.wait_ge(proj, 3 * TZ + 6 * j + 3 * s + n + 1)
                        eng.activation(cb_y[s][:, a:e], bank(s, n)[:, 0:e - a], ACT.Silu)
                    eng.activation(samp_z[:, bass.ds(2 * j + s, 1), :].squeeze(1), sample_bank(s),
                                   ACT.Silu).then_inc(evac_done, 1)
                    split_next(TZ + 2 * j + s, s, R + j + 2)
                    for n in range(2):
                        eng.wait_ge(wo_in[n], 16 * (2 * j + s + 1))
                        eng.activation(wo_hi[:, bass.ds(4 * j + 2 * s + n, 1), :].squeeze(1), wo_raw[n][:, :],
                                       ACT.Copy).then_inc(wo_hi_done, 1)

            loop(eng, H // 2, body10)

            def qkv(j, prefetch):
                for s in range(2):
                    eng.wait_ge(cb_conv, 8 * j + 4 * s)
                    eng.wait_ge(cb_state, 4 * j + 2 * s)
                    for n, (a, m) in enumerate(GROUPS):
                        e = min(a + m, SEQ)
                        eng.wait_ge(proj, 3 * TQ + 6 * j + 3 * s + n + 1)
                        eng.activation(cb_x[s][:, HIST + a:HIST + e], bank(s, n)[:, 0:e - a], ACT.Copy)
                    eng.activation(sample_rows(cb_x[s])[:, :, HIST:SROW], by_sample(sample_bank(s)),
                                   ACT.Copy).then_inc(evac_done, 1)
                    if prefetch:
                        split_next(TQ + 2 * j + s, s, R + H // 2 + j + 2)
                    eng.wait_ge(cb_conv, 8 * j + 4 * (s + 1))
                    eng.activation(by_sample(samp_qkv[:, bass.ds(2 * j + s, 1), :].squeeze(1)),
                                   sample_rows(cb_y[s])[:, :, 0:LS], ACT.Silu)
                    eng.activation(cb_y[s][:, 0:SEQ], cb_y[s][:, 0:SEQ], ACT.Silu).then_inc(cb_silu, 1)

            loop(eng, PAIRS - 1, lambda j: qkv(j, True))
            qkv(PAIRS - 1, False)

        @block.vector
        def _(eng):
            eng.wait_ge(const_in, NCONST)

            def norm_tile(m, s, n, toks):
                eng.wait_ge(rstd, m + 1)
                eng.scalar_tensor_tensor(out=xn[s][0:n, :], in0=xin[s][0:n, :], scalar=stat[0:n, 1:2],
                                         in1=normw[0:n, :], op0=ALU.mult, op1=ALU.mult).then_inc(xn_done, 1)
                for half in range(2):
                    eng.wait_ge(ht_hi_done, 2 * m + half + 1)
                    ins = eng.tensor_tensor(ht_lo[:, 4 * half:4 * half + 4, toks],
                                            bank(s, half)[:, :].rearrange("p (f t) -> p f t", t=P)[:, :, 0:n],
                                            f32(ht_hi[:, 4 * half:4 * half + 4, toks]), ALU.subtract)
                ins.then_inc(xt_free[s], 1)

            def body12(j):
                for s in range(2):
                    norm_tile(2 * j + s, s, P, bass.ds(2 * P * j + s * P, P))

            loop(eng, NC // 2, body12)
            norm_tile(NC, 0, TS, slice(SEQ, T))
            eng.wait_ge(gw_hi_done, 1)
            eng.tensor_tensor(gw_lo[:, :, :], gw_raw[:, :, :], f32(gw_hi[:, :, :]), ALU.subtract).then_inc(gw_lo_done, 1)

            def split_w(t, s):
                eng.wait_ge(w_hi_done, t + 1)
                eng.tensor_tensor(w_lo[s][:, :, :], w_raw[s][:, :, :], f32(w_hi[s][:, :, :]),
                                  ALU.subtract).then_inc(w_lo_done, 1)

            for s in range(2):
                split_w(s, s)
            count = [0]

            def step(ins):
                ins.then_inc(chain, 1)
                count[0] += 1
                eng.wait_ge(chain, count[0])

            step(eng.memset(graw[TS:P, NC, :], 0.0))
            eng.wait_ge(gate_tok, 1)
            eng.tensor_copy(graw[:, 0:NC, :].rearrange("p c h -> p (c h)"), psum[6][:, 0:NC * 2 * H])
            eng.tensor_copy(graw[0:TS, NC, :], psum[6][0:TS, NC * 2 * H:MT * 2 * H]).then_inc(graw_done, 1)
            eng.wait_ge(graw_done, 1)
            n = MT * H
            step(eng.tensor_tensor(sp[:, 0, 0:n].rearrange("p (c h) -> p c h", h=H), graw[:, :, H:2 * H],
                                   alog[:, H:2 * H].unsqueeze(1).to_broadcast([P, MT, H]), ALU.add))
            step(eng.tensor_scalar(sp[:, 0, n:], rg_par[:, 7, :], -1.0, None, ALU.mult))
            eng.scalar_tensor_tensor(out=sp[:, 1, :], in0=sp[:, 0, :], scalar=-1.0, in1=sp[:, 0, :],
                                     op0=ALU.mult, op1=ALU.max).then_inc(sp_arg, 1)
            eng.memset(rb_x[:, 0:HIST], 0.0)
            eng.memset(rb_gy[:, :], 0.0).then_inc(rg_init, 1)
            x, e, z, z2, acc = (sp[:, n, :] for n in range(5))
            eng.wait_ge(exp_done, 1)
            step(eng.tensor_scalar(z2, e, 2.0, None, ALU.add))
            step(eng.reciprocal(z2, z2))
            step(eng.tensor_tensor(z, e, z2, ALU.mult))
            step(eng.tensor_tensor(z2, z, z, ALU.mult))
            step(eng.tensor_scalar(acc, z2, 1 / 15, 1 / 13, ALU.mult, ALU.add))
            for c in (11, 9, 7, 5, 3, 1):
                step(eng.tensor_tensor(acc, acc, z2, ALU.mult))
                step(eng.tensor_scalar(acc, acc, 1 / c, None, ALU.add))
            step(eng.tensor_tensor(acc, acc, z, ALU.mult))
            step(eng.tensor_scalar(z, x, 0.0, None, ALU.max))
            step(eng.scalar_tensor_tensor(out=acc, in0=acc, scalar=2.0, in1=z, op0=ALU.mult, op1=ALU.add))
            n = MT * H
            eng.tensor_scalar(rg_calc[:, 0:2, :], rg_par[:, 5:7, :], 0.5, None, ALU.mult)
            eng.tensor_scalar(rg_calc[:, 2, :], acc[:, n:], 2.0, None, ALU.mult)
            eng.scalar_tensor_tensor(out=g[:, :, :], in0=acc[:, 0:n].rearrange("p (c h) -> p c h", h=H), scalar=-1.0,
                                     in1=alog[:, 0:H].unsqueeze(1).to_broadcast([P, MT, H]),
                                     op0=ALU.mult, op1=ALU.mult).then_inc(g_done, 1)
            eng.wait_ge(g_done, 1)
            eng.tensor_tensor(gblk[:, :, :], g[0:TS, NC, :].unsqueeze(1).to_broadcast([TS, NS, H]),
                              blk.unsqueeze(2).to_broadcast([TS, NS, H]), ALU.mult).then_inc(g_done, 1)

            def conv(dst, src, taps, bias, sem, done):
                if bias is None:
                    eng.tensor_scalar(dst, src[:, 0:WC], taps(0), None, ALU.mult).then_inc(sem, 1)
                else:
                    eng.tensor_scalar(dst, src[:, 0:WC], taps(0), bias, ALU.mult, ALU.add).then_inc(sem, 1)
                for q in range(1, 4):
                    eng.wait_ge(sem, done + q)
                    eng.scalar_tensor_tensor(out=dst, in0=src[:, q:q + WC], scalar=taps(q), in1=dst,
                                             op0=ALU.mult, op1=ALU.add).then_inc(sem, 1)

            def body13(j):
                one = bass.ds(j, 1)
                eng.wait_ge(evac_done, 2 * j + 2)
                eng.wait_ge(rg_hist, j + 1)
                eng.wait_ge(rg_sq, j)
                eng.tensor_copy(rg_now[:, :], rg_calc[:, :, one].squeeze(2))
                conv(rb_xc[:, 0:WC], rb_x, lambda q: rg_par[:, q, one], rg_par[:, 4, one], rg_conv, 4 * j)
                split_w(2 * j + 2, 0)
                split_w(2 * j + 3, 1)
                n = [0]

                def vec(ins, last=False):
                    ins.then_inc(rg_vec, 1)
                    n[0] += 1
                    if not last:
                        eng.wait_ge(rg_vec, VEC * j + n[0])

                u, a_, q_ = rb_xc[:, 0:WC], rb_t[:, 0:WC], rb_i[:, 0:WC]
                eng.wait_ge(rg_sq, j + 1)
                vec(eng.tensor_scalar(rb_r[:, 0:WC], a_, 1.0, None, ALU.add))
                vec(eng.reciprocal(rb_r[:, 0:WC], rb_r[:, 0:WC]))
                vec(eng.tensor_scalar(a_, rb_r[:, 0:WC], 2.0, -1.0, ALU.mult, ALU.add))
                vec(eng.scalar_tensor_tensor(out=q_, in0=q_, scalar=1.0, in1=u, op0=ALU.add, op1=ALU.mult))
                vec(eng.tensor_tensor(rb_sq[:, 0:WC], rb_sq[:, 0:WC], rb_r[:, 0:WC], ALU.mult))
                vec(eng.tensor_tensor(u, q_, rb_sq[:, 0:WC], ALU.mult))
                first = lambda row: sample_rows(row)[:, :, 0]
                vec(eng.tensor_tensor(rb_tmp[:, :], first(rb_t), rg_h0[:, one, :].squeeze(1), ALU.mult))
                vec(eng.tensor_tensor(first(rb_xc), first(rb_xc), rb_tmp[:, :], ALU.add))
                vec(eng.memset(first(rb_t), 0.0))
                vec(eng.tensor_tensor_scan(rb_h[:, 0:WC], a_, u, 0.0, ALU.mult, ALU.add))
                vec(eng.tensor_copy(st_h[:, one, 0:1].squeeze(1), rb_h[:, SEQ - 1:SEQ]), True)
                vec(eng.tensor_copy(st_h[:, one, 1:].squeeze(1), sample_rows(rb_h)[:, :, LS - 1]), True)
                vec(eng.tensor_tensor(by_sample(samp_rg[:, one, :].squeeze(1)), sample_rows(rb_gy)[:, :, 0:LS],
                                      sample_rows(rb_h)[:, :, 0:LS], ALU.mult), True)
                vec(eng.tensor_tensor(rb_gy[:, 0:SEQ], rb_gy[:, 0:SEQ], rb_h[:, 0:SEQ], ALU.mult), True)

            loop(eng, R, body13)
            eng.wait_ge(rg_out, 16 * R)
            eng.wait_ge(rg_state, 2 * R)
            for s in range(2):
                eng.memset(cb_x[s][:, 0:HIST], 0.0).then_inc(cb_init, 1)
            def body14(j):
                for s in range(2):
                    split_w(TZ + 2 * j + s + 2, s)
                    for n in range(2):
                        eng.wait_ge(wo_hi_done, 4 * j + 2 * s + n + 1)
                        eng.tensor_tensor(wo_lo[:, bass.ds(4 * j + 2 * s + n, 1), :].squeeze(1), wo_raw[n][:, :],
                                          f32(wo_hi[:, bass.ds(4 * j + 2 * s + n, 1), :].squeeze(1)),
                                          ALU.subtract).then_inc(wo_lo_done, 1)

            loop(eng, H // 2, body14)

            def qkv(j, prefetch):
                for s in range(2):
                    eng.wait_ge(evac_done, TQ + 2 * j + s + 2)
                    eng.wait_ge(cb_hist, 2 * j + s + 1)
                    eng.wait_ge(cb_out[s], 16 * j)
                    eng.wait_ge(cb_silu, 2 * j)
                    row = bass.ds(2 * j + s, 1)
                    conv(cb_y[s][:, 0:WC], cb_x[s], lambda q: conv_w[:, row, q], None, cb_conv, 8 * j + 4 * s)
                    if prefetch:
                        split_w(TQ + 2 * j + s + 2, s)

            for s in range(2):
                eng.wait_ge(z_out[s], 16 * H // 2)
            loop(eng, PAIRS - 1, lambda j: qkv(j, True))
            qkv(PAIRS - 1, False)

        @block.gpsimd
        def _(eng):
            eng.wait_ge(const_in, NCONST)

            def norm_tile(m, n):
                eng.wait_ge(ssq, m + 1)
                eng.tensor_tensor(stat[0:n, 0:1], stat[0:n, 0:1], eps_col[0:n, :], ALU.add).then_inc(pool_ms, 1)
                eng.wait_ge(pool_ms, m + 1)
                eng.tensor_tensor(stat[0:n, 1:2], stat[0:n, 0:1], minus_half[0:n, :], ALU.pow).then_inc(rstd, 1)

            def body16(m):
                norm_tile(m, P)

            loop(eng, NC, body16)
            norm_tile(NC, TS)

            def rows(buf, hist, state, t, ev, hist_done, state_done, free):
                for sem, v in free:
                    eng.wait_ge(sem, v)
                eng.tensor_copy(sample_rows(buf)[:, :, 0:HIST],
                                hist[:, bass.ds(t, 1), :].squeeze(1).rearrange("p (b r) -> p b r", r=HIST)
                                ).then_inc(hist_done, 1)
                eng.wait_ge(evac_done, ev)
                out = state[:, bass.ds(t, 1), :].squeeze(1)
                eng.tensor_copy(out[:, 0:HIST], buf[:, SEQ:SEQ + HIST]).then_inc(state_done, 1)
                eng.tensor_copy(out[:, HIST:].rearrange("p (b r) -> p b r", r=HIST),
                                sample_rows(buf)[:, :, LS:SROW]).then_inc(state_done, 1)

            eng.wait_ge(rg_init, 1)
            def body17(j):
                rows(rb_x, hist_rg, st_rg, j, 2 * j + 2, rg_hist, rg_state, [(rg_conv, 4 * j)])

            loop(eng, R, body17)
            eng.wait_ge(cb_init, 2)
            def body18(j):
                for s in range(2):
                    rows(cb_x[s], hist_g, st_g, 2 * j + s, TQ + 2 * j + s + 2, cb_hist, cb_state,
                         [(cb_conv, 8 * j)])

            loop(eng, PAIRS, body18)


def mixer_block(nc, i, o, scratch, psum, B, k):
    cst, ident, ht_hi, ht_lo, stat, normw = (k[n] for n in ("cst", "ident", "ht_hi", "ht_lo", "stat", "normw"))
    wo_hi, wo_lo, samp_qkv, samp_z, samp_rg = (k[n] for n in ("wo_hi", "wo_lo", "samp_qkv", "samp_z", "samp_rg"))
    beta, g, edec, esamp, expo, gnw = (k[n] for n in ("beta", "g", "edec", "esamp", "expo", "gnw"))
    minus_half, eps_col = k["minus_half"], k["eps_col"]
    tle, ugt, strict, ones, tle8, ugt8, strict8, blk, mlow = (
        k[n] for n in ("tle", "ugt", "strict", "ones", "tle8", "ugt8", "strict8", "blk", "mlow"))
    four = lambda name: B(name, [P, H, P])
    at = B.at
    qkv_in, z_in, rg_in = B("qkv_in", [P, QKV, P]), four("z_in"), four("rg_in")
    x_in = B("x_in", [P, D])
    xn = B("xn2", [P, D])
    v_tok, kn, kg, ktail, kt = four("v_tok"), four("kn"), four("kg"), four("ktail"), four("kt")
    e_, u_, mq, pp, y_, x_ = four("decay"), four("u"), four("mq"), four("pp"), four("inv_t"), four("inv")
    nw, vnew, st = four("nw"), four("vnew"), four("state")
    mix_hi, mix_lo = B("mix_hi", [P, KT, P], F32R), B("mix_lo", [P, KT, P], F32R)
    rn = B("rn", [P, 2 * H])
    fac = B("fac", [P, 3, H])
    B = Plan(nc, at)
    s_state = B("s_state", [P, NS, P])
    v_exp = B("v_exp", [TS, NS, P])
    assert B.at <= at + 4 * (QKV + 2 * H) * P

    S = nc.alloc_semaphore
    names = ("gn_scaled s_init q_ld z_ld rg_ld x_ld n2_ld sq_done k_tr v_tr ss_mm rn_raw rn_done kn_done v_done "
             "kt_tr kt_done gr_done d_mm e_done e2_done ml_done kg_done ktail_done kk_mm qk_mm u1_done mq_done u_done "
             "ut_tr pp_done y_tr y_done x_done p_mm y_mm x_mm w_mm nw_done v_mm o1_mm vnew_done o2_mm ds_mm s_done "
             "t1_done o_done osq_done so_done fac_step fac_done on_done on_tr mix_done mixhi_done mixlo_done "
             "rghi_done rglo_done wo_mm x1_done ssq2 ms2 rstd2 xn_done hx_tr hhi_done hlo_done x1_out "
             "ss_ld ws_mm ws_ev vh_mm vh_done vexp_done dss_mm ss_dec ss_done ss_out sp_out").split()
    m_ = {n: S(f"mx_{n}") for n in names}
    NL = len(LEVELS)

    class Tile:

        def __init__(self, c):
            self.c = c
            self.samples = isinstance(c, int) and c == NC
            self.n = TS if self.samples else P
            self.levels = SAMPLE_LEVELS if self.samples else NL
            if self.samples:
                self.qkv, self.z, self.rg = samp_qkv, samp_z, samp_rg
                self.tle, self.ugt, self.strict = tle8, ugt8, strict8
            else:
                self.qkv, self.z, self.rg = qkv_in, z_in, rg_in
                self.tle, self.ugt, self.strict = tle, ugt, strict
            self.tok = slice(SEQ, T) if self.samples else bass.ds(P * c, P)

        def col(self, t):
            return t[0:self.n, bass.ds(self.c, 1), :].squeeze(1)

    def spread(ap, n, m=P):
        return ap.unsqueeze(2).to_broadcast([n, H, m])

    def over(ap, n):
        return ap.unsqueeze(1).to_broadcast([n, H, ap.shape[1]])

    def b4(q, n=P, m=P):
        return psum[q][0:n, :].rearrange("p (h m) -> p h m", m=P)[:, :, 0:m]

    def chunked(rows, c):
        return rows.rearrange("t p (c n) -> c p t n", n=P)[bass.ds(c, 1)].squeeze(0)

    def token_rows(a, t):
        return a[SEQ:T, :] if t.samples else a[0:SEQ, :].rearrange("(c p) d -> c p d", p=P)[bass.ds(t.c, 1)].squeeze(0)

    with nc.Block() as block:

        @block.sync
        def _(eng):
            eng.dma_start(normw[:, :], i["norm2"]).then_inc(m_["n2_ld"], 16)

            def chunk(c):
                t = Tile(c)
                if not t.samples:
                    eng.wait_ge(m_["o1_mm"], c)
                    eng.dma_start(qkv_in[:, :, :], chunked(scratch["qkv"], c)
                                  ).then_inc(m_["q_ld"], 16)
                    eng.wait_ge(m_["rghi_done"], c)
                    eng.wait_ge(m_["rglo_done"], c)
                    eng.dma_start(rg_in[:, :, :], chunked(scratch["rg"], c)
                                  ).then_inc(m_["rg_ld"], 16)
                    eng.wait_ge(m_["mix_done"], c)
                    eng.dma_start(z_in[:, :, :], chunked(scratch["z"], c)
                                  ).then_inc(m_["z_ld"], 16)
                eng.wait_ge(m_["x1_out"], 16 * c)
                eng.wait_ge(m_["xn_done"], c)
                eng.dma_start(x_in[0:t.n, :], token_rows(i["x"], t)).then_inc(m_["x_ld"], 16)
                eng.wait_ge(m_["x1_done"], 2 * (c + 1))
                eng.dma_start(token_rows(scratch["x1"], t), x_in[0:t.n, :]).then_inc(m_["x1_out"], 16)

            loop(eng, NC, chunk)
            eng.wait_ge(m_["s_done"], NC)
            eng.dma_start(o["S_prompt"], st[:, :, :]).then_inc(m_["sp_out"], 16)
            eng.wait_ge(m_["o1_mm"], NC)
            eng.wait_ge(m_["mix_done"], NC)
            eng.wait_ge(m_["rghi_done"], NC)
            eng.wait_ge(m_["rglo_done"], NC)
            for h in range(H):
                eng.wait_ge(m_["ss_out"], 16 * h)
                eng.dma_start(s_state[:, :, :], i["state_S"][h]).then_inc(m_["ss_ld"], 16)
                eng.wait_ge(m_["ss_done"], h + 1)
                eng.dma_start(o["S_sample"][h], s_state[:, :, :]).then_inc(m_["ss_out"], 16)
            chunk(NC)
            eng.wait_ge(m_["ss_out"], 16 * H)
            eng.wait_ge(m_["sp_out"], 16)
            eng.wait_ge(m_["x1_out"], 16 * MT)

        @block.tensor
        def _(eng):

            def chunk(c):
                t = Tile(c)
                n = t.n
                if not t.samples:
                    eng.wait_ge(m_["q_ld"], 16 * (c + 1))
                eng.wait_ge(m_["vnew_done"], c)
                eng.wait_ge(m_["t1_done"], c)
                for q, off, sem in ((2, H, "k_tr"), (3, 2 * H, "v_tr")):
                    for h in range(H):
                        mm = eng.transpose(psum[q][0:n, h * P:(h + 1) * P], t.qkv[:, off + h, 0:n], ident)
                    mm.then_inc(m_[sem], 1)
                eng.wait_ge(m_["sq_done"], c + 1)
                eng.wait_ge(m_["s_done"], c)
                sq = xn[:, :].rearrange("p (t n) -> p t n", n=P)
                for h in range(2 * H):
                    mm = eng.matmul(psum[7][0:n, h:h + 1], sq[:, h, 0:n], ones[:, 0:1], start=True, stop=True)
                mm.then_inc(m_["ss_mm"], 1)
                eng.wait_ge(m_["kn_done"], c + 1)
                eng.wait_ge(m_["nw_done"], c)
                for h in range(H):
                    mm = eng.transpose(psum[4][:, h * P:h * P + n], kn[0:n, h, :], ident[0:n, 0:n])
                mm.then_inc(m_["kt_tr"], 1)
                eng.wait_ge(m_["gr_done"], c + 1)
                eng.wait_ge(m_["o_done"], c)
                eng.matmul(b4(5, n, n), t.ugt, pp[0:n, :, 0:n], start=True, stop=True).then_inc(m_["d_mm"], 1)
                eng.wait_ge(m_["kt_done"], c + 1)
                for h in range(H):
                    mm = eng.matmul(psum[2][0:n, h * P:h * P + n], kt[:, h, 0:n], kt[:, h, 0:n], start=True, stop=True)
                mm.then_inc(m_["kk_mm"], 1)
                eng.wait_ge(m_["v_done"], c + 1)
                for h in range(H):
                    mm = eng.matmul(psum[3][0:n, h * P:h * P + n], kt[:, h, 0:n], t.qkv[:, h, 0:n],
                                    start=True, stop=True)
                mm.then_inc(m_["qk_mm"], 1)
                eng.wait_ge(m_["u_done"], c + 1)
                for h in range(H):
                    mm = eng.transpose(psum[4][0:n, h * P:h * P + n], u_[0:n, h, 0:n], ident[0:n, 0:n])
                mm.then_inc(m_["ut_tr"], 1)
                eng.wait_ge(m_["pp_done"], NL * c + 1)
                eng.wait_ge(m_["mix_done"], c)
                for h in range(H):
                    mm = eng.transpose(psum[6][0:n, h * P:h * P + n], pp[0:n, h, 0:n], ident[0:n, 0:n])
                mm.then_inc(m_["y_tr"], 1)
                for q in range(1, t.levels):
                    last = q == t.levels - 1
                    eng.wait_ge(m_["y_done"], NL * c + q)
                    eng.wait_ge(m_["x_done"], (NL - 1) * c + q)
                    for h in range(H):
                        mm = eng.matmul(psum[5][0:n, h * P:h * P + n], u_[0:n, h, 0:n], x_[0:n, h, 0:n],
                                        start=True, stop=True)
                    mm.then_inc(m_["p_mm"], 1)
                    eng.wait_ge(m_["pp_done"], NL * c + q + 1)
                    for h in range(H):
                        mm = eng.matmul(psum[6][0:n, h * P:h * P + n], pp[0:n, h, 0:n], y_[0:n, h, 0:n],
                                        start=True, stop=True)
                    mm.then_inc(m_["y_mm"], 1)
                    if not last:
                        for h in range(H):
                            mm = eng.matmul(psum[7][0:n, h * P:h * P + n], y_[0:n, h, 0:n], pp[0:n, h, 0:n],
                                            start=True, stop=True)
                        mm.then_inc(m_["x_mm"], 1)
                eng.wait_ge(m_["y_done"], NL * c + t.levels)
                eng.wait_ge(m_["kg_done"], c + 1)
                for h in range(H):
                    mm = eng.matmul(psum[4][:, h * P:h * P + n], kg[0:n, h, :], y_[0:n, h, 0:n], start=True, stop=True)
                mm.then_inc(m_["w_mm"], 1)
                eng.wait_ge(m_["nw_done"], c + 1)
                if t.samples:
                    samples_states(t)
                else:
                    eng.wait_ge(m_["s_done"], c)
                    eng.wait_ge(m_["s_init"], 1)
                    for h in range(H):
                        eng.matmul(psum[2][:, h * P:(h + 1) * P], y_[:, h, :], v_tok[:, h, :], start=True, stop=False)
                        mm = eng.matmul(psum[2][:, h * P:(h + 1) * P], nw[:, h, :], st[:, h, :],
                                        start=False, stop=True)
                    mm.then_inc(m_["v_mm"], 1)
                    eng.wait_ge(m_["mq_done"], c + 1)
                    for h in range(H):
                        mm = eng.matmul(psum[3][:, h * P:(h + 1) * P], qkv_in[:, h, :], st[:, h, :],
                                        start=True, stop=True)
                    mm.then_inc(m_["o1_mm"], 1)
                    eng.wait_ge(m_["vnew_done"], c + 1)
                    eng.wait_ge(m_["ktail_done"], c + 1)
                    for h in range(H):
                        mm = eng.matmul(psum[7][:, h * P:(h + 1) * P], ktail[:, h, :], vnew[:, h, :],
                                        start=True, stop=True)
                    mm.then_inc(m_["ds_mm"], 1)
                for h in range(H):
                    mm = eng.matmul(psum[5][0:n, h * P:(h + 1) * P], mq[0:n, h, 0:n], vnew[0:n, h, :],
                                    start=True, stop=True)
                mm.then_inc(m_["o2_mm"], 1)
                eng.wait_ge(m_["on_done"], c + 1)
                for h in range(H):
                    mm = eng.transpose(psum[6][:, h * P:h * P + n], mq[0:n, h, :], ident[0:n, 0:n])
                mm.then_inc(m_["on_tr"], 1)
                eng.wait_ge(m_["hlo_done"], 2 * c)
                eng.wait_ge(m_["rghi_done"], c + 1)
                eng.wait_ge(m_["rglo_done"], c + 1)
                for first, feats in ((True, range(R)), (False, range(R, KT))):
                    if not first:
                        eng.wait_ge(m_["mixhi_done"], c + 1)
                        eng.wait_ge(m_["mixlo_done"], c + 1)
                    for half in range(2):
                        for f in feats:
                            sl = slice(half * BANK, (half + 1) * BANK)
                            mm = mm3(eng, psum[half][0:n, :], mix_hi[:, f, 0:n], mix_lo[:, f, 0:n],
                                     wo_hi[:, f, sl], wo_lo[:, f, sl], f == 0, f == KT - 1)
                        if not first:
                            mm.then_inc(m_["wo_mm"], 1)
                eng.wait_ge(m_["xn_done"], c + 1)
                for half in range(2):
                    for kk in range(4):
                        f = 4 * half + kk
                        mm = eng.transpose(psum[half][:, kk * P:kk * P + n], xn[0:n, f * P:(f + 1) * P],
                                           ident[0:n, 0:n])
                    mm.then_inc(m_["hx_tr"], 1)

            def samples_states(t):
                eng.wait_ge(m_["mq_done"], NC + 1)
                for h in range(H):
                    eng.wait_ge(m_["ss_ld"], 16 * (h + 1))
                    eng.wait_ge(m_["ws_ev"], h)
                    for q, src in enumerate((nw, samp_qkv)):
                        for b in range(NS):
                            mm = eng.matmul(psum[5][:, q * TS + b * LS:q * TS + (b + 1) * LS], s_state[:, b, :],
                                            src[:, h, b * LS:(b + 1) * LS], start=True, stop=True)
                    mm.then_inc(m_["ws_mm"], 1)
                    eng.wait_ge(m_["ws_ev"], h + 1)
                    hs = slice(h * P, (h + 1) * P)
                    eng.wait_ge(m_["vh_done"], h)
                    eng.matmul(psum[2][0:TS, hs], y_[0:TS, h, 0:TS], v_tok[0:TS, h, :], start=True, stop=False)
                    eng.matmul(psum[2][0:TS, hs], x_[:, h, 0:TS], ident, start=False, stop=True)
                    eng.matmul(psum[3][0:TS, hs], x_[:, h, TS:2 * TS], ident,
                               start=True, stop=True).then_inc(m_["vh_mm"], 1)
                    eng.wait_ge(m_["vexp_done"], h + 1)
                    eng.wait_ge(m_["ktail_done"], NC + 1)
                    eng.wait_ge(m_["ss_done"], h)
                    for q in range(2):
                        mm = eng.matmul(psum[6 + q][:, :], ktail[0:TS, h, :],
                                        v_exp[:, 4 * q:4 * q + 4, :].rearrange("p b d -> p (b d)"),
                                        start=True, stop=True)
                    mm.then_inc(m_["dss_mm"], 1)
                eng.wait_ge(m_["ss_done"], H)

            loop(eng, NC, chunk)
            chunk(NC)

        @block.scalar
        def _(eng):

            def chunk(c):
                t = Tile(c)
                n = t.n
                if not t.samples:
                    eng.wait_ge(m_["q_ld"], 16 * (c + 1))
                eng.wait_ge(m_["hx_tr"], 2 * c)
                eng.activation(xn[:, :].rearrange("p (t n) -> p t n", n=P)[:, :, 0:n], t.qkv[:, 0:2 * H, 0:n],
                               ACT.Square).then_inc(m_["sq_done"], 1)
                eng.wait_ge(m_["v_tr"], c + 1)
                eng.activation(v_tok[0:n, :, :], b4(3, n), ACT.Copy).then_inc(m_["v_done"], 1)
                if not t.samples:
                    eng.wait_ge(m_["rg_ld"], 16 * (c + 1))
                eng.wait_ge(m_["wo_mm"], 2 * c)
                eng.activation(mix_hi[:, 0:R, 0:n], t.rg[:, :, 0:n], ACT.Copy).then_inc(m_["rghi_done"], 1)
                eng.wait_ge(m_["kt_tr"], c + 1)
                eng.activation(kt[:, :, 0:n], b4(4, P, n), ACT.Copy).then_inc(m_["kt_done"], 1)
                eng.wait_ge(m_["d_mm"], c + 1)
                eng.activation(e_[0:n, :, 0:n], b4(5, n, n), ACT.Exp).then_inc(m_["e_done"], 1)
                eng.wait_ge(m_["w_mm"], c + 1)
                eng.activation(nw[:, :, 0:n], b4(4, P, n), ACT.Copy, scale=-1.0).then_inc(m_["nw_done"], 1)
                if t.samples:
                    for h in range(H):
                        eng.wait_ge(m_["ws_mm"], h + 1)
                        eng.activation(x_[:, h, :], psum[5][:, 0:2 * TS], ACT.Copy).then_inc(m_["ws_ev"], 1)
                eng.wait_ge(m_["o_done"], c + 1)
                eng.activation(x_[0:n, :, :], kn[0:n, :, :], ACT.Square, scale=1.0 / P).then_inc(m_["osq_done"], 1)
                eng.wait_ge(m_["mix_done"], c + 1)
                eng.activation(mix_hi[:, R:KT, 0:n], u_[:, :, 0:n], ACT.Copy).then_inc(m_["mixhi_done"], 1)
                eng.wait_ge(m_["x1_done"], 2 * (c + 1))
                eng.activation(xn[0:n, :], x_in[0:n, :], ACT.Square, scale=D ** -0.5,
                               accum_out=stat[0:n, 0:1]).then_inc(m_["ssq2"], 1)
                for half in range(2):
                    eng.wait_ge(m_["hx_tr"], 2 * c + half + 1)
                    eng.activation(ht_hi[:, 4 * half:4 * half + 4, t.tok], b4(half, P, n),
                                   ACT.Copy).then_inc(m_["hhi_done"], 1)

            loop(eng, NC, chunk)
            chunk(NC)

        @block.vector
        def _(eng):
            eng.tensor_scalar(fac[:, 2, 0:1], gnw[:, :], P ** -0.5, None, ALU.mult).then_inc(m_["gn_scaled"], 1)
            eng.memset(st[:, :, :], 0.0).then_inc(m_["s_init"], 1)

            def chunk(c):
                t = Tile(c)
                n = t.n
                eng.wait_ge(m_["ss_mm"], c + 1)
                eng.tensor_scalar(rn[0:n, :], psum[7][0:n, 0:2 * H], EPS, None, ALU.add).then_inc(m_["rn_raw"], 1)
                eng.wait_ge(m_["k_tr"], c + 1)
                eng.wait_ge(m_["rn_done"], c + 1)
                eng.tensor_tensor(kn[0:n, :, :], b4(2, n), spread(rn[0:n, H:], n), ALU.mult).then_inc(m_["kn_done"], 1)
                eng.wait_ge(m_["kk_mm"], c + 1)
                eng.wait_ge(m_["e2_done"], c + 1)
                eng.tensor_tensor(u_[0:n, :, 0:n], b4(2, n, n), e_[0:n, :, 0:n], ALU.mult).then_inc(m_["u1_done"], 1)
                eng.wait_ge(m_["qk_mm"], c + 1)
                eng.tensor_tensor(mq[0:n, :, 0:n], b4(3, n, n), e_[0:n, :, 0:n], ALU.mult).then_inc(m_["mq_done"], 1)
                eng.wait_ge(m_["u1_done"], c + 1)
                eng.wait_ge(m_["ml_done"], c + 1)
                eng.tensor_tensor(u_[0:n, :, 0:n], u_[0:n, :, 0:n], x_[0:n, :, 0:n], ALU.mult).then_inc(m_["u_done"], 1)
                eng.wait_ge(m_["ut_tr"], c + 1)
                eye = over(ident[0:n, 0:n], n)
                eng.tensor_tensor(pp[0:n, :, 0:n], b4(4, n, n), over(mlow[0][0:n, 0:n], n),
                                  ALU.mult).then_inc(m_["pp_done"], 1)
                eng.wait_ge(m_["pp_done"], NL * c + 1)
                eng.tensor_tensor(x_[0:n, :, 0:n], eye, pp[0:n, :, 0:n], ALU.subtract).then_inc(m_["x_done"], 1)
                eng.wait_ge(m_["y_tr"], c + 1)
                eng.tensor_tensor(y_[0:n, :, 0:n], eye, b4(6, n, n), ALU.subtract).then_inc(m_["y_done"], 1)
                for q in range(1, t.levels):
                    last = q == t.levels - 1
                    eng.wait_ge(m_["p_mm"], (NL - 1) * c + q)
                    eng.tensor_tensor(pp[0:n, :, 0:n], b4(5, n, n), over(mlow[q][0:n, 0:n], n),
                                      ALU.mult).then_inc(m_["pp_done"], 1)
                    eng.wait_ge(m_["y_mm"], (NL - 1) * c + q)
                    if not last:
                        eng.wait_ge(m_["x_mm"], (NL - 2) * c + q)
                    eng.tensor_tensor(y_[0:n, :, 0:n], y_[0:n, :, 0:n], b4(6, n, n),
                                      ALU.subtract).then_inc(m_["y_done"], 1)
                    if not last:
                        eng.tensor_tensor(x_[0:n, :, 0:n], x_[0:n, :, 0:n], b4(7, n, n),
                                          ALU.subtract).then_inc(m_["x_done"], 1)
                if t.samples:
                    for h in range(H):
                        eng.wait_ge(m_["vh_mm"], h + 1)
                        eng.tensor_scalar(vnew[0:n, h, :], psum[2][0:n, h * P:(h + 1) * P],
                                          beta[0:n, NC, h:h + 1], None, ALU.mult).then_inc(m_["vh_done"], 1)
                        eng.wait_ge(m_["vh_done"], h + 1)
                        eng.tensor_tensor(v_exp[:, :, :], vnew[0:n, h, :].unsqueeze(1).to_broadcast([n, NS, P]),
                                          blk.unsqueeze(2).to_broadcast([n, NS, P]),
                                          ALU.mult).then_inc(m_["vexp_done"], 1)
                        eng.wait_ge(m_["ws_mm"], h + 1)
                        eng.tensor_tensor(s_state[:, :, :], s_state[:, :, :],
                                          esamp[:, :, h:h + 1].to_broadcast([P, NS, P]),
                                          ALU.mult).then_inc(m_["ss_dec"], 1)
                        eng.wait_ge(m_["ss_dec"], h + 1)
                        eng.wait_ge(m_["dss_mm"], h + 1)
                        for q in range(2):
                            part = s_state[:, 4 * q:4 * q + 4, :]
                            ins = eng.tensor_tensor(part, part, b4(6 + q), ALU.add)
                        ins.then_inc(m_["ss_done"], 1)
                else:
                    eng.wait_ge(m_["v_mm"], c + 1)
                    eng.tensor_tensor(vnew[:, :, :], b4(2), spread(t.col(beta), n), ALU.mult).then_inc(m_["vnew_done"], 1)
                    eng.wait_ge(m_["o1_mm"], c + 1)
                eng.wait_ge(m_["kg_done"], c + 1)
                eng.wait_ge(m_["ktail_done"], c + 1)
                eng.tensor_tensor(kn[0:n, :, :], b4(3, n), spread(edec[0:n, 0, bass.ds(c, 1), :].squeeze(1), n),
                                  ALU.mult).then_inc(m_["t1_done"], 1)
                if not t.samples:
                    eng.wait_ge(m_["ds_mm"], c + 1)
                    for h in range(H):
                        ins = eng.scalar_tensor_tensor(out=st[:, h, :], in0=st[:, h, :],
                                                       scalar=edec[:, 2, bass.ds(c, 1), h], in1=b4(7)[:, h, :],
                                                       op0=ALU.mult, op1=ALU.add)
                    ins.then_inc(m_["s_done"], 1)
                eng.wait_ge(m_["o2_mm"], c + 1)
                eng.wait_ge(m_["t1_done"], c + 1)
                eng.tensor_tensor(kn[0:n, :, :], kn[0:n, :, :], b4(5, n), ALU.add).then_inc(m_["o_done"], 1)
                eng.wait_ge(m_["osq_done"], c + 1)
                eng.tensor_reduce(fac[0:n, 0, :], x_[0:n, :, :], AX, ALU.add).then_inc(m_["so_done"], 1)
                eng.wait_ge(m_["fac_done"], c + 1)
                eng.tensor_tensor(mq[0:n, :, :], kn[0:n, :, :], spread(fac[0:n, 1, :], n),
                                  ALU.mult).then_inc(m_["on_done"], 1)
                eng.wait_ge(m_["on_tr"], c + 1)
                if not t.samples:
                    eng.wait_ge(m_["z_ld"], 16 * (c + 1))
                eng.wait_ge(m_["gn_scaled"], 1)
                eng.scalar_tensor_tensor(out=u_[:, :, 0:n], in0=b4(6, P, n), scalar=fac[:, 2, 0:1],
                                         in1=t.z[:, :, 0:n], op0=ALU.mult, op1=ALU.mult).then_inc(m_["mix_done"], 1)
                eng.wait_ge(m_["mixhi_done"], c + 1)
                eng.tensor_tensor(mix_lo[:, R:KT, 0:n], u_[:, :, 0:n], f32(mix_hi[:, R:KT, 0:n]),
                                  ALU.subtract).then_inc(m_["mixlo_done"], 1)
                eng.wait_ge(m_["x_ld"], 16 * (c + 1))
                for half in range(2):
                    part = x_in[0:n, half * BANK:(half + 1) * BANK]
                    eng.wait_ge(m_["wo_mm"], 2 * c + half + 1)
                    eng.tensor_tensor(part, part, psum[half][0:n, :], ALU.add).then_inc(m_["x1_done"], 1)
                eng.wait_ge(m_["n2_ld"], 16)
                eng.wait_ge(m_["rstd2"], c + 1)
                eng.scalar_tensor_tensor(out=xn[0:n, :], in0=x_in[0:n, :], scalar=stat[0:n, 1:2], in1=normw[0:n, :],
                                         op0=ALU.mult, op1=ALU.mult).then_inc(m_["xn_done"], 1)
                for half in range(2):
                    eng.wait_ge(m_["hhi_done"], 2 * c + half + 1)
                    eng.tensor_tensor(ht_lo[:, 4 * half:4 * half + 4, t.tok], b4(half, P, n),
                                      f32(ht_hi[:, 4 * half:4 * half + 4, t.tok]),
                                      ALU.subtract).then_inc(m_["hlo_done"], 1)

            loop(eng, NC, chunk)
            chunk(NC)

        @block.gpsimd
        def _(eng):

            def chunk(c):
                t = Tile(c)
                n = t.n
                eng.wait_ge(m_["w_mm"], c)
                eng.tensor_tensor(pp[0:n, :, 0:n], over(t.tle, n), spread(t.col(g), n, n),
                                  ALU.mult).then_inc(m_["gr_done"], 1)
                eng.wait_ge(m_["so_done"], c)
                eng.tensor_tensor(x_[0:n, :, 0:n], over(t.strict, n), spread(t.col(beta), n, n),
                                  ALU.mult).then_inc(m_["ml_done"], 1)
                eng.wait_ge(m_["rn_raw"], c + 1)
                eng.tensor_tensor(rn[0:n, :], rn[0:n, :], expo[0:n, 0:2 * H], ALU.pow).then_inc(m_["rn_done"], 1)
                eng.wait_ge(m_["e_done"], c + 1)
                eng.tensor_tensor(e_[0:n, :, 0:n], e_[0:n, :, 0:n], over(t.tle, n), ALU.mult).then_inc(m_["e2_done"], 1)
                eng.wait_ge(m_["kn_done"], c + 1)
                eng.tensor_tensor(kg[0:n, :, :], kn[0:n, :, :], spread(edec[0:n, 0, bass.ds(c, 1), :].squeeze(1), n),
                                  ALU.mult).then_inc(m_["kg_done"], 1)
                eng.tensor_tensor(ktail[0:n, :, :], kn[0:n, :, :], spread(edec[0:n, 1, bass.ds(c, 1), :].squeeze(1), n),
                                  ALU.mult).then_inc(m_["ktail_done"], 1)
                eng.wait_ge(m_["rghi_done"], c + 1)
                eng.tensor_tensor(mix_lo[:, 0:R, 0:n], t.rg[:, :, 0:n], f32(mix_hi[:, 0:R, 0:n]),
                                  ALU.subtract).then_inc(m_["rglo_done"], 1)
                so, f = fac[0:n, 0, :], fac[0:n, 1, :]
                eng.wait_ge(m_["so_done"], c + 1)
                steps = ((f, rn[0:n, 0:H], rn[0:n, 0:H], ALU.mult), (so, so, f, ALU.mult),
                         (so, so, expo[0:n, 2 * H:], ALU.add), (so, so, expo[0:n, 0:H], ALU.pow))
                for q, (dst, a, b, op) in enumerate(steps):
                    eng.tensor_tensor(dst, a, b, op).then_inc(m_["fac_step"], 1)
                    eng.wait_ge(m_["fac_step"], 4 * c + q + 1)
                eng.tensor_tensor(f, so, rn[0:n, 0:H], ALU.mult).then_inc(m_["fac_done"], 1)
                eng.wait_ge(m_["ssq2"], c + 1)
                eng.tensor_tensor(stat[0:n, 0:1], stat[0:n, 0:1], eps_col[0:n, :], ALU.add).then_inc(m_["ms2"], 1)
                eng.wait_ge(m_["ms2"], c + 1)
                eng.tensor_tensor(stat[0:n, 1:2], stat[0:n, 0:1], minus_half[0:n, :],
                                  ALU.pow).then_inc(m_["rstd2"], 1)

            loop(eng, NC, chunk)
            chunk(NC)



def ffn_block(nc, i, o, scratch, psum, B, k):
    ht_hi, ht_lo, normw, minus_half, eps_col = (k[n] for n in ("ht_hi", "ht_lo", "normw", "minus_half", "eps_col"))
    acc = B("acc", [P, MT, D])
    h_hi = B("h_hi", [P, 2, T], F32R)
    h_lo = B("h_lo", [P, 2, T], F32R)
    gu_hi = [B(f"gu_hi{s}", [P, 2, KT, P], F32R) for s in range(2)]
    gu_lo = [B(f"gu_lo{s}", [P, 2, KT, P], F32R) for s in range(2)]
    dn_hi = B("dn_hi", [P, 2, D], F32R)
    dn_lo = B("dn_lo", [P, 2, D], F32R)
    most = max(m for _, m in GROUPS)
    sg = [B(f"sg{s}", [P, most]) for s in range(2)]
    hf = [B(f"hf{s}", [P, most]) for s in range(2)]
    fstat = B("fstat", [P, MT, 2])
    raw_at = B.at
    gu_raw = [B(f"gu_raw{s}", [P, 2, KT, P]) for s in range(2)]
    dn_raw = B("dn_raw", [P, 2, D])
    B = Plan(nc, raw_at)
    y_out = [B(f"y_out{s}", [P, D]) for s in range(2)]

    S = nc.alloc_semaphore
    x1_in, n3_in = S("ff_x1_in"), S("ff_n3_in")
    gu_in, dn_in = [S(f"gu_in{s}") for s in range(2)], S("dn_in")
    gu_hi_done, gu_lo_done, dn_hi_done, dn_lo_done = S("gu_hi_done"), S("gu_lo_done"), S("dn_hi_done"), S("dn_lo_done")
    gu_mm, sg_done, hf_done, h_hi_done, h_lo_done = S("gu_mm"), S("sg_done"), S("hf_done"), S("h_hi_done"), S("h_lo_done")
    dn_mm, acc_done = S("dn_mm"), S("acc_done")
    ssq, ms, rstd, y_done, y_dma = S("ff_ssq"), S("ff_ms"), S("ff_rstd"), S("ff_y_done"), [S(f"y_dma{s}") for s in range(2)]
    NG = len(GROUPS)
    PAIR = 2 * NG
    SUMS = 2 * MT
    NP = FT // 2

    def group_of(m):
        last = min((m + 1) * P, T) - 1
        return next(n for n, (a, ln) in enumerate(GROUPS) if last < a + ln)

    def first(n):
        return isinstance(n, int) and n < 2

    with nc.Block() as block:

        @block.sync
        def _(eng):
            def load_gu(j, s):
                t = 2 * j + s
                for q, name in enumerate(("w_gate", "w_up")):
                    eng.dma_start(gu_raw[s][:, q], i[name][bass.ds(t, 1)].squeeze(0)).then_inc(gu_in[s], 16)

            def load_dn(j):
                eng.dma_start(dn_raw[:, :, :], i["w_down"].rearrange("(j s) p d -> j p s d", s=2)[bass.ds(j, 1)]
                              .squeeze(0)).then_inc(dn_in, 16)

            load_gu(0, 0)
            load_gu(0, 1)
            load_dn(0)
            eng.dma_start(acc[:, 0:NC, :], scratch["x1"][0:SEQ, :].rearrange("(c p) d -> p c d", p=P)).then_inc(x1_in, 16)
            eng.dma_start(acc[0:TS, NC, :], scratch["x1"][SEQ:T, :]).then_inc(x1_in, 16)
            eng.dma_start(normw[:, :], i["norm3"]).then_inc(n3_in, 16)

            def pair(j):
                for s in range(2):
                    eng.wait_ge(gu_hi_done, 2 * j + s + 1)
                    eng.wait_ge(gu_lo_done, 2 * j + s + 1)
                    load_gu(j + 1, s)
                eng.wait_ge(dn_hi_done, j + 1)
                eng.wait_ge(dn_lo_done, j + 1)
                load_dn(j + 1)

            loop(eng, NP - 1, pair)
            for m in range(MT):
                n = P if m < NC else TS
                eng.wait_ge(y_done, m + 1)
                eng.dma_start(o["y"][m * P:m * P + n, :], y_out[m % 2][0:n, :]).then_inc(y_dma[m % 2], 16)
            eng.wait_ge(y_dma[0], 16 * (MT // 2 + 1))
            eng.wait_ge(y_dma[1], 16 * (MT // 2))

        @block.tensor
        def _(eng):
            def pair(j):
                for s in range(2):
                    eng.wait_ge(gu_hi_done, 2 * j + s + 1)
                    eng.wait_ge(gu_lo_done, 2 * j + s + 1)
                    for g, (a, m) in enumerate(GROUPS):
                        n = PAIR * j + NG * s + g
                        b = 2 * ((NG * s + g) % 2)
                        if not first(n):
                            eng.wait_ge(hf_done, n - 1)
                        for q in range(2):
                            for f in range(KT):
                                mm = mm3(eng, psum[b + q][:, 0:m], gu_hi[s][:, q, f, :], gu_lo[s][:, q, f, :],
                                         ht_hi[:, f, a:a + m], ht_lo[:, f, a:a + m], f == 0, f == KT - 1)
                            mm.then_inc(gu_mm, 1)
                eng.wait_ge(dn_hi_done, j + 1)
                eng.wait_ge(dn_lo_done, j + 1)
                for m in range(MT):
                    n = P if m < NC else TS
                    toks = slice(m * P, m * P + n)
                    if m == 0 or group_of(m) != group_of(m - 1):
                        eng.wait_ge(h_lo_done, PAIR * j + NG + group_of(m) + 1)
                    for half in range(2):
                        cols = slice(half * BANK, (half + 1) * BANK)
                        eng.wait_ge(acc_done, SUMS * j + (2 * (m - 2) + half + 1 if m >= 2 else 0))
                        for s in range(2):
                            mm = mm3(eng, psum[4 + 2 * (m % 2) + half][0:n, :], h_hi[:, s, toks], h_lo[:, s, toks],
                                     dn_hi[:, s, cols], dn_lo[:, s, cols], s == 0, s == 1)
                        mm.then_inc(dn_mm, 1)

            loop(eng, NP, pair)

        @block.scalar
        def _(eng):
            def split_gu(j, s):
                eng.wait_ge(gu_in[s], 32 * (j + 1))
                eng.wait_ge(gu_mm, 2 * PAIR * (j - 1) + 2 * NG * (s + 1))
                eng.activation(gu_hi[s][:, :, :, :], gu_raw[s][:, :, :, :], ACT.Copy).then_inc(gu_hi_done, 1)

            def split_dn(j):
                eng.wait_ge(dn_in, 16 * (j + 1))
                eng.wait_ge(dn_mm, SUMS * j)
                eng.activation(dn_hi[:, :, :], dn_raw[:, :, :], ACT.Copy).then_inc(dn_hi_done, 1)

            def pair(j, more):
                for s in range(2):
                    for g, (a, m) in enumerate(GROUPS):
                        n = PAIR * j + NG * s + g
                        b = (NG * s + g) % 2
                        eng.wait_ge(gu_mm, 2 * n + 1)
                        if not first(n):
                            eng.wait_ge(hf_done, n - 1)
                        eng.activation(sg[b][:, 0:m], psum[2 * b][:, 0:m], ACT.Silu).then_inc(sg_done, 1)
                        eng.wait_ge(hf_done, n + 1)
                        eng.activation(h_hi[:, s, a:a + m], hf[b][:, 0:m], ACT.Copy).then_inc(h_hi_done, 1)
                        if s == 0 and g == 0:
                            split_dn(j)
                    if more:
                        split_gu(j + 1, s)

            for s in range(2):
                eng.wait_ge(gu_in[s], 32)
                eng.activation(gu_hi[s][:, :, :, :], gu_raw[s][:, :, :, :], ACT.Copy).then_inc(gu_hi_done, 1)
            loop(eng, NP - 1, lambda j: pair(j, True))
            pair(NP - 1, False)
            for m in range(MT):
                n = P if m < NC else TS
                eng.wait_ge(acc_done, SUMS * (NP - 1) + 2 * m + 2)
                if m >= 2:
                    eng.wait_ge(y_dma[m % 2], 16 * (m // 2))
                eng.activation(y_out[m % 2][0:n, :], acc[0:n, m, :], ACT.Square, scale=D ** -0.5,
                               accum_out=fstat[0:n, m, 0:1]).then_inc(ssq, 1)

        @block.vector
        def _(eng):
            def split_gu(j, s):
                eng.wait_ge(gu_hi_done, 2 * j + s + 1)
                eng.tensor_tensor(gu_lo[s][:, :, :, :], gu_raw[s][:, :, :, :], f32(gu_hi[s][:, :, :, :]),
                                  ALU.subtract).then_inc(gu_lo_done, 1)

            def pair(j, more):
                for s in range(2):
                    for g, (a, m) in enumerate(GROUPS):
                        n = PAIR * j + NG * s + g
                        b = (NG * s + g) % 2
                        eng.wait_ge(gu_mm, 2 * n + 2)
                        eng.wait_ge(sg_done, n + 1)
                        if not first(n):
                            eng.wait_ge(h_lo_done, n - 1)
                        eng.tensor_tensor(hf[b][:, 0:m], sg[b][:, 0:m], psum[2 * b + 1][:, 0:m],
                                          ALU.mult).then_inc(hf_done, 1)
                        eng.wait_ge(h_hi_done, n + 1)
                        eng.tensor_tensor(h_lo[:, s, a:a + m], hf[b][:, 0:m], f32(h_hi[:, s, a:a + m]),
                                          ALU.subtract).then_inc(h_lo_done, 1)
                        if s == 0 and g == 0:
                            eng.wait_ge(dn_hi_done, j + 1)
                            eng.tensor_tensor(dn_lo[:, :, :], dn_raw[:, :, :], f32(dn_hi[:, :, :]),
                                              ALU.subtract).then_inc(dn_lo_done, 1)
                    if more:
                        split_gu(j + 1, s)
                for m in range(MT):
                    n = P if m < NC else TS
                    for half in range(2):
                        part = acc[0:n, m, half * BANK:(half + 1) * BANK]
                        eng.wait_ge(dn_mm, SUMS * j + 2 * m + half + 1)
                        eng.tensor_tensor(part, part, psum[4 + 2 * (m % 2) + half][0:n, :], ALU.add).then_inc(acc_done, 1)

            for s in range(2):
                split_gu(0, s)
            eng.wait_ge(x1_in, 32)
            loop(eng, NP - 1, lambda j: pair(j, True))
            pair(NP - 1, False)
            eng.wait_ge(n3_in, 16)
            for m in range(MT):
                n = P if m < NC else TS
                eng.wait_ge(rstd, m + 1)
                eng.scalar_tensor_tensor(out=y_out[m % 2][0:n, :], in0=acc[0:n, m, :], scalar=fstat[0:n, m, 1:2],
                                         in1=normw[0:n, :], op0=ALU.mult, op1=ALU.mult).then_inc(y_done, 1)

        @block.gpsimd
        def _(eng):
            for m in range(MT):
                n = P if m < NC else TS
                eng.wait_ge(ssq, m + 1)
                eng.tensor_tensor(fstat[0:n, m, 0:1], fstat[0:n, m, 0:1], eps_col[0:n, :], ALU.add).then_inc(ms, 1)
                eng.wait_ge(ms, m + 1)
                eng.tensor_tensor(fstat[0:n, m, 1:2], fstat[0:n, m, 0:1], minus_half[0:n, :], ALU.pow).then_inc(rstd, 1)



def lay_out(v):
    f = lambda n: np.asarray(v[n], np.float32)
    c = np.ascontiguousarray
    tiles = lambda w: w.reshape(w.shape[0], -1, P)
    win = f("w_in")[0]
    dr = R * P
    cols = []
    for t in range(R):
        cols += [np.arange(t * P, (t + 1) * P), np.arange(dr + t * P, dr + (t + 1) * P)]
    z0 = 2 * dr + QKV * P
    cols += [np.arange(z0 + t * P, z0 + (t + 1) * P) for t in range(H)]
    cols += [np.arange(2 * dr + t * P, 2 * dr + (t + 1) * P) for t in range(QKV)]
    w4 = win.reshape(KT, P, -1)
    i = {"x": np.concatenate([f("x_prompt")[0], f("x_sample").reshape(TS, D)])}
    i["w_in"] = c(np.stack([w4[:, :, cc].transpose(1, 0, 2) for cc in cols]))
    i["w_gates"] = c(w4[:, :, z0 + H * P:].transpose(1, 0, 2))
    i["w_out"] = f("w_out")[0].reshape(KT, P, D)
    for n, s in (("norm1", f("norm1")[0]), ("norm2", f("norm2")[0]), ("norm3", f("final_norm"))):
        i[n] = c(np.broadcast_to(s, (P, D)))
    feat = lambda a: c(a.reshape(a.shape[:-1] + (-1, P)))
    i["rg_par"] = c(np.stack([*feat(f("rg_conv_w")[0]), feat(f("rg_conv_b")[0]), feat(f("rg_ba")[0]),
                              feat(f("rg_bi")[0]), feat(f("rg_lambda")[0])]).transpose(2, 0, 1))
    i["rg_h0"] = c(feat(f("state_rglru_h")[0]).transpose(2, 1, 0))
    i["hist_rg"] = c(feat(f("state_rglru_conv")[0]).transpose(3, 2, 0, 1).reshape(P, R, NS * HIST))
    i["hist_g"] = c(feat(f("state_gdn_conv")[0]).transpose(3, 2, 0, 1).reshape(P, QKV, NS * HIST))
    i["conv_w"] = c(feat(f("gdn_conv_w")[0]).transpose(2, 1, 0))
    i["alog"] = c(np.broadcast_to(np.concatenate([f("gdn_A_log")[0], f("gdn_dt_bias")[0]]), (P, 2 * H)))
    rw = np.zeros((R, P, 2, P), np.float32)
    half = P // 2
    for q, n in enumerate(("rg_wa", "rg_wi")):
        for b in range(2 * R):
            s = b % 2 * half
            rw[b // 2, s:s + half, q, s:s + half] = f(n)[0][b]
    i["rg_w"] = rw
    i["gnw"] = c(f("gdn_norm_w")[0][:, None])
    i["state_S"] = c(f("state_gdn_S")[0].transpose(1, 2, 0, 3))
    i["w_gate"] = c(f("w_gate")[0].reshape(KT, P, FT, P).transpose(2, 1, 0, 3))
    i["w_up"] = c(f("w_up")[0].reshape(KT, P, FT, P).transpose(2, 1, 0, 3))
    i["w_down"] = f("w_down")[0].reshape(FT, P, D)
    i["expo"] = c(np.broadcast_to(np.array([-0.5] * 2 * H + [EPS] * H, np.float32), (P, 3 * H)))
    a, b = np.arange(P)[:, None], np.arange(P)[None, :]
    masks = [a == b, a <= b, a > b, a < b, a >= 0 * b]
    masks += [(a // (2 * n) == b // (2 * n)) & (a // n % 2 == 1) & (b // n % 2 == 0) for n in LEVELS]
    i["cst"] = c(np.stack([np.broadcast_to(m, (P, P)) for m in masks], 1).astype(np.float32))
    same = (a // LS == b // LS)[:TS, :TS]
    sm = [m[:TS, :TS] & same for m in masks[1:4]] + [(a // LS == b)[:TS, :NS]]
    i["cs"] = c(np.concatenate(sm, 1).astype(np.float32))
    return i


_OUTS = {"y": (T, D), "st_rg": (P, R, (1 + NS) * HIST), "st_h": (P, R, 1 + NS), "st_g": (P, QKV, (1 + NS) * HIST),
         "S_prompt": (P, H, P), "S_sample": (H, P, NS, P)}
_SCRATCH = {"rg": (R, P, SEQ), "z": (H, P, SEQ), "qkv": (QKV, P, SEQ), "x1": (T, D)}


def kernel(**inputs):
    import concourse.bacc as bacc
    from concourse.bass_utils import run_bass_kernel_spmd

    nc = bacc.Bacc("TRN2", target_bir_lowering=False, num_devices=1)
    arrays = {f"in_{n}": a for n, a in lay_out(inputs).items()}
    i = {n[3:]: nc.dram_tensor(n, a.shape, F32, kind="ExternalInput").ap() for n, a in arrays.items()}
    o = {n: nc.dram_tensor(f"out_{n}", s, F32, kind="ExternalOutput").ap() for n, s in _OUTS.items()}
    scratch = {n: nc.dram_tensor(f"scratch_{n}", s, F32, kind="Internal").ap() for n, s in _SCRATCH.items()}
    build(nc, i, o, scratch)
    r = run_bass_kernel_spmd(nc, [arrays], core_ids=[0]).results[0]
    y, rg, h, gd, sp, ss = (r[f"out_{n}"] for n in _OUTS)
    c = np.ascontiguousarray

    def rows(a):
        return c(a.reshape(P, -1, 1 + NS, HIST).transpose(2, 3, 1, 0).reshape(1, 1 + NS, HIST, -1))

    rc, gc = rows(rg), rows(gd)
    hh = c(h.transpose(2, 1, 0).reshape(1, 1 + NS, -1))
    return (c(y[:SEQ].reshape(1, SEQ, D)), c(y[SEQ:].reshape(NS, LS, D)),
            c(rc[:, :1]), c(hh[:, :1]), c(gc[:, :1]), c(sp.transpose(1, 0, 2)[None, None]),
            c(rc[:, 1:]), c(hh[:, 1:]), c(gc[:, 1:]), c(ss.transpose(2, 0, 1, 3)[None]))
```

```python
import numpy as np
import concourse.bass as bass
from concourse import mybir

F32 = mybir.dt.float32
F32R = mybir.dt.float32r
ACT = mybir.ActivationFunctionType
ALU = mybir.AluOpType
AX = mybir.AxisListType.X

P = 128
D = 1024
KT = D // P
SEQ = 1024
NS, LS = 8, 8
TS = NS * LS
T = SEQ + TS
NC = SEQ // P
MT = NC + 1
R = 4
H = 4
QKV = 3 * H
FF = 2816
FT = FF // P
EPS = 1e-6
GROUPS = [(0, 364), (364, 364), (728, 360)]
HIST = 3
SROW = HIST + LS
W = HIST + SEQ + NS * SROW
WC = W - HIST
S0 = SEQ + HIST
GATE_GROUPS = [(0, 372), (372, 370), (742, 370)]
NT = 2 * R + H + QKV
LEVELS = [1, 2, 4, 8, 16, 32, 64]
SAMPLE_LEVELS = 3
BANK = 512


class Plan:

    def __init__(self, nc, at):
        self.nc, self.at = nc, at

    def __call__(self, name, shape, dt=F32):
        n = 4 * int(np.prod(shape[1:]))
        t = self.nc.alloc_sbuf_tensor_at(name, shape, dt, offset=self.at)
        self.at += (n + 31) // 32 * 32
        assert self.at <= self.nc.sbuf_usable_end, (name, self.at)
        return t


def f32(ap):
    return ap.bitcast(F32)


def sample_rows(row):
    return row[:, S0:W].rearrange("p (b r) -> p b r", r=SROW)


def loop(eng, n, body):
    body(0)
    with eng.Fori(1, n) as j:
        body(j)


def mm3(pe, out, w_hi, w_lo, x_hi, x_lo, start, stop):
    pe.matmul(out, w_hi, x_hi, start=start, stop=False)
    pe.matmul(out, w_hi, x_lo, start=False, stop=False)
    return pe.matmul(out, w_lo, x_hi, start=False, stop=stop)


def build(nc, i, o, scratch):
    A = Plan(nc, (nc.sbuf_base + 31) // 32 * 32)
    psum = [nc.alloc_psum_tensor(f"bank{b}", [P, BANK], F32) for b in range(8)]
    expo = A("expo", [P, 3 * H])
    minus_half, eps_col = expo[:, 0:1], expo[:, 2 * H:2 * H + 1]
    stat = A("stat", [P, 2])
    normw = A("normw", [P, D])
    ht_hi = A("ht_hi", [P, KT, T], F32R)
    ht_lo = A("ht_lo", [P, KT, T], F32R)
    ffn_at = A.at
    cst = A("cst", [P, 12, P])
    ident, tle, ugt, strict, ones = (cst[:, n, :] for n in range(5))
    mlow = [cst[:, 5 + n, :] for n in range(len(LEVELS))]
    cs = A("cs", [TS, 3 * TS + NS])
    tle8, ugt8, strict8, blk = cs[:, 0:TS], cs[:, TS:2 * TS], cs[:, 2 * TS:3 * TS], cs[:, 3 * TS:]
    samp_qkv = A("samp_qkv", [P, QKV, TS])
    samp_z = A("samp_z", [P, H, TS])
    samp_rg = A("samp_rg", [P, R, TS])
    beta = A("beta", [P, MT, H])
    g = A("g", [P, MT, H])
    edec = A("edec", [P, 3, MT, H])
    esamp = A("esamp", [P, NS, H])
    gnw = A("gnw", [P, 1])
    base = A.at
    B = Plan(nc, base)
    wo_hi = B("wo_hi", [P, KT, D], F32R)
    wo_lo = B("wo_lo", [P, KT, D], F32R)
    after_wo = B.at

    input_block(nc, i, o, scratch, psum, Plan(nc, after_wo), locals())
    mixer_block(nc, i, o, scratch, psum, Plan(nc, after_wo), locals())
    ffn_block(nc, i, o, scratch, psum, Plan(nc, ffn_at), locals())



def input_block(nc, i, o, scratch, psum, B, k):
    cst, cs, ident, ht_hi, ht_lo, stat, normw = (k[n] for n in ("cst", "cs", "ident", "ht_hi", "ht_lo", "stat", "normw"))
    wo_hi, wo_lo, samp_qkv, samp_z, samp_rg = (k[n] for n in ("wo_hi", "wo_lo", "samp_qkv", "samp_z", "samp_rg"))
    beta, g, edec, esamp, minus_half, eps_col, gnw = (k[n] for n in ("beta", "g", "edec", "esamp", "minus_half", "eps_col", "gnw"))
    tle, ugt, ones, tle8, ugt8, blk = (k[n] for n in ("tle", "ugt", "ones", "tle8", "ugt8", "blk"))
    w_raw = [B(f"w_raw{s}", [P, KT, P]) for s in range(2)]
    w_hi = [B(f"w_hi{s}", [P, KT, P], F32R) for s in range(2)]
    w_lo = [B(f"w_lo{s}", [P, KT, P], F32R) for s in range(2)]
    rg_par = B("rg_par", [P, 8, R])
    rg_calc = B("rg_calc", [P, 3, R])
    rg_now = B("rg_now", [P, 3])
    rg_h0 = B("rg_h0", [P, R, NS])
    hist_rg = B("hist_rg", [P, R, NS * HIST])
    hist_g = B("hist_g", [P, QKV, NS * HIST])
    st_rg = B("st_rg", [P, R, (1 + NS) * HIST])
    st_h = B("st_h", [P, R, 1 + NS])
    st_g = B("st_g", [P, QKV, (1 + NS) * HIST])
    conv_w = B("conv_w", [P, QKV, 4])
    alog = B("alog", [P, 2 * H])
    rg_w = B("rg_w", [P, 2, P])
    NSP = MT * H + R
    sp = B("sp", [P, 5, NSP])
    graw = B("graw", [P, MT, 2 * H])
    gblk = B("gblk", [TS, NS, H])
    top = B.at
    B = Plan(nc, k["base"])
    xin = [B(f"xin{s}", [P, D]) for s in range(2)]
    xn = [B(f"xn{s}", [P, D]) for s in range(2)]
    gw_raw = B("gw_raw", [P, KT, 2 * H])
    gw_hi = B("gw_hi", [P, KT, 2 * H], F32R)
    gw_lo = B("gw_lo", [P, KT, 2 * H], F32R)
    gt = B("gt", [2 * H, T])
    B = Plan(nc, k["base"])
    rb_x, rb_xc, rb_gy, rb_r, rb_i, rb_t, rb_sq, rb_h = (
        B(f"rb_{n}", [P, W]) for n in ("x", "xc", "gy", "r", "i", "t", "sq", "h"))
    rb_tmp = B("rb_tmp", [P, NS])
    B = Plan(nc, top)
    cb_x = [B(f"cb_x{s}", [P, W]) for s in range(2)]
    cb_y = [B(f"cb_y{s}", [P, W]) for s in range(2)]
    wo_raw = [B(f"wo_raw{s}", [P, D]) for s in range(2)]

    S = nc.alloc_semaphore
    const_in, x_in = S("const_in"), [S(f"x_in{s}") for s in range(2)]
    ssq, root, xn_done = S("in_ssq"), S("in_root"), S("xn_done")
    xt_done, ht_hi_done, xt_free = S("xt_done"), S("ht_hi_done"), [S(f"xt_free{s}") for s in range(2)]
    gw_in, gw_hi_done, gw_lo_done = S("gw_in"), S("gw_hi_done"), S("gw_lo_done")
    gate_proj, gate_evac, gate_tok = S("gate_proj"), S("gate_evac"), S("gate_tok")
    graw_done, sp_arg, exp_done, beta_done = S("graw_done"), S("sp_arg"), S("exp_done"), S("beta_done")
    chain, g_done, decays = S("dve_chain"), S("g_done"), S("decays")
    w_in, w_hi_done, w_lo_done = [S(f"w_in{s}") for s in range(2)], S("w_hi_done"), S("w_lo_done")
    proj, evac_done = S("proj_done"), S("evac_done")
    rg_init, rg_hist, rg_state = S("rg_init"), S("rg_hist"), S("rg_state")
    rg_conv, rg_w_in, gate_mm, rg_tanh = S("rg_conv"), S("rg_w_in"), S("gate_mm"), S("rg_tanh")
    rg_t, rg_sq, rg_vec, rg_out = S("rg_t"), S("rg_sq"), S("rg_vec"), S("rg_out")
    z_out, wo_in = [S(f"z_out{s}") for s in range(2)], [S(f"wo_in{s}") for s in range(2)]
    wo_hi_done, wo_lo_done = S("wo_hi_done"), S("wo_lo_done")
    cb_init, cb_hist, cb_state = S("cb_init"), S("cb_hist"), S("cb_state")
    cb_conv, cb_silu, cb_out = S("cb_conv"), S("cb_silu"), [S(f"cb_out{s}") for s in range(2)]
    st_out = S("st_out")
    consts = ((cst[:, :, :], "cst"), (cs[:, :], "cs"), (normw[:, :], "norm1"), (rg_par[:, :, :], "rg_par"),
              (rg_h0[:, :, :], "rg_h0"), (hist_rg[:, :, :], "hist_rg"), (hist_g[:, :, :], "hist_g"),
              (conv_w[:, :, :], "conv_w"), (alog[:, :], "alog"), (gnw[:, :], "gnw"), (k["expo"][:, :], "expo"))
    NCONST = 16 * len(consts)
    VEC = 14
    PAIRS = QKV // 2
    TZ, TQ = 2 * R, 2 * R + H

    def bank(s, n):
        return psum[3 * s + n]

    def sample_bank(s):
        a = GROUPS[-1][0]
        return bank(s, 2)[:, SEQ - a:T - a]

    def by_sample(ap):
        return ap.rearrange("p (b l) -> p b l", l=LS)

    with nc.Block() as block:

        @block.sync
        def _(eng):
            eng.dma_start(xin[0][:, :], i["x"][0:P, :]).then_inc(x_in[0], 16)
            for dst, name in consts:
                eng.dma_start(dst, i[name]).then_inc(const_in, 16)
            eng.dma_start(xin[1][:, :], i["x"][P:2 * P, :]).then_inc(x_in[1], 16)
            eng.dma_start(gw_raw[:, :, :], i["w_gates"]).then_inc(gw_in, 16)
            for s in range(2):
                eng.dma_start(w_raw[s][:, :, :], i["w_in"][s]).then_inc(w_in[s], 16)
            for m in range(2, MT):
                eng.wait_ge(xn_done, m - 1)
                n = P if m < NC else TS
                eng.dma_start(xin[m % 2][0:n, :], i["x"][m * P:m * P + n, :]).then_inc(x_in[m % 2], 16)

            def load_w(t, s):
                eng.wait_ge(w_hi_done, t + 1)
                eng.wait_ge(w_lo_done, t + 1)
                eng.dma_start(w_raw[s][:, :, :], i["w_in"][bass.ds(t + 2, 1)].squeeze(0)).then_inc(w_in[s], 16)

            def body1(j):
                eng.wait_ge(gate_mm, 6 * j)
                eng.dma_start(rg_w[:, :, :], i["rg_w"][bass.ds(j, 1)].squeeze(0)).then_inc(rg_w_in, 16)
                load_w(2 * j, 0)
                load_w(2 * j + 1, 1)
                eng.wait_ge(rg_vec, VEC * (j + 1))
                eng.dma_start(scratch["rg"][bass.ds(j, 1)].squeeze(0), rb_gy[:, 0:SEQ]).then_inc(rg_out, 16)

            loop(eng, R, body1)
            eng.wait_ge(rg_out, 16 * R)
            def body2(j):
                for s in range(2):
                    for n in range(2):
                        eng.wait_ge(wo_hi_done, 4 * j + 2 * s)
                        eng.wait_ge(wo_lo_done, 4 * j + 2 * s)
                        eng.dma_start(wo_raw[n][:, :],
                                      i["w_out"][bass.ds(4 * j + 2 * s + n, 1)].squeeze(0)).then_inc(wo_in[n], 16)
                    load_w(TZ + 2 * j + s, s)
                for s in range(2):
                    eng.wait_ge(evac_done, TZ + 2 * j + s + 2)
                    eng.dma_start(scratch["z"][bass.ds(2 * j + s, 1)].squeeze(0),
                                  cb_y[s][:, 0:SEQ]).then_inc(z_out[s], 16)

            loop(eng, H // 2, body2)

            def qkv(j, prefetch):
                for s in range(2):
                    if prefetch:
                        load_w(TQ + 2 * j + s, s)
                for s in range(2):
                    eng.wait_ge(cb_silu, 2 * j + s + 1)
                    eng.dma_start(scratch["qkv"][bass.ds(2 * j + s, 1)].squeeze(0),
                                  cb_y[s][:, 0:SEQ]).then_inc(cb_out[s], 16)

            loop(eng, PAIRS - 1, lambda j: qkv(j, True))
            qkv(PAIRS - 1, False)
            eng.wait_ge(rg_state, 2 * R)
            eng.wait_ge(rg_vec, VEC * R)
            eng.wait_ge(cb_state, 2 * QKV)
            for name, src in (("st_rg", st_rg), ("st_h", st_h), ("st_g", st_g)):
                eng.dma_start(o[name], src[:, :, :]).then_inc(st_out, 16)
            eng.wait_ge(st_out, 48)
            for s in range(2):
                eng.wait_ge(z_out[s], 16 * H // 2)
                eng.wait_ge(cb_out[s], 16 * PAIRS)

        @block.tensor
        def _(eng):
            eng.wait_ge(const_in, NCONST)

            def transposes(s, n):
                for half in range(2):
                    for kk in range(4):
                        f = 4 * half + kk
                        mm = eng.transpose(bank(s, half)[:, kk * P:kk * P + n],
                                           xn[s][0:n, f * P:(f + 1) * P], ident[0:n, 0:n])
                    mm.then_inc(xt_done, 1)

            def body4(j):
                for s in range(2):
                    eng.wait_ge(xn_done, 2 * j + s + 1)
                    eng.wait_ge(xt_free[s], j)
                    transposes(s, P)

            loop(eng, NC // 2, body4)
            eng.wait_ge(xn_done, MT)
            eng.wait_ge(xt_free[0], NC // 2)
            transposes(0, TS)
            for s in range(2):
                eng.wait_ge(xt_free[s], NC // 2 + 1 - s)
            eng.wait_ge(gw_hi_done, 1)
            eng.wait_ge(gw_lo_done, 1)
            for n, (a, m) in enumerate(GROUPS):
                for f in range(KT):
                    mm = mm3(eng, bank(1, n)[0:2 * H, 0:m], gw_hi[:, f, :], gw_lo[:, f, :],
                             ht_hi[:, f, a:a + m], ht_lo[:, f, a:a + m], f == 0, f == KT - 1)
                mm.then_inc(gate_proj, 1)
            eng.wait_ge(evac_done, 1)
            for m in range(MT):
                n = P if m < NC else TS
                mm = eng.transpose(psum[6][0:n, m * 2 * H:(m + 1) * 2 * H], gt[:, m * P:m * P + n],
                                   ident[0:2 * H, 0:2 * H])
            mm.then_inc(gate_tok, 1)

            def project(t, s):
                eng.wait_ge(w_hi_done, t + 1)
                eng.wait_ge(w_lo_done, t + 1)
                eng.wait_ge(evac_done, t)
                for n, (a, m) in enumerate(GROUPS):
                    for f in range(KT):
                        mm = mm3(eng, bank(s, n)[:, 0:m], w_hi[s][:, f, :], w_lo[s][:, f, :],
                                 ht_hi[:, f, a:a + m], ht_lo[:, f, a:a + m], f == 0, f == KT - 1)
                    mm.then_inc(proj, 1)

            eng.wait_ge(graw_done, 1)
            def body5(j):
                for s in range(2):
                    project(2 * j + s, s)
                eng.wait_ge(rg_conv, 4 * (j + 1))
                eng.wait_ge(rg_w_in, 16 * (j + 1))
                for n, (a, m) in enumerate(GATE_GROUPS):
                    for q in range(2):
                        eng.wait_ge(rg_tanh, 6 * j + max(0, 2 * n + q - 1))
                        eng.matmul(psum[6 + q][:, 0:m], rg_w[:, q, :], rb_xc[:, a:a + m],
                                   start=True, stop=True).then_inc(gate_mm, 1)

            loop(eng, R, body5)
            eng.wait_ge(g_done, 2)
            eng.wait_ge(rg_tanh, 6 * R)
            gp = g[:, 0:NC, :].rearrange("p c h -> p (c h)")
            n, full = NC * H, MT * H
            for q, m in enumerate((tle, ugt, ones)):
                eng.matmul(psum[6][:, q * full:q * full + n], m, gp, start=True, stop=True)
            for q, m in enumerate((tle8, ugt8)):
                eng.matmul(psum[6][0:TS, q * full + n:(q + 1) * full], m, g[0:TS, NC, :], start=True, stop=True)
            eng.matmul(psum[7][:, 0:NS * H], ones[0:TS, :], gblk[:, :, :].rearrange("p b h -> p (b h)"),
                       start=True, stop=True).then_inc(decays, 1)
            def body6(j):
                for s in range(2):
                    project(TZ + 2 * j + s, s)

            loop(eng, H // 2, body6)
            def body7(j):
                for s in range(2):
                    project(TQ + 2 * j + s, s)

            loop(eng, PAIRS, body7)

        @block.scalar
        def _(eng):
            eng.wait_ge(const_in, NCONST)

            def norm_tile(m, s, load, n, toks):
                eng.wait_ge(x_in[s], 16 * load)
                eng.wait_ge(xn_done, m)
                eng.activation(xn[s][0:n, :], xin[s][0:n, :], ACT.Square, scale=D ** -0.5,
                               accum_out=stat[0:n, 0:1]).then_inc(ssq, 1)
                for half in range(2):
                    eng.wait_ge(xt_done, 2 * m + half + 1)
                    eng.activation(ht_hi[:, 4 * half:4 * half + 4, toks],
                                   bank(s, half)[:, :].rearrange("p (f t) -> p f t", t=P)[:, :, 0:n],
                                   ACT.Copy).then_inc(ht_hi_done, 1)

            def body8(j):
                for s in range(2):
                    norm_tile(2 * j + s, s, j + 1, P, bass.ds(2 * P * j + s * P, P))

            loop(eng, NC // 2, body8)
            norm_tile(NC, 0, NC // 2 + 1, TS, slice(SEQ, T))
            eng.wait_ge(gw_in, 16)
            eng.activation(gw_hi[:, :, :], gw_raw[:, :, :], ACT.Copy).then_inc(gw_hi_done, 1)

            for s in range(2):
                eng.wait_ge(w_in[s], 16)
                eng.activation(w_hi[s][:, :, :], w_raw[s][:, :, :], ACT.Copy).then_inc(w_hi_done, 1)
            for n, (a, m) in enumerate(GROUPS):
                eng.wait_ge(gate_proj, n + 1)
                ins = eng.activation(gt[:, a:a + m], bank(1, n)[0:2 * H, 0:m], ACT.Copy)
            ins.then_inc(evac_done, 1)
            eng.wait_ge(sp_arg, 1)
            eng.activation(sp[:, 1, :], sp[:, 1, :], ACT.Exp, scale=-1.0)
            eng.activation(alog[:, 0:H], alog[:, 0:H], ACT.Exp).then_inc(exp_done, 1)
            eng.activation(beta[:, :, :], graw[:, :, 0:H], ACT.Sigmoid).then_inc(beta_done, 1)

            def split_next(t, s, load):
                eng.wait_ge(w_in[s], 16 * load)
                eng.activation(w_hi[s][:, :, :], w_raw[s][:, :, :], ACT.Copy).then_inc(w_hi_done, 1)

            eng.wait_ge(rg_init, 1)
            eng.wait_ge(g_done, 2)
            def body9(j):
                eng.wait_ge(rg_conv, 4 * j)
                eng.wait_ge(rg_state, 2 * j)
                for n, (a, m) in enumerate(GROUPS):
                    e = min(a + m, SEQ)
                    eng.wait_ge(proj, 6 * j + n + 1)
                    eng.activation(rb_x[:, HIST + a:HIST + e], bank(0, n)[:, 0:e - a], ACT.Copy)
                eng.activation(sample_rows(rb_x)[:, :, HIST:SROW], by_sample(sample_bank(0)),
                               ACT.Copy).then_inc(evac_done, 1)
                split_next(2 * j, 0, j + 2)
                eng.wait_ge(rg_out, 16 * j)
                eng.wait_ge(rg_vec, VEC * j)
                for n, (a, m) in enumerate(GROUPS):
                    e = min(a + m, SEQ)
                    eng.wait_ge(proj, 6 * j + n + 4)
                    eng.activation(rb_gy[:, a:e], bank(1, n)[:, 0:e - a], ACT.Gelu_apprx_tanh)
                eng.activation(sample_rows(rb_gy)[:, :, 0:LS], by_sample(sample_bank(1)),
                               ACT.Gelu_apprx_tanh).then_inc(evac_done, 1)
                split_next(2 * j + 1, 1, j + 2)
                for n, (a, m) in enumerate(GATE_GROUPS):
                    for q, row in enumerate((rb_r, rb_i)):
                        eng.wait_ge(gate_mm, 6 * j + 2 * n + q + 1)
                        eng.activation(row[:, a:a + m], psum[6 + q][:, 0:m], ACT.Tanh, scale=0.5,
                                       bias=rg_now[:, q:q + 1]).then_inc(rg_tanh, 1)
                eng.wait_ge(rg_tanh, 6 * j + 6)
                eng.activation(rb_t[:, 0:WC], rb_r[:, 0:WC], ACT.Tanh, scale=rg_now[:, 2:3], bias=rg_now[:, 2:3]).then_inc(rg_t, 1)
                eng.wait_ge(rg_t, j + 1)
                eng.activation(rb_sq[:, 0:WC], rb_t[:, 0:WC], ACT.Sqrt).then_inc(rg_sq, 1)

            loop(eng, R, body9)
            eng.wait_ge(decays, 1)
            n, full = NC * H, MT * H
            eng.activation(edec[:, :, 0:NC, :].rearrange("p q c h -> p q (c h)"),
                           psum[6][:, 0:3 * full].rearrange("p (q n) -> p q n", n=full)[:, :, 0:n], ACT.Exp)
            eng.activation(edec[0:TS, 0:2, NC, :],
                           psum[6][0:TS, 0:2 * full].rearrange("p (q n) -> p q n", n=full)[:, :, n:], ACT.Exp)
            eng.activation(esamp[:, :, :].rearrange("p b h -> p (b h)"), psum[7][:, 0:NS * H], ACT.Exp)
            eng.wait_ge(rg_vec, VEC * R)
            eng.wait_ge(rg_state, 2 * R)
            eng.wait_ge(rg_out, 16 * R)
            def body10(j):
                for s in range(2):
                    eng.wait_ge(z_out[s], 16 * j)
                    for n, (a, m) in enumerate(GROUPS):
                        e = min(a + m, SEQ)
                        eng.wait_ge(proj, 3 * TZ + 6 * j + 3 * s + n + 1)
                        eng.activation(cb_y[s][:, a:e], bank(s, n)[:, 0:e - a], ACT.Silu)
                    eng.activation(samp_z[:, bass.ds(2 * j + s, 1), :].squeeze(1), sample_bank(s),
                                   ACT.Silu).then_inc(evac_done, 1)
                    split_next(TZ + 2 * j + s, s, R + j + 2)
                    for n in range(2):
                        eng.wait_ge(wo_in[n], 16 * (2 * j + s + 1))
                        eng.activation(wo_hi[:, bass.ds(4 * j + 2 * s + n, 1), :].squeeze(1), wo_raw[n][:, :],
                                       ACT.Copy).then_inc(wo_hi_done, 1)

            loop(eng, H // 2, body10)

            def qkv(j, prefetch):
                for s in range(2):
                    eng.wait_ge(cb_conv, 8 * j + 4 * s)
                    eng.wait_ge(cb_state, 4 * j + 2 * s)
                    for n, (a, m) in enumerate(GROUPS):
                        e = min(a + m, SEQ)
                        eng.wait_ge(proj, 3 * TQ + 6 * j + 3 * s + n + 1)
                        eng.activation(cb_x[s][:, HIST + a:HIST + e], bank(s, n)[:, 0:e - a], ACT.Copy)
                    eng.activation(sample_rows(cb_x[s])[:, :, HIST:SROW], by_sample(sample_bank(s)),
                                   ACT.Copy).then_inc(evac_done, 1)
                    if prefetch:
                        split_next(TQ + 2 * j + s, s, R + H // 2 + j + 2)
                    eng.wait_ge(cb_conv, 8 * j + 4 * (s + 1))
                    eng.activation(by_sample(samp_qkv[:, bass.ds(2 * j + s, 1), :].squeeze(1)),
                                   sample_rows(cb_y[s])[:, :, 0:LS], ACT.Silu)
                    eng.activation(cb_y[s][:, 0:SEQ], cb_y[s][:, 0:SEQ], ACT.Silu).then_inc(cb_silu, 1)

            loop(eng, PAIRS - 1, lambda j: qkv(j, True))
            qkv(PAIRS - 1, False)

        @block.vector
        def _(eng):
            eng.wait_ge(const_in, NCONST)

            def norm_tile(m, s, n, toks):
                eng.wait_ge(root, 2 * m + 2)
                eng.scalar_tensor_tensor(out=xn[s][0:n, :], in0=xin[s][0:n, :], scalar=stat[0:n, 1:2],
                                         in1=normw[0:n, :], op0=ALU.mult, op1=ALU.mult).then_inc(xn_done, 1)
                for half in range(2):
                    eng.wait_ge(ht_hi_done, 2 * m + half + 1)
                    ins = eng.tensor_tensor(ht_lo[:, 4 * half:4 * half + 4, toks],
                                            bank(s, half)[:, :].rearrange("p (f t) -> p f t", t=P)[:, :, 0:n],
                                            f32(ht_hi[:, 4 * half:4 * half + 4, toks]), ALU.subtract)
                ins.then_inc(xt_free[s], 1)

            def body12(j):
                for s in range(2):
                    norm_tile(2 * j + s, s, P, bass.ds(2 * P * j + s * P, P))

            loop(eng, NC // 2, body12)
            norm_tile(NC, 0, TS, slice(SEQ, T))
            eng.wait_ge(gw_hi_done, 1)
            eng.tensor_tensor(gw_lo[:, :, :], gw_raw[:, :, :], f32(gw_hi[:, :, :]), ALU.subtract).then_inc(gw_lo_done, 1)

            def split_w(t, s):
                eng.wait_ge(w_hi_done, t + 1)
                eng.tensor_tensor(w_lo[s][:, :, :], w_raw[s][:, :, :], f32(w_hi[s][:, :, :]),
                                  ALU.subtract).then_inc(w_lo_done, 1)

            for s in range(2):
                split_w(s, s)
            count = [0]

            def step(ins):
                ins.then_inc(chain, 1)
                count[0] += 1
                eng.wait_ge(chain, count[0])

            step(eng.memset(graw[TS:P, NC, :], 0.0))
            eng.wait_ge(gate_tok, 1)
            eng.tensor_copy(graw[:, 0:NC, :].rearrange("p c h -> p (c h)"), psum[6][:, 0:NC * 2 * H])
            eng.tensor_copy(graw[0:TS, NC, :], psum[6][0:TS, NC * 2 * H:MT * 2 * H]).then_inc(graw_done, 1)
            eng.wait_ge(graw_done, 1)
            n = MT * H
            step(eng.tensor_tensor(sp[:, 0, 0:n].rearrange("p (c h) -> p c h", h=H), graw[:, :, H:2 * H],
                                   alog[:, H:2 * H].unsqueeze(1).to_broadcast([P, MT, H]), ALU.add))
            step(eng.tensor_scalar(sp[:, 0, n:], rg_par[:, 7, :], -1.0, None, ALU.mult))
            eng.scalar_tensor_tensor(out=sp[:, 1, :], in0=sp[:, 0, :], scalar=-1.0, in1=sp[:, 0, :],
                                     op0=ALU.mult, op1=ALU.max).then_inc(sp_arg, 1)
            eng.memset(rb_x[:, 0:HIST], 0.0)
            eng.memset(rb_gy[:, :], 0.0).then_inc(rg_init, 1)
            x, e, z, z2, acc = (sp[:, n, :] for n in range(5))
            eng.wait_ge(exp_done, 1)
            step(eng.tensor_scalar(z2, e, 2.0, None, ALU.add))
            step(eng.reciprocal(z2, z2))
            step(eng.tensor_tensor(z, e, z2, ALU.mult))
            step(eng.tensor_tensor(z2, z, z, ALU.mult))
            step(eng.tensor_scalar(acc, z2, 1 / 15, 1 / 13, ALU.mult, ALU.add))
            for c in (11, 9, 7, 5, 3, 1):
                step(eng.tensor_tensor(acc, acc, z2, ALU.mult))
                step(eng.tensor_scalar(acc, acc, 1 / c, None, ALU.add))
            step(eng.tensor_tensor(acc, acc, z, ALU.mult))
            step(eng.tensor_scalar(z, x, 0.0, None, ALU.max))
            step(eng.scalar_tensor_tensor(out=acc, in0=acc, scalar=2.0, in1=z, op0=ALU.mult, op1=ALU.add))
            n = MT * H
            eng.tensor_scalar(rg_calc[:, 0:2, :], rg_par[:, 5:7, :], 0.5, None, ALU.mult)
            eng.tensor_scalar(rg_calc[:, 2, :], acc[:, n:], 2.0, None, ALU.mult)
            eng.scalar_tensor_tensor(out=g[:, :, :], in0=acc[:, 0:n].rearrange("p (c h) -> p c h", h=H), scalar=-1.0,
                                     in1=alog[:, 0:H].unsqueeze(1).to_broadcast([P, MT, H]),
                                     op0=ALU.mult, op1=ALU.mult).then_inc(g_done, 1)
            eng.wait_ge(g_done, 1)
            eng.tensor_tensor(gblk[:, :, :], g[0:TS, NC, :].unsqueeze(1).to_broadcast([TS, NS, H]),
                              blk.unsqueeze(2).to_broadcast([TS, NS, H]), ALU.mult).then_inc(g_done, 1)

            def conv(dst, src, taps, bias, sem, done):
                if bias is None:
                    eng.tensor_scalar(dst, src[:, 0:WC], taps(0), None, ALU.mult).then_inc(sem, 1)
                else:
                    eng.tensor_scalar(dst, src[:, 0:WC], taps(0), bias, ALU.mult, ALU.add).then_inc(sem, 1)
                for q in range(1, 4):
                    eng.wait_ge(sem, done + q)
                    eng.scalar_tensor_tensor(out=dst, in0=src[:, q:q + WC], scalar=taps(q), in1=dst,
                                             op0=ALU.mult, op1=ALU.add).then_inc(sem, 1)

            def body13(j):
                one = bass.ds(j, 1)
                eng.wait_ge(evac_done, 2 * j + 2)
                eng.wait_ge(rg_hist, j + 1)
                eng.wait_ge(rg_sq, j)
                eng.tensor_copy(rg_now[:, :], rg_calc[:, :, one].squeeze(2))
                conv(rb_xc[:, 0:WC], rb_x, lambda q: rg_par[:, q, one], rg_par[:, 4, one], rg_conv, 4 * j)
                split_w(2 * j + 2, 0)
                split_w(2 * j + 3, 1)
                n = [0]

                def vec(ins, last=False):
                    ins.then_inc(rg_vec, 1)
                    n[0] += 1
                    if not last:
                        eng.wait_ge(rg_vec, VEC * j + n[0])

                u, a_, q_ = rb_xc[:, 0:WC], rb_t[:, 0:WC], rb_i[:, 0:WC]
                eng.wait_ge(rg_sq, j + 1)
                vec(eng.tensor_scalar(rb_r[:, 0:WC], a_, 1.0, None, ALU.add))
                vec(eng.reciprocal(rb_r[:, 0:WC], rb_r[:, 0:WC]))
                vec(eng.tensor_scalar(a_, rb_r[:, 0:WC], 2.0, -1.0, ALU.mult, ALU.add))
                vec(eng.scalar_tensor_tensor(out=q_, in0=q_, scalar=1.0, in1=u, op0=ALU.add, op1=ALU.mult))
                vec(eng.tensor_tensor(rb_sq[:, 0:WC], rb_sq[:, 0:WC], rb_r[:, 0:WC], ALU.mult))
                vec(eng.tensor_tensor(u, q_, rb_sq[:, 0:WC], ALU.mult))
                first = lambda row: sample_rows(row)[:, :, 0]
                vec(eng.tensor_tensor(rb_tmp[:, :], first(rb_t), rg_h0[:, one, :].squeeze(1), ALU.mult))
                vec(eng.tensor_tensor(first(rb_xc), first(rb_xc), rb_tmp[:, :], ALU.add))
                vec(eng.memset(first(rb_t), 0.0))
                vec(eng.tensor_tensor_scan(rb_h[:, 0:WC], a_, u, 0.0, ALU.mult, ALU.add))
                vec(eng.tensor_copy(st_h[:, one, 0:1].squeeze(1), rb_h[:, SEQ - 1:SEQ]), True)
                vec(eng.tensor_copy(st_h[:, one, 1:].squeeze(1), sample_rows(rb_h)[:, :, LS - 1]), True)
                vec(eng.tensor_tensor(by_sample(samp_rg[:, one, :].squeeze(1)), sample_rows(rb_gy)[:, :, 0:LS],
                                      sample_rows(rb_h)[:, :, 0:LS], ALU.mult), True)
                vec(eng.tensor_tensor(rb_gy[:, 0:SEQ], rb_gy[:, 0:SEQ], rb_h[:, 0:SEQ], ALU.mult), True)

            loop(eng, R, body13)
            eng.wait_ge(rg_out, 16 * R)
            eng.wait_ge(rg_state, 2 * R)
            for s in range(2):
                eng.memset(cb_x[s][:, 0:HIST], 0.0).then_inc(cb_init, 1)
            def body14(j):
                for s in range(2):
                    split_w(TZ + 2 * j + s + 2, s)
                    for n in range(2):
                        eng.wait_ge(wo_hi_done, 4 * j + 2 * s + n + 1)
                        eng.tensor_tensor(wo_lo[:, bass.ds(4 * j + 2 * s + n, 1), :].squeeze(1), wo_raw[n][:, :],
                                          f32(wo_hi[:, bass.ds(4 * j + 2 * s + n, 1), :].squeeze(1)),
                                          ALU.subtract).then_inc(wo_lo_done, 1)

            loop(eng, H // 2, body14)

            def qkv(j, prefetch):
                for s in range(2):
                    eng.wait_ge(evac_done, TQ + 2 * j + s + 2)
                    eng.wait_ge(cb_hist, 2 * j + s + 1)
                    eng.wait_ge(cb_out[s], 16 * j)
                    eng.wait_ge(cb_silu, 2 * j)
                    row = bass.ds(2 * j + s, 1)
                    conv(cb_y[s][:, 0:WC], cb_x[s], lambda q: conv_w[:, row, q], None, cb_conv, 8 * j + 4 * s)
                    if prefetch:
                        split_w(TQ + 2 * j + s + 2, s)

            for s in range(2):
                eng.wait_ge(z_out[s], 16 * H // 2)
            loop(eng, PAIRS - 1, lambda j: qkv(j, True))
            qkv(PAIRS - 1, False)

        @block.gpsimd
        def _(eng):
            eng.wait_ge(const_in, NCONST)

            def norm_tile(m, n):
                eng.wait_ge(ssq, m + 1)
                eng.tensor_tensor(stat[0:n, 0:1], stat[0:n, 0:1], eps_col[0:n, :], ALU.add).then_inc(root, 1)
                eng.wait_ge(root, 2 * m + 1)
                eng.tensor_tensor(stat[0:n, 1:2], stat[0:n, 0:1], minus_half[0:n, :], ALU.pow).then_inc(root, 1)

            def body16(m):
                norm_tile(m, P)

            loop(eng, NC, body16)
            norm_tile(NC, TS)

            def rows(buf, hist, state, t, ev, hist_done, state_done, free):
                for sem, v in free:
                    eng.wait_ge(sem, v)
                eng.tensor_copy(sample_rows(buf)[:, :, 0:HIST],
                                hist[:, bass.ds(t, 1), :].squeeze(1).rearrange("p (b r) -> p b r", r=HIST)
                                ).then_inc(hist_done, 1)
                eng.wait_ge(evac_done, ev)
                out = state[:, bass.ds(t, 1), :].squeeze(1)
                eng.tensor_copy(out[:, 0:HIST], buf[:, SEQ:SEQ + HIST]).then_inc(state_done, 1)
                eng.tensor_copy(out[:, HIST:].rearrange("p (b r) -> p b r", r=HIST),
                                sample_rows(buf)[:, :, LS:SROW]).then_inc(state_done, 1)

            eng.wait_ge(rg_init, 1)
            def body17(j):
                rows(rb_x, hist_rg, st_rg, j, 2 * j + 2, rg_hist, rg_state, [(rg_conv, 4 * j)])

            loop(eng, R, body17)
            eng.wait_ge(cb_init, 2)
            def body18(j):
                for s in range(2):
                    rows(cb_x[s], hist_g, st_g, 2 * j + s, TQ + 2 * j + s + 2, cb_hist, cb_state,
                         [(cb_conv, 8 * j)])

            loop(eng, PAIRS, body18)


def mixer_block(nc, i, o, scratch, psum, B, k):
    cst, ident, ht_hi, ht_lo, stat, normw = (k[n] for n in ("cst", "ident", "ht_hi", "ht_lo", "stat", "normw"))
    wo_hi, wo_lo, samp_qkv, samp_z, samp_rg = (k[n] for n in ("wo_hi", "wo_lo", "samp_qkv", "samp_z", "samp_rg"))
    beta, g, edec, esamp, expo, gnw = (k[n] for n in ("beta", "g", "edec", "esamp", "expo", "gnw"))
    minus_half, eps_col = k["minus_half"], k["eps_col"]
    tle, ugt, strict, ones, tle8, ugt8, strict8, blk, mlow = (
        k[n] for n in ("tle", "ugt", "strict", "ones", "tle8", "ugt8", "strict8", "blk", "mlow"))
    four = lambda name: B(name, [P, H, P])
    at = B.at
    qkv_in, q_in, rg_in, z_in = B("qkv_in", [P, QKV, P]), four("q_in"), four("rg_in"), four("z_in")
    x_in = B("x_in", [P, D])
    xn = B("xn2", [P, D])
    sq = xn[:, :].rearrange("p (t n) -> p t n", n=P)
    o_, on = four("o"), four("on")
    v_tok, kn, kg, ktail, kt = four("v_tok"), four("kn"), four("kg"), four("ktail"), four("kt")
    e_, u_, mq, pp, y_, x_ = four("decay"), four("u"), four("mq"), four("pp"), four("inv_t"), four("inv")
    st = four("state")
    vnew, nw, gr = kn, kt, kg
    mix_hi, mix_lo = B("mix_hi", [P, KT, P], F32R), B("mix_lo", [P, KT, P], F32R)
    sums = B("sums", [P, 2 * H])
    rn = B("rn", [P, 2 * H])
    epsq = B("epsq", [P, H])
    fac = B("fac", [P, 3, H])
    B = Plan(nc, at)
    s_states = [B(f"s_state{s}", [P, NS, P]) for s in range(3)]
    v_exp = xn[0:TS, :].rearrange("p (b d) -> p b d", d=P)
    assert B.at <= at + 4 * (QKV + 3 * H) * P

    S = nc.alloc_semaphore
    names = ("init_done q_ld qo_ld z_ld rg_ld x_ld n2_ld sq_done k_tr v_tr ss_mm rn_raw rn_done kn_done v_done "
             "kt_tr kt_done gr_done d_mm e_done e2_done ml_done kg_done ktail_done kk_mm qk_mm u1_done mq_done u_done "
             "ut_tr pp_done y_tr y_done x_done p_mm y_mm x_mm w_mm nw_done v_mm o1_mm vnew_done o2_mm ds_mm s_done "
             "t1_done o_done osq_done so_done fac_step fac_done on_done on_tr mix_done mixhi_done mixlo_done "
             "rghi_done rglo_done wo_mm x1_done ssq2 root2 xn_done hx_tr hhi_done hlo_done x1_out "
             "ss_ld0 ss_ld1 ss_ld2 ws_mm ws_ev vh_mm vh_done vexp_done dss_mm ss_dec ss_done ss_out0 ss_out1 ss_out2 sp_out").split()
    m_ = {n: S(f"mx_{n}") for n in names}
    NL = len(LEVELS)

    class Tile:

        def __init__(self, c):
            self.c = c
            self.samples = isinstance(c, int) and c == NC
            self.n = TS if self.samples else P
            self.levels = SAMPLE_LEVELS if self.samples else NL
            if self.samples:
                self.qkv, self.z, self.rg = samp_qkv, samp_z, samp_rg
                self.tle, self.ugt, self.strict = tle8, ugt8, strict8
            else:
                self.qkv, self.z, self.rg = qkv_in, z_in, rg_in
                self.tle, self.ugt, self.strict = tle, ugt, strict
            self.tok = slice(SEQ, T) if self.samples else bass.ds(P * c, P)

            self.q_o = samp_qkv if self.samples else q_in

        def col(self, t):
            return t[0:self.n, bass.ds(self.c, 1), :].squeeze(1)

    def spread(ap, n, m=P):
        return ap.unsqueeze(2).to_broadcast([n, H, m])

    def over(ap, n):
        return ap.unsqueeze(1).to_broadcast([n, H, ap.shape[1]])

    def b4(q, n=P, m=P):
        return psum[q][0:n, :].rearrange("p (h m) -> p h m", m=P)[:, :, 0:m]

    def chunked(rows, c):
        return rows.rearrange("t p (c n) -> c p t n", n=P)[bass.ds(c, 1)].squeeze(0)

    def token_rows(a, t):
        return a[SEQ:T, :] if t.samples else a[0:SEQ, :].rearrange("(c p) d -> c p d", p=P)[bass.ds(t.c, 1)].squeeze(0)

    P_BANK, Y_BANK, X_BANK = (5, 2), (6, 3), (7, 4)

    def mlow2(q, n):
        return over(mlow[q][0:n, 0:n], n)[:, 0:2]

    def pair_of(ap, n, r, m=P):
        return ap[0:n, 2 * r:2 * r + 2, 0:m]

    with nc.Block() as block:

        @block.sync
        def _(eng):
            eng.dma_start(normw[:, :], i["norm2"]).then_inc(m_["n2_ld"], 16)

            def load_qkv(c):
                eng.dma_start(qkv_in[:, :, :], chunked(scratch["qkv"], c)).then_inc(m_["q_ld"], 16)

            def chunk(c, more):
                eng.wait_ge(m_["o1_mm"], c)
                eng.dma_start(q_in[:, :, :], chunked(scratch["qkv"][0:H], c)).then_inc(m_["qo_ld"], 16)
                eng.wait_ge(m_["mix_done"], c)
                eng.dma_start(z_in[:, :, :], chunked(scratch["z"], c)).then_inc(m_["z_ld"], 16)
                eng.wait_ge(m_["rghi_done"], c)
                eng.wait_ge(m_["rglo_done"], c)
                eng.dma_start(rg_in[:, :, :], chunked(scratch["rg"], c)).then_inc(m_["rg_ld"], 16)
                if more:
                    eng.wait_ge(m_["qk_mm"], c + 1)
                    load_qkv(c + 1)

            def residual(c, stored):
                t = Tile(c)
                if stored:
                    store_x1(Tile(c - 1))
                eng.wait_ge(m_["x1_out"], 16 * c)
                eng.wait_ge(m_["xn_done"], c)
                eng.dma_start(x_in[0:t.n, :], token_rows(i["x"], t)).then_inc(m_["x_ld"], 16)

            def store_x1(t):
                eng.wait_ge(m_["x1_done"], 2 * (t.c + 1))
                eng.dma_start(token_rows(scratch["x1"], t), x_in[0:t.n, :]).then_inc(m_["x1_out"], 16)

            load_qkv(0)
            chunk(0, True)
            residual(0, False)
            with eng.Fori(1, NC - 1) as c:
                chunk(c, True)
                residual(c, True)
            chunk(NC - 1, False)
            residual(NC - 1, True)

            def load_states(h):
                eng.dma_start(s_states[h % 3][:, :, :], i["state_S"][h]).then_inc(m_[f"ss_ld{h % 3}"], 16)

            eng.wait_ge(m_["qk_mm"], NC)
            load_states(0)
            eng.wait_ge(m_["s_done"], NC)
            eng.dma_start(o["S_prompt"], st[:, :, :]).then_inc(m_["sp_out"], 16)
            eng.wait_ge(m_["o1_mm"], NC)
            load_states(1)
            eng.wait_ge(m_["mix_done"], NC)
            eng.wait_ge(m_["rghi_done"], NC)
            eng.wait_ge(m_["rglo_done"], NC)
            load_states(2)
            residual(NC, True)
            for h in range(H):
                eng.wait_ge(m_["ss_done"], h + 1)
                eng.dma_start(o["S_sample"][h], s_states[h % 3][:, :, :]).then_inc(m_[f"ss_out{h % 3}"], 16)
                if h + 3 < H:
                    eng.wait_ge(m_[f"ss_out{h % 3}"], 16 * (h // 3 + 1))
                    load_states(h + 3)
            store_x1(Tile(NC))
            for s in range(3):
                eng.wait_ge(m_[f"ss_out{s}"], 16 * (2 if s == 0 else 1))
            eng.wait_ge(m_["sp_out"], 16)
            eng.wait_ge(m_["x1_out"], 16 * MT)

        @block.tensor
        def _(eng):

            def turn_o(t):
                eng.wait_ge(m_["on_done"], t.c + 1)
                for h in range(H):
                    mm = eng.transpose(psum[6][:, h * P:h * P + t.n], on[0:t.n, h, :], ident[0:t.n, 0:t.n])
                mm.then_inc(m_["on_tr"], 1)

            def project(t, steps):
                for half, f in steps:
                    if (half, f) == (0, 0):
                        eng.wait_ge(m_["hlo_done"], 2 * t.c)
                        eng.wait_ge(m_["rglo_done"], t.c + 1)
                    if (half, f) == (0, R):
                        eng.wait_ge(m_["mixlo_done"], t.c + 1)
                    cols = slice(half * BANK, (half + 1) * BANK)
                    mm = mm3(eng, psum[half][0:t.n, :], mix_hi[:, f, 0:t.n], mix_lo[:, f, 0:t.n],
                             wo_hi[:, f, cols], wo_lo[:, f, cols], f == 0, f == KT - 1)
                    if f == KT - 1:
                        mm.then_inc(m_["wo_mm"], 1)

            def turn_x(t, half):
                eng.wait_ge(m_["xn_done"], t.c + 1)
                for kk in range(4):
                    f = 4 * half + kk
                    mm = eng.transpose(psum[half][:, kk * P:kk * P + t.n], xn[0:t.n, f * P:(f + 1) * P],
                                       ident[0:t.n, 0:t.n])
                mm.then_inc(m_["hx_tr"], 1)

            rg_steps = [(half, f) for half in range(2) for f in range(R)]
            o_steps = [(half, f) for half in range(2) for f in range(R, KT)]

            def chunk(c, tail):
                t = Tile(c)
                n = t.n
                if not t.samples:
                    eng.wait_ge(m_["q_ld"], 16 * (c + 1))
                eng.wait_ge(m_["vnew_done"], c)
                eng.wait_ge(m_["t1_done"], c)
                for q, off, sem in ((2, H, "k_tr"), (3, 2 * H, "v_tr")):
                    for h in range(H):
                        mm = eng.transpose(psum[q][0:n, h * P:(h + 1) * P], t.qkv[:, off + h, 0:n], ident)
                    mm.then_inc(m_[sem], 1)
                eng.wait_ge(m_["sq_done"], c + 1)
                eng.wait_ge(m_["s_done"], c)
                for h in range(2 * H):
                    mm = eng.matmul(psum[7][0:n, h:h + 1], sq[:, h, 0:n], ones[:, 0:1], start=True, stop=True)
                mm.then_inc(m_["ss_mm"], 1)
                eng.wait_ge(m_["gr_done"], c + 1)
                eng.wait_ge(m_["o_done"], c)
                eng.matmul(b4(5, n, n), t.ugt, gr[0:n, :, 0:n], start=True, stop=True).then_inc(m_["d_mm"], 1)
                if tail:
                    project(tail, rg_steps[0:3])
                eng.wait_ge(m_["kn_done"], c + 1)
                eng.wait_ge(m_["nw_done"], c)
                for h in range(H):
                    mm = eng.transpose(psum[4][:, h * P:h * P + n], kn[0:n, h, :], ident[0:n, 0:n])
                mm.then_inc(m_["kt_tr"], 1)
                if tail:
                    project(tail, rg_steps[3:5])
                eng.wait_ge(m_["kt_done"], c + 1)
                for h in range(H):
                    mm = eng.matmul(psum[2][0:n, h * P:h * P + n], kt[:, h, 0:n], kt[:, h, 0:n], start=True, stop=True)
                mm.then_inc(m_["kk_mm"], 1)
                eng.wait_ge(m_["v_done"], c + 1)
                for h in range(H):
                    mm = eng.matmul(psum[3][0:n, h * P:h * P + n], kt[:, h, 0:n], t.qkv[:, h, 0:n],
                                    start=True, stop=True)
                mm.then_inc(m_["qk_mm"], 1)
                if tail:
                    turn_o(tail)
                eng.wait_ge(m_["u_done"], c + 1)
                for h in range(H):
                    mm = eng.transpose(psum[4][0:n, h * P:h * P + n], u_[0:n, h, 0:n], ident[0:n, 0:n])
                mm.then_inc(m_["ut_tr"], 1)
                if tail:
                    project(tail, rg_steps[5:])
                eng.wait_ge(m_["mix_done"], c)
                eng.wait_ge(m_["mq_done"], c + 1)
                for r in range(2):
                    eng.wait_ge(m_["pp_done"], 2 * NL * c + r + 1)
                    for h in (2 * r, 2 * r + 1):
                        mm = eng.transpose(psum[Y_BANK[r]][0:n, h * P:h * P + n], pp[0:n, h, 0:n], ident[0:n, 0:n])
                    mm.then_inc(m_["y_tr"], 1)
                per_slot = 2 if t.samples else 1
                for q in range(1, t.levels):
                    last = q == t.levels - 1
                    slots = [o_steps[(2 * (q - 1) + s) * per_slot:(2 * (q - 1) + s + 1) * per_slot] for s in range(2)]
                    for r in range(2):
                        eng.wait_ge(m_["x_done"], 2 * (NL - 1) * c + 2 * (q - 1) + r + 1)
                        for h in (2 * r, 2 * r + 1):
                            mm = eng.matmul(psum[P_BANK[r]][0:n, h * P:h * P + n], u_[0:n, h, 0:n], x_[0:n, h, 0:n],
                                            start=True, stop=True)
                        mm.then_inc(m_["p_mm"], 1)
                    if tail:
                        project(tail, slots[0])
                    for r in range(2):
                        eng.wait_ge(m_["y_done"], 2 * NL * c + 2 * (q - 1) + r + 1)
                        eng.wait_ge(m_["pp_done"], 2 * NL * c + 2 * q + r + 1)
                        for h in (2 * r, 2 * r + 1):
                            mm = eng.matmul(psum[Y_BANK[r]][0:n, h * P:h * P + n], pp[0:n, h, 0:n], y_[0:n, h, 0:n],
                                            start=True, stop=True)
                        mm.then_inc(m_["y_mm"], 1)
                        if not last:
                            for h in (2 * r, 2 * r + 1):
                                mm = eng.matmul(psum[X_BANK[r]][0:n, h * P:h * P + n], y_[0:n, h, 0:n],
                                                pp[0:n, h, 0:n], start=True, stop=True)
                            mm.then_inc(m_["x_mm"], 1)
                    if tail:
                        project(tail, slots[1])
                if tail and not t.samples:
                    turn_x(tail, 0)
                eng.wait_ge(m_["y_done"], 2 * NL * c + 2 * t.levels)
                eng.wait_ge(m_["kg_done"], c + 1)
                for h in range(H):
                    mm = eng.matmul(psum[4][:, h * P:h * P + n], kg[0:n, h, :], y_[0:n, h, 0:n], start=True, stop=True)
                mm.then_inc(m_["w_mm"], 1)
                if tail:
                    if t.samples:
                        turn_x(tail, 0)
                    turn_x(tail, 1)
                eng.wait_ge(m_["nw_done"], c + 1)
                if t.samples:
                    samples_states(t)
                else:
                    eng.wait_ge(m_["s_done"], c)
                    eng.wait_ge(m_["init_done"], 1)
                    for h in range(H):
                        eng.matmul(psum[2][:, h * P:(h + 1) * P], y_[:, h, :], v_tok[:, h, :], start=True, stop=False)
                        mm = eng.matmul(psum[2][:, h * P:(h + 1) * P], nw[:, h, :], st[:, h, :],
                                        start=False, stop=True)
                    mm.then_inc(m_["v_mm"], 1)
                    eng.wait_ge(m_["mq_done"], c + 1)
                    eng.wait_ge(m_["qo_ld"], 16 * (c + 1))
                    for h in range(H):
                        mm = eng.matmul(psum[3][:, h * P:(h + 1) * P], q_in[:, h, :], st[:, h, :],
                                        start=True, stop=True)
                    mm.then_inc(m_["o1_mm"], 1)
                    eng.wait_ge(m_["vnew_done"], c + 1)
                    eng.wait_ge(m_["ktail_done"], c + 1)
                    for h in range(H):
                        mm = eng.matmul(psum[7][:, h * P:(h + 1) * P], ktail[:, h, :], vnew[:, h, :],
                                        start=True, stop=True)
                    mm.then_inc(m_["ds_mm"], 1)
                for h in range(H):
                    mm = eng.matmul(psum[5][0:n, h * P:(h + 1) * P], mq[0:n, h, 0:n], vnew[0:n, h, :],
                                    start=True, stop=True)
                mm.then_inc(m_["o2_mm"], 1)

            def samples_states(t):
                eng.wait_ge(m_["mq_done"], NC + 1)

                def state_products(h):
                    eng.wait_ge(m_[f"ss_ld{h % 3}"], 16 * (h // 3 + 1))
                    eng.wait_ge(m_["ws_ev"], h - h % 2)
                    for q, src in enumerate((nw, samp_qkv)):
                        for b in range(NS):
                            mm = eng.matmul(psum[4 + h % 2][:, q * TS + b * LS:q * TS + (b + 1) * LS],
                                            s_states[h % 3][:, b, :], src[:, h, b * LS:(b + 1) * LS],
                                            start=True, stop=True)
                    mm.then_inc(m_["ws_mm"], 1)

                for h in range(H):
                    if h % 2 == 0:
                        state_products(h)
                        state_products(h + 1)
                    eng.wait_ge(m_["ws_ev"], h + 1)
                    hs = slice(h * P, (h + 1) * P)
                    eng.wait_ge(m_["vh_done"], h)
                    eng.matmul(psum[2][0:TS, hs], y_[0:TS, h, 0:TS], v_tok[0:TS, h, :], start=True, stop=False)
                    eng.matmul(psum[2][0:TS, hs], x_[:, h, 0:TS], ident, start=False, stop=True)
                    eng.matmul(psum[3][0:TS, hs], x_[:, h, TS:2 * TS], ident,
                               start=True, stop=True).then_inc(m_["vh_mm"], 1)
                    eng.wait_ge(m_["vexp_done"], h + 1)
                    eng.wait_ge(m_["ktail_done"], NC + 1)
                    eng.wait_ge(m_["ss_done"], h)
                    for q in range(2):
                        mm = eng.matmul(psum[6 + q][:, :], ktail[0:TS, h, :],
                                        v_exp[:, 4 * q:4 * q + 4, :].rearrange("p b d -> p (b d)"),
                                        start=True, stop=True)
                    mm.then_inc(m_["dss_mm"], 1)
                eng.wait_ge(m_["ss_done"], H)

            chunk(0, None)
            with eng.Fori(1, NC) as c:
                chunk(c, Tile(c - 1))
            chunk(NC, Tile(NC - 1))
            end = Tile(NC)
            turn_o(end)
            project(end, rg_steps + o_steps)
            for half in range(2):
                turn_x(end, half)

        @block.scalar
        def _(eng):

            def square_o(t):
                eng.wait_ge(m_["o_done"], t.c + 1)
                eng.activation(on[0:t.n, :, :], o_[0:t.n, :, :], ACT.Square, scale=1.0 / P).then_inc(m_["osq_done"], 1)

            def mix(t):
                eng.wait_ge(m_["mix_done"], t.c + 1)
                eng.activation(mix_hi[:, R:KT, 0:t.n], o_[:, :, 0:t.n], ACT.Copy).then_inc(m_["mixhi_done"], 1)

            def square_x(t):
                eng.wait_ge(m_["x1_done"], 2 * (t.c + 1))
                eng.activation(xn[0:t.n, :], x_in[0:t.n, :], ACT.Square, scale=D ** -0.5,
                               accum_out=stat[0:t.n, 0:1]).then_inc(m_["ssq2"], 1)

            def split_x(t, half):
                eng.wait_ge(m_["hx_tr"], 2 * t.c + half + 1)
                eng.activation(ht_hi[:, 4 * half:4 * half + 4, t.tok], b4(half, P, t.n),
                               ACT.Copy).then_inc(m_["hhi_done"], 1)

            def chunk(c, tail):
                t = Tile(c)
                n = t.n
                if not t.samples:
                    eng.wait_ge(m_["q_ld"], 16 * (c + 1))
                eng.wait_ge(m_["v_mm"], c)
                eng.activation(sq[:, :, 0:n], t.qkv[:, 0:2 * H, 0:n], ACT.Square).then_inc(m_["sq_done"], 1)
                if tail:
                    square_o(tail)
                eng.wait_ge(m_["v_tr"], c + 1)
                eng.activation(v_tok[0:n, :, :], b4(3, n), ACT.Copy).then_inc(m_["v_done"], 1)
                eng.wait_ge(m_["d_mm"], c + 1)
                eng.activation(e_[0:n, :, 0:n], b4(5, n, n), ACT.Exp).then_inc(m_["e_done"], 1)
                eng.wait_ge(m_["kt_tr"], c + 1)
                eng.activation(kt[:, :, 0:n], b4(4, P, n), ACT.Copy).then_inc(m_["kt_done"], 1)
                if tail:
                    mix(tail)
                    square_x(tail)
                eng.wait_ge(m_["w_mm"], c + 1)
                eng.activation(nw[:, :, 0:n], b4(4, P, n), ACT.Copy, scale=-1.0).then_inc(m_["nw_done"], 1)
                if not t.samples:
                    eng.wait_ge(m_["rg_ld"], 16 * (c + 1))
                eng.wait_ge(m_["wo_mm"], 2 * c)
                eng.activation(mix_hi[:, 0:R, 0:n], t.rg[:, :, 0:n], ACT.Copy).then_inc(m_["rghi_done"], 1)
                if tail:
                    for half in range(2):
                        split_x(tail, half)
                if t.samples:
                    for h in range(H):
                        eng.wait_ge(m_["ws_mm"], h + 1)
                        eng.activation(x_[:, h, :], psum[4 + h % 2][:, 0:2 * TS], ACT.Copy).then_inc(m_["ws_ev"], 1)

            chunk(0, None)
            with eng.Fori(1, NC) as c:
                chunk(c, Tile(c - 1))
            chunk(NC, Tile(NC - 1))
            end = Tile(NC)
            square_o(end)
            mix(end)
            square_x(end)
            for half in range(2):
                split_x(end, half)

        @block.vector
        def _(eng):
            eng.tensor_scalar(fac[:, 2, 0:1], gnw[:, :], P ** -0.5, None, ALU.mult)
            eng.memset(st[:, :, :], 0.0).then_inc(m_["init_done"], 1)

            def sum_o(t):
                eng.wait_ge(m_["osq_done"], t.c + 1)
                eng.tensor_reduce(fac[0:t.n, 0, :], on[0:t.n, :, :], AX, ALU.add).then_inc(m_["so_done"], 1)

            def norm_o(t):
                eng.wait_ge(m_["fac_done"], t.c + 1)
                eng.tensor_tensor(on[0:t.n, :, :], o_[0:t.n, :, :], spread(fac[0:t.n, 1, :], t.n),
                                  ALU.mult).then_inc(m_["on_done"], 1)

            def mix(t):
                eng.wait_ge(m_["on_tr"], t.c + 1)
                if not t.samples:
                    eng.wait_ge(m_["z_ld"], 16 * (t.c + 1))
                eng.wait_ge(m_["init_done"], 1)
                eng.scalar_tensor_tensor(out=o_[:, :, 0:t.n], in0=b4(6, P, t.n), scalar=fac[:, 2, 0:1],
                                         in1=t.z[:, :, 0:t.n], op0=ALU.mult, op1=ALU.mult).then_inc(m_["mix_done"], 1)

            def mix_low(t):
                eng.wait_ge(m_["mixhi_done"], t.c + 1)
                eng.tensor_tensor(mix_lo[:, R:KT, 0:t.n], o_[:, :, 0:t.n], f32(mix_hi[:, R:KT, 0:t.n]),
                                  ALU.subtract).then_inc(m_["mixlo_done"], 1)

            def add_x(t, half):
                part = x_in[0:t.n, half * BANK:(half + 1) * BANK]
                eng.wait_ge(m_["x_ld"], 16 * (t.c + 1))
                eng.wait_ge(m_["wo_mm"], 2 * t.c + half + 1)
                eng.tensor_tensor(part, part, psum[half][0:t.n, :], ALU.add).then_inc(m_["x1_done"], 1)

            def norm_x(t):
                eng.wait_ge(m_["n2_ld"], 16)
                eng.wait_ge(m_["root2"], 2 * t.c + 2)
                eng.scalar_tensor_tensor(out=xn[0:t.n, :], in0=x_in[0:t.n, :], scalar=stat[0:t.n, 1:2],
                                         in1=normw[0:t.n, :], op0=ALU.mult, op1=ALU.mult).then_inc(m_["xn_done"], 1)

            def split_x(t, half):
                eng.wait_ge(m_["hhi_done"], 2 * t.c + half + 1)
                eng.tensor_tensor(ht_lo[:, 4 * half:4 * half + 4, t.tok], b4(half, P, t.n),
                                  f32(ht_hi[:, 4 * half:4 * half + 4, t.tok]),
                                  ALU.subtract).then_inc(m_["hlo_done"], 1)

            def chunk(c, tail):
                t = Tile(c)
                n = t.n
                if tail:
                    sum_o(tail)
                eng.wait_ge(m_["ss_mm"], c + 1)
                eng.wait_ge(m_["rn_done"], c)
                eng.tensor_scalar(sums[0:n, :], psum[7][0:n, 0:2 * H], EPS, None, ALU.add).then_inc(m_["rn_raw"], 1)
                eng.wait_ge(m_["k_tr"], c + 1)
                eng.wait_ge(m_["rn_done"], c + 1)
                eng.tensor_tensor(kn[0:n, :, :], b4(2, n), spread(rn[0:n, H:], n),
                                  ALU.mult).then_inc(m_["kn_done"], 1)
                if tail:
                    norm_o(tail)
                eng.wait_ge(m_["kk_mm"], c + 1)
                eng.wait_ge(m_["e2_done"], c + 1)
                eng.tensor_tensor(u_[0:n, :, 0:n], b4(2, n, n), e_[0:n, :, 0:n], ALU.mult).then_inc(m_["u1_done"], 1)
                eng.wait_ge(m_["u1_done"], c + 1)
                eng.wait_ge(m_["ml_done"], c + 1)
                eng.tensor_tensor(u_[0:n, :, 0:n], u_[0:n, :, 0:n], x_[0:n, :, 0:n], ALU.mult).then_inc(m_["u_done"], 1)
                eng.wait_ge(m_["qk_mm"], c + 1)
                eng.tensor_tensor(mq[0:n, :, 0:n], b4(3, n, n), e_[0:n, :, 0:n], ALU.mult).then_inc(m_["mq_done"], 1)
                eng.wait_ge(m_["ut_tr"], c + 1)
                eye = over(ident[0:n, 0:n], n)
                for r in range(2):
                    eng.tensor_tensor(pair_of(pp, n, r, n), pair_of(b4(4), n, r, n), mlow2(0, n),
                                      ALU.mult).then_inc(m_["pp_done"], 1)
                if tail:
                    mix(tail)
                for r in range(2):
                    eng.wait_ge(m_["pp_done"], 2 * NL * c + r + 1)
                    eng.tensor_tensor(pair_of(x_, n, r, n), eye[:, 0:2], pair_of(pp, n, r, n),
                                      ALU.subtract).then_inc(m_["x_done"], 1)
                for r in range(2):
                    eng.wait_ge(m_["y_tr"], 2 * c + r + 1)
                    eng.tensor_tensor(pair_of(y_, n, r, n), eye[:, 0:2], pair_of(b4(Y_BANK[r]), n, r, n),
                                      ALU.subtract).then_inc(m_["y_done"], 1)
                if tail:
                    mix_low(tail)
                for q in range(1, t.levels):
                    last = q == t.levels - 1
                    for r in range(2):
                        eng.wait_ge(m_["p_mm"], 2 * (NL - 1) * c + 2 * (q - 1) + r + 1)
                        eng.tensor_tensor(pair_of(pp, n, r, n), pair_of(b4(P_BANK[r]), n, r, n), mlow2(q, n),
                                          ALU.mult).then_inc(m_["pp_done"], 1)
                    if tail and not t.samples:
                        if q in (3, 5):
                            add_x(tail, (q - 3) // 2)
                        if q == 6:
                            norm_x(tail)
                    if tail and t.samples and q == 2:
                        add_x(tail, 0)
                    for r in range(2):
                        eng.wait_ge(m_["y_mm"], 2 * (NL - 1) * c + 2 * (q - 1) + r + 1)
                        if not last:
                            eng.wait_ge(m_["x_mm"], 2 * (NL - 2) * c + 2 * (q - 1) + r + 1)
                        eng.tensor_tensor(pair_of(y_, n, r, n), pair_of(y_, n, r, n), pair_of(b4(Y_BANK[r]), n, r, n),
                                          ALU.subtract).then_inc(m_["y_done"], 1)
                        if not last:
                            eng.tensor_tensor(pair_of(x_, n, r, n), pair_of(x_, n, r, n),
                                              pair_of(b4(X_BANK[r]), n, r, n), ALU.subtract).then_inc(m_["x_done"], 1)
                if tail and t.samples:
                    add_x(tail, 1)
                    norm_x(tail)
                if t.samples:
                    for half in range(2):
                        split_x(tail, half)
                    samples_states(n)
                else:
                    eng.wait_ge(m_["v_mm"], c + 1)
                    eng.wait_ge(m_["kg_done"], c + 1)
                    eng.wait_ge(m_["ktail_done"], c + 1)
                    eng.tensor_tensor(vnew[:, :, :], b4(2), spread(t.col(beta), n), ALU.mult).then_inc(m_["vnew_done"], 1)
                    if tail:
                        for half in range(2):
                            split_x(tail, half)
                    eng.wait_ge(m_["o1_mm"], c + 1)
                if tail:
                    eng.wait_ge(m_["mixlo_done"], c)
                eng.tensor_tensor(o_[0:n, :, :], b4(3, n), spread(edec[0:n, 0, bass.ds(c, 1), :].squeeze(1), n),
                                  ALU.mult).then_inc(m_["t1_done"], 1)
                if not t.samples:
                    eng.wait_ge(m_["ds_mm"], c + 1)
                    for h in range(H):
                        ins = eng.scalar_tensor_tensor(out=st[:, h, :], in0=st[:, h, :],
                                                       scalar=edec[:, 2, bass.ds(c, 1), h], in1=b4(7)[:, h, :],
                                                       op0=ALU.mult, op1=ALU.add)
                    ins.then_inc(m_["s_done"], 1)
                eng.wait_ge(m_["o2_mm"], c + 1)
                eng.wait_ge(m_["t1_done"], c + 1)
                eng.tensor_tensor(o_[0:n, :, :], o_[0:n, :, :], b4(5, n), ALU.add).then_inc(m_["o_done"], 1)

            def samples_states(n):
                for h in range(H):
                    state = s_states[h % 3]
                    eng.wait_ge(m_["kg_done"], NC + 1)
                    eng.wait_ge(m_["ktail_done"], NC + 1)
                    eng.wait_ge(m_["vh_mm"], h + 1)
                    eng.tensor_scalar(vnew[0:n, h, :], psum[2][0:n, h * P:(h + 1) * P],
                                      beta[0:n, NC, h:h + 1], None, ALU.mult).then_inc(m_["vh_done"], 1)
                    eng.wait_ge(m_["vh_done"], h + 1)
                    eng.wait_ge(m_["hx_tr"], 2 * NC)
                    eng.tensor_tensor(v_exp[:, :, :], vnew[0:n, h, :].unsqueeze(1).to_broadcast([n, NS, P]),
                                      blk.unsqueeze(2).to_broadcast([n, NS, P]),
                                      ALU.mult).then_inc(m_["vexp_done"], 1)
                    eng.wait_ge(m_["ws_mm"], h + 1)
                    eng.tensor_tensor(state[:, :, :], state[:, :, :],
                                      esamp[:, :, h:h + 1].to_broadcast([P, NS, P]),
                                      ALU.mult).then_inc(m_["ss_dec"], 1)
                    eng.wait_ge(m_["ss_dec"], h + 1)
                    eng.wait_ge(m_["dss_mm"], h + 1)
                    for q in range(2):
                        part = state[:, 4 * q:4 * q + 4, :]
                        ins = eng.tensor_tensor(part, part, b4(6 + q), ALU.add)
                    ins.then_inc(m_["ss_done"], 1)

            chunk(0, None)
            with eng.Fori(1, NC) as c:
                chunk(c, Tile(c - 1))
            chunk(NC, Tile(NC - 1))
            end = Tile(NC)
            sum_o(end)
            norm_o(end)
            mix(end)
            mix_low(end)
            for half in range(2):
                add_x(end, half)
            norm_x(end)
            for half in range(2):
                split_x(end, half)

        @block.gpsimd
        def _(eng):

            def scale_o(t):
                so, f = fac[0:t.n, 0, :], fac[0:t.n, 1, :]
                eng.wait_ge(m_["so_done"], t.c + 1)
                eng.tensor_tensor(so, so, epsq[0:t.n, :], ALU.add).then_inc(m_["fac_step"], 1)
                eng.wait_ge(m_["on_done"], t.c)
                eng.wait_ge(m_["fac_step"], t.c + 1)
                eng.tensor_tensor(f, so, expo[0:t.n, 0:H], ALU.pow).then_inc(m_["fac_done"], 1)

            def root_x(t):
                eng.wait_ge(m_["ssq2"], t.c + 1)
                eng.tensor_tensor(stat[0:t.n, 0:1], stat[0:t.n, 0:1], eps_col[0:t.n, :], ALU.add).then_inc(m_["root2"], 1)
                eng.wait_ge(m_["root2"], 2 * t.c + 1)
                eng.tensor_tensor(stat[0:t.n, 1:2], stat[0:t.n, 0:1], minus_half[0:t.n, :],
                                  ALU.pow).then_inc(m_["root2"], 1)

            def chunk(c, tail):
                t = Tile(c)
                n = t.n
                eng.wait_ge(m_["w_mm"], c)
                eng.tensor_tensor(gr[0:n, :, 0:n], over(t.tle, n), spread(t.col(g), n, n),
                                  ALU.mult).then_inc(m_["gr_done"], 1)
                if tail:
                    scale_o(tail)
                eng.wait_ge(m_["rn_raw"], c + 1)
                eng.tensor_tensor(epsq[0:n, :], sums[0:n, 0:H], expo[0:n, 2 * H:], ALU.mult)
                eng.tensor_tensor(rn[0:n, :], sums[0:n, :], expo[0:n, 0:2 * H], ALU.pow).then_inc(m_["rn_done"], 1)
                eng.wait_ge(m_["w_mm"], c)
                eng.tensor_tensor(x_[0:n, :, 0:n], over(t.strict, n), spread(t.col(beta), n, n),
                                  ALU.mult).then_inc(m_["ml_done"], 1)
                eng.wait_ge(m_["e_done"], c + 1)
                eng.tensor_tensor(e_[0:n, :, 0:n], e_[0:n, :, 0:n], over(t.tle, n), ALU.mult).then_inc(m_["e2_done"], 1)
                eng.wait_ge(m_["kn_done"], c + 1)
                eng.tensor_tensor(kg[0:n, :, :], kn[0:n, :, :], spread(edec[0:n, 0, bass.ds(c, 1), :].squeeze(1), n),
                                  ALU.mult).then_inc(m_["kg_done"], 1)
                eng.tensor_tensor(ktail[0:n, :, :], kn[0:n, :, :], spread(edec[0:n, 1, bass.ds(c, 1), :].squeeze(1), n),
                                  ALU.mult).then_inc(m_["ktail_done"], 1)
                if tail:
                    root_x(tail)
                eng.wait_ge(m_["rghi_done"], c + 1)
                eng.tensor_tensor(mix_lo[:, 0:R, 0:n], t.rg[:, :, 0:n], f32(mix_hi[:, 0:R, 0:n]),
                                  ALU.subtract).then_inc(m_["rglo_done"], 1)

            chunk(0, None)
            with eng.Fori(1, NC) as c:
                chunk(c, Tile(c - 1))
            chunk(NC, Tile(NC - 1))
            scale_o(Tile(NC))
            root_x(Tile(NC))



def ffn_block(nc, i, o, scratch, psum, B, k):
    ht_hi, ht_lo, normw, minus_half, eps_col = (k[n] for n in ("ht_hi", "ht_lo", "normw", "minus_half", "eps_col"))
    acc = B("acc", [P, MT, D])
    h_hi = B("h_hi", [P, 2, T], F32R)
    h_lo = B("h_lo", [P, 2, T], F32R)
    gu_hi = [B(f"gu_hi{s}", [P, 2, KT, P], F32R) for s in range(2)]
    gu_lo = [B(f"gu_lo{s}", [P, 2, KT, P], F32R) for s in range(2)]
    dn_hi = B("dn_hi", [P, 2, D], F32R)
    dn_lo = B("dn_lo", [P, 2, D], F32R)
    most = max(m for _, m in GROUPS)
    sg = [B(f"sg{s}", [P, most]) for s in range(2)]
    hf = [B(f"hf{s}", [P, most]) for s in range(2)]
    fstat = B("fstat", [P, MT, 2])
    raw_at = B.at
    gu_raw = [B(f"gu_raw{s}", [P, 2, KT, P]) for s in range(2)]
    dn_raw = B("dn_raw", [P, 2, D])
    B = Plan(nc, raw_at)
    y_out = [B(f"y_out{s}", [P, D]) for s in range(2)]

    S = nc.alloc_semaphore
    x1_in, n3_in = S("ff_x1_in"), S("ff_n3_in")
    gu_in, dn_in = [S(f"gu_in{s}") for s in range(2)], S("dn_in")
    gu_hi_done, gu_lo_done, dn_hi_done, dn_lo_done = S("gu_hi_done"), S("gu_lo_done"), S("dn_hi_done"), S("dn_lo_done")
    gu_mm, sg_done, hf_done, h_hi_done, h_lo_done = S("gu_mm"), S("sg_done"), S("hf_done"), S("h_hi_done"), S("h_lo_done")
    dn_mm, acc_done = S("dn_mm"), S("acc_done")
    ssq, root, y_done, y_dma = S("ff_ssq"), S("ff_root"), S("ff_y_done"), [S(f"y_dma{s}") for s in range(2)]
    NG = len(GROUPS)
    PAIR = 2 * NG
    SUMS = 2 * MT
    NP = FT // 2

    def group_of(m):
        last = min((m + 1) * P, T) - 1
        return next(n for n, (a, ln) in enumerate(GROUPS) if last < a + ln)

    def first(n):
        return isinstance(n, int) and n < 2

    with nc.Block() as block:

        @block.sync
        def _(eng):
            def load_gu(j, s):
                t = 2 * j + s
                for q, name in enumerate(("w_gate", "w_up")):
                    eng.dma_start(gu_raw[s][:, q], i[name][bass.ds(t, 1)].squeeze(0)).then_inc(gu_in[s], 16)

            def load_dn(j):
                eng.dma_start(dn_raw[:, :, :], i["w_down"].rearrange("(j s) p d -> j p s d", s=2)[bass.ds(j, 1)]
                              .squeeze(0)).then_inc(dn_in, 16)

            load_gu(0, 0)
            load_gu(0, 1)
            load_dn(0)
            eng.dma_start(acc[:, 0:NC, :], scratch["x1"][0:SEQ, :].rearrange("(c p) d -> p c d", p=P)).then_inc(x1_in, 16)
            eng.dma_start(acc[0:TS, NC, :], scratch["x1"][SEQ:T, :]).then_inc(x1_in, 16)
            eng.dma_start(normw[:, :], i["norm3"]).then_inc(n3_in, 16)

            def pair(j):
                for s in range(2):
                    eng.wait_ge(gu_hi_done, 2 * j + s + 1)
                    eng.wait_ge(gu_lo_done, 2 * j + s + 1)
                    load_gu(j + 1, s)
                eng.wait_ge(dn_hi_done, j + 1)
                eng.wait_ge(dn_lo_done, j + 1)
                load_dn(j + 1)

            loop(eng, NP - 1, pair)
            for m in range(MT):
                n = P if m < NC else TS
                eng.wait_ge(y_done, m + 1)
                eng.dma_start(o["y"][m * P:m * P + n, :], y_out[m % 2][0:n, :]).then_inc(y_dma[m % 2], 16)
            eng.wait_ge(y_dma[0], 16 * (MT // 2 + 1))
            eng.wait_ge(y_dma[1], 16 * (MT // 2))

        @block.tensor
        def _(eng):
            def pair(j):
                for s in range(2):
                    eng.wait_ge(gu_hi_done, 2 * j + s + 1)
                    eng.wait_ge(gu_lo_done, 2 * j + s + 1)
                    for g, (a, m) in enumerate(GROUPS):
                        n = PAIR * j + NG * s + g
                        b = 2 * ((NG * s + g) % 2)
                        if not first(n):
                            eng.wait_ge(hf_done, n - 1)
                        for q in range(2):
                            for f in range(KT):
                                mm = mm3(eng, psum[b + q][:, 0:m], gu_hi[s][:, q, f, :], gu_lo[s][:, q, f, :],
                                         ht_hi[:, f, a:a + m], ht_lo[:, f, a:a + m], f == 0, f == KT - 1)
                            mm.then_inc(gu_mm, 1)
                eng.wait_ge(dn_hi_done, j + 1)
                eng.wait_ge(dn_lo_done, j + 1)
                for m in range(MT):
                    n = P if m < NC else TS
                    toks = slice(m * P, m * P + n)
                    if m == 0 or group_of(m) != group_of(m - 1):
                        eng.wait_ge(h_lo_done, PAIR * j + NG + group_of(m) + 1)
                    for half in range(2):
                        cols = slice(half * BANK, (half + 1) * BANK)
                        eng.wait_ge(acc_done, SUMS * j + (2 * (m - 2) + half + 1 if m >= 2 else 0))
                        for s in range(2):
                            mm = mm3(eng, psum[4 + 2 * (m % 2) + half][0:n, :], h_hi[:, s, toks], h_lo[:, s, toks],
                                     dn_hi[:, s, cols], dn_lo[:, s, cols], s == 0, s == 1)
                        mm.then_inc(dn_mm, 1)

            loop(eng, NP, pair)

        @block.scalar
        def _(eng):
            def split_gu(j, s):
                eng.wait_ge(gu_in[s], 32 * (j + 1))
                eng.wait_ge(gu_mm, 2 * PAIR * (j - 1) + 2 * NG * (s + 1))
                eng.activation(gu_hi[s][:, :, :, :], gu_raw[s][:, :, :, :], ACT.Copy).then_inc(gu_hi_done, 1)

            def split_dn(j):
                eng.wait_ge(dn_in, 16 * (j + 1))
                eng.wait_ge(dn_mm, SUMS * j)
                eng.activation(dn_hi[:, :, :], dn_raw[:, :, :], ACT.Copy).then_inc(dn_hi_done, 1)

            def pair(j, more):
                for s in range(2):
                    for g, (a, m) in enumerate(GROUPS):
                        n = PAIR * j + NG * s + g
                        b = (NG * s + g) % 2
                        eng.wait_ge(gu_mm, 2 * n + 1)
                        if not first(n):
                            eng.wait_ge(hf_done, n - 1)
                        eng.activation(sg[b][:, 0:m], psum[2 * b][:, 0:m], ACT.Silu).then_inc(sg_done, 1)
                        eng.wait_ge(hf_done, n + 1)
                        eng.activation(h_hi[:, s, a:a + m], hf[b][:, 0:m], ACT.Copy).then_inc(h_hi_done, 1)
                        if s == 0 and g == 0:
                            split_dn(j)
                    if more:
                        split_gu(j + 1, s)

            for s in range(2):
                eng.wait_ge(gu_in[s], 32)
                eng.activation(gu_hi[s][:, :, :, :], gu_raw[s][:, :, :, :], ACT.Copy).then_inc(gu_hi_done, 1)
            loop(eng, NP - 1, lambda j: pair(j, True))
            pair(NP - 1, False)
            for m in range(MT):
                n = P if m < NC else TS
                eng.wait_ge(acc_done, SUMS * (NP - 1) + 2 * m + 2)
                if m >= 2:
                    eng.wait_ge(y_dma[m % 2], 16 * (m // 2))
                eng.activation(y_out[m % 2][0:n, :], acc[0:n, m, :], ACT.Square, scale=D ** -0.5,
                               accum_out=fstat[0:n, m, 0:1]).then_inc(ssq, 1)

        @block.vector
        def _(eng):
            def split_gu(j, s):
                eng.wait_ge(gu_hi_done, 2 * j + s + 1)
                eng.tensor_tensor(gu_lo[s][:, :, :, :], gu_raw[s][:, :, :, :], f32(gu_hi[s][:, :, :, :]),
                                  ALU.subtract).then_inc(gu_lo_done, 1)

            def norm_tile(m):
                n = P if m < NC else TS
                eng.wait_ge(n3_in, 16)
                eng.wait_ge(root, 2 * m + 2)
                eng.scalar_tensor_tensor(out=y_out[m % 2][0:n, :], in0=acc[0:n, m, :], scalar=fstat[0:n, m, 1:2],
                                         in1=normw[0:n, :], op0=ALU.mult, op1=ALU.mult).then_inc(y_done, 1)

            def pair(j, more):
                for s in range(2):
                    for g, (a, m) in enumerate(GROUPS):
                        n = PAIR * j + NG * s + g
                        b = (NG * s + g) % 2
                        eng.wait_ge(gu_mm, 2 * n + 2)
                        eng.wait_ge(sg_done, n + 1)
                        if not first(n):
                            eng.wait_ge(h_lo_done, n - 1)
                        eng.tensor_tensor(hf[b][:, 0:m], sg[b][:, 0:m], psum[2 * b + 1][:, 0:m],
                                          ALU.mult).then_inc(hf_done, 1)
                        eng.wait_ge(h_hi_done, n + 1)
                        eng.tensor_tensor(h_lo[:, s, a:a + m], hf[b][:, 0:m], f32(h_hi[:, s, a:a + m]),
                                          ALU.subtract).then_inc(h_lo_done, 1)
                        if s == 0 and g == 0:
                            eng.wait_ge(dn_hi_done, j + 1)
                            eng.tensor_tensor(dn_lo[:, :, :], dn_raw[:, :, :], f32(dn_hi[:, :, :]),
                                              ALU.subtract).then_inc(dn_lo_done, 1)
                    if more:
                        split_gu(j + 1, s)
                for m in range(MT):
                    n = P if m < NC else TS
                    if not more and m >= 2:
                        norm_tile(m - 2)
                    for half in range(2):
                        part = acc[0:n, m, half * BANK:(half + 1) * BANK]
                        eng.wait_ge(dn_mm, SUMS * j + 2 * m + half + 1)
                        eng.tensor_tensor(part, part, psum[4 + 2 * (m % 2) + half][0:n, :], ALU.add).then_inc(acc_done, 1)

            for s in range(2):
                split_gu(0, s)
            eng.wait_ge(x1_in, 32)
            loop(eng, NP - 1, lambda j: pair(j, True))
            pair(NP - 1, False)
            norm_tile(MT - 2)
            norm_tile(MT - 1)

        @block.gpsimd
        def _(eng):
            for m in range(MT):
                n = P if m < NC else TS
                eng.wait_ge(ssq, m + 1)
                eng.tensor_tensor(fstat[0:n, m, 0:1], fstat[0:n, m, 0:1], eps_col[0:n, :], ALU.add).then_inc(root, 1)
                eng.wait_ge(root, 2 * m + 1)
                eng.tensor_tensor(fstat[0:n, m, 1:2], fstat[0:n, m, 0:1], minus_half[0:n, :], ALU.pow).then_inc(root, 1)



def lay_out(v):
    f = lambda n: np.asarray(v[n], np.float32)
    c = np.ascontiguousarray
    tiles = lambda w: w.reshape(w.shape[0], -1, P)
    win = f("w_in")[0]
    dr = R * P
    cols = []
    for t in range(R):
        cols += [np.arange(t * P, (t + 1) * P), np.arange(dr + t * P, dr + (t + 1) * P)]
    z0 = 2 * dr + QKV * P
    cols += [np.arange(z0 + t * P, z0 + (t + 1) * P) for t in range(H)]
    cols += [np.arange(2 * dr + t * P, 2 * dr + (t + 1) * P) for t in range(QKV)]
    w4 = win.reshape(KT, P, -1)
    i = {"x": np.concatenate([f("x_prompt")[0], f("x_sample").reshape(TS, D)])}
    i["w_in"] = c(np.stack([w4[:, :, cc].transpose(1, 0, 2) for cc in cols]))
    i["w_gates"] = c(w4[:, :, z0 + H * P:].transpose(1, 0, 2))
    i["w_out"] = f("w_out")[0].reshape(KT, P, D)
    for n, s in (("norm1", f("norm1")[0]), ("norm2", f("norm2")[0]), ("norm3", f("final_norm"))):
        i[n] = c(np.broadcast_to(s, (P, D)))
    feat = lambda a: c(a.reshape(a.shape[:-1] + (-1, P)))
    i["rg_par"] = c(np.stack([*feat(f("rg_conv_w")[0]), feat(f("rg_conv_b")[0]), feat(f("rg_ba")[0]),
                              feat(f("rg_bi")[0]), feat(f("rg_lambda")[0])]).transpose(2, 0, 1))
    i["rg_h0"] = c(feat(f("state_rglru_h")[0]).transpose(2, 1, 0))
    i["hist_rg"] = c(feat(f("state_rglru_conv")[0]).transpose(3, 2, 0, 1).reshape(P, R, NS * HIST))
    i["hist_g"] = c(feat(f("state_gdn_conv")[0]).transpose(3, 2, 0, 1).reshape(P, QKV, NS * HIST))
    i["conv_w"] = c(feat(f("gdn_conv_w")[0]).transpose(2, 1, 0))
    i["alog"] = c(np.broadcast_to(np.concatenate([f("gdn_A_log")[0], f("gdn_dt_bias")[0]]), (P, 2 * H)))
    rw = np.zeros((R, P, 2, P), np.float32)
    half = P // 2
    for q, n in enumerate(("rg_wa", "rg_wi")):
        for b in range(2 * R):
            s = b % 2 * half
            rw[b // 2, s:s + half, q, s:s + half] = f(n)[0][b]
    i["rg_w"] = rw
    i["gnw"] = c(f("gdn_norm_w")[0][:, None])
    i["state_S"] = c(f("state_gdn_S")[0].transpose(1, 2, 0, 3))
    i["w_gate"] = c(f("w_gate")[0].reshape(KT, P, FT, P).transpose(2, 1, 0, 3))
    i["w_up"] = c(f("w_up")[0].reshape(KT, P, FT, P).transpose(2, 1, 0, 3))
    i["w_down"] = f("w_down")[0].reshape(FT, P, D)
    i["expo"] = c(np.broadcast_to(np.array([-0.5] * 2 * H + [EPS] * H, np.float32), (P, 3 * H)))
    a, b = np.arange(P)[:, None], np.arange(P)[None, :]
    masks = [a == b, a <= b, a > b, a < b, a >= 0 * b]
    masks += [(a // (2 * n) == b // (2 * n)) & (a // n % 2 == 1) & (b // n % 2 == 0) for n in LEVELS]
    i["cst"] = c(np.stack([np.broadcast_to(m, (P, P)) for m in masks], 1).astype(np.float32))
    same = (a // LS == b // LS)[:TS, :TS]
    sm = [m[:TS, :TS] & same for m in masks[1:4]] + [(a // LS == b)[:TS, :NS]]
    i["cs"] = c(np.concatenate(sm, 1).astype(np.float32))
    return i


_OUTS = {"y": (T, D), "st_rg": (P, R, (1 + NS) * HIST), "st_h": (P, R, 1 + NS), "st_g": (P, QKV, (1 + NS) * HIST),
         "S_prompt": (P, H, P), "S_sample": (H, P, NS, P)}
_SCRATCH = {"rg": (R, P, SEQ), "z": (H, P, SEQ), "qkv": (QKV, P, SEQ), "x1": (T, D)}


def kernel(**inputs):
    import concourse.bacc as bacc
    from concourse.bass_utils import run_bass_kernel_spmd

    nc = bacc.Bacc("TRN2", target_bir_lowering=False, num_devices=1)
    arrays = {f"in_{n}": a for n, a in lay_out(inputs).items()}
    i = {n[3:]: nc.dram_tensor(n, a.shape, F32, kind="ExternalInput").ap() for n, a in arrays.items()}
    o = {n: nc.dram_tensor(f"out_{n}", s, F32, kind="ExternalOutput").ap() for n, s in _OUTS.items()}
    scratch = {n: nc.dram_tensor(f"scratch_{n}", s, F32, kind="Internal").ap() for n, s in _SCRATCH.items()}
    build(nc, i, o, scratch)
    r = run_bass_kernel_spmd(nc, [arrays], core_ids=[0]).results[0]
    y, rg, h, gd, sp, ss = (r[f"out_{n}"] for n in _OUTS)
    c = np.ascontiguousarray

    def rows(a):
        return c(a.reshape(P, -1, 1 + NS, HIST).transpose(2, 3, 1, 0).reshape(1, 1 + NS, HIST, -1))

    rc, gc = rows(rg), rows(gd)
    hh = c(h.transpose(2, 1, 0).reshape(1, 1 + NS, -1))
    return (c(y[:SEQ].reshape(1, SEQ, D)), c(y[SEQ:].reshape(NS, LS, D)),
            c(rc[:, :1]), c(hh[:, :1]), c(gc[:, :1]), c(sp.transpose(1, 0, 2)[None, None]),
            c(rc[:, 1:]), c(hh[:, 1:]), c(gc[:, 1:]), c(ss.transpose(2, 0, 1, 3)[None]))
```

```python
import numpy as np
import concourse.bass as bass
from concourse import mybir

F32 = mybir.dt.float32
F32R = mybir.dt.float32r
ACT = mybir.ActivationFunctionType
ALU = mybir.AluOpType
AX = mybir.AxisListType.X

P = 128
D = 1024
KT = D // P
SEQ = 1024
NS, LS = 8, 8
TS = NS * LS
T = SEQ + TS
NC = SEQ // P
MT = NC + 1
R = 4
H = 4
QKV = 3 * H
FF = 2816
FT = FF // P
EPS = 1e-6
GROUPS = [(0, 364), (364, 364), (728, 360)]
HIST = 3
SROW = HIST + LS
W = HIST + SEQ + NS * SROW
WC = W - HIST
S0 = SEQ + HIST
GATE_GROUPS = [(0, 372), (372, 370), (742, 370)]
LEVELS = [1, 2, 4, 8, 16, 32, 64]
SAMPLE_LEVELS = 3
BANK = 512


class Plan:

    def __init__(self, nc, at):
        self.nc, self.at = nc, at

    def __call__(self, name, shape, dt=F32):
        n = 4 * int(np.prod(shape[1:]))
        t = self.nc.alloc_sbuf_tensor_at(name, shape, dt, offset=self.at)
        self.at += (n + 31) // 32 * 32
        assert self.at <= self.nc.sbuf_usable_end, (name, self.at)
        return t


def f32(ap):
    return ap.bitcast(F32)


def sample_rows(row):
    return row[:, S0:W].rearrange("p (b r) -> p b r", r=SROW)


def loop(eng, n, body):
    body(0)
    with eng.Fori(1, n) as j:
        body(j)


def chunk_of(rows, c):
    return rows.rearrange("t p (c n) -> c p t n", n=P)[bass.ds(c, 1)].squeeze(0)


def mm3(pe, out, w_hi, w_lo, x_hi, x_lo, start, stop):
    pe.matmul(out, w_hi, x_hi, start=start, stop=False)
    pe.matmul(out, w_hi, x_lo, start=False, stop=False)
    return pe.matmul(out, w_lo, x_hi, start=False, stop=stop)


def build(nc, i, o, scratch):
    A = Plan(nc, (nc.sbuf_base + 31) // 32 * 32)
    psum = [nc.alloc_psum_tensor(f"bank{b}", [P, BANK], F32) for b in range(8)]
    expo = A("expo", [P, 3 * H])
    minus_half, eps_col = expo[:, 0:1], expo[:, 2 * H:2 * H + 1]
    stat = A("stat", [P, 2])
    normw = A("normw", [P, D])
    ht_hi = A("ht_hi", [P, KT, T], F32R)
    ht_lo = A("ht_lo", [P, KT, T], F32R)
    ffn_at = A.at
    cst = A("cst", [P, 12, P])
    ident, tle, ugt, strict, ones = (cst[:, n, :] for n in range(5))
    mlow = [cst[:, 5 + n, :] for n in range(len(LEVELS))]
    cs = A("cs", [TS, 3 * TS + NS])
    tle8, ugt8, strict8, blk = cs[:, 0:TS], cs[:, TS:2 * TS], cs[:, 2 * TS:3 * TS], cs[:, 3 * TS:]
    samp_qkv = A("samp_qkv", [P, QKV, TS])
    samp_z = A("samp_z", [P, H, TS])
    samp_rg = A("samp_rg", [P, R, TS])
    beta = A("beta", [P, MT, H])
    g = A("g", [P, MT, H])
    edec = A("edec", [P, 3, MT, H])
    esamp = A("esamp", [P, NS, H])
    gnw = A("gnw", [P, 1])
    base = A.at
    B = Plan(nc, base)
    wo_hi = B("wo_hi", [P, KT, D], F32R)
    wo_lo = B("wo_lo", [P, KT, D], F32R)
    after_wo = B.at

    q_ld, gu_first_in, gu_first_done, gu_mm = (
        nc.alloc_semaphore(n) for n in ("q_ld", "gu_first_in", "gu_first_done", "gu_mm"))
    qkv_in, qkv_at = input_block(nc, i, o, scratch, psum, Plan(nc, after_wo), locals())
    gu_first, rest = mixer_block(nc, i, o, scratch, psum, Plan(nc, after_wo), locals())
    ffn_block(nc, i, o, scratch, psum, Plan(nc, ffn_at), locals())

def input_block(nc, i, o, scratch, psum, B, k):
    cst, cs, ident, ht_hi, ht_lo, normw = (k[n] for n in ("cst", "cs", "ident", "ht_hi", "ht_lo", "normw"))
    wo_hi, wo_lo, samp_qkv, samp_z, samp_rg = (k[n] for n in ("wo_hi", "wo_lo", "samp_qkv", "samp_z", "samp_rg"))
    beta, g, edec, esamp, minus_half, eps_col, gnw = (
        k[n] for n in ("beta", "g", "edec", "esamp", "minus_half", "eps_col", "gnw"))
    tle, ugt, ones, tle8, ugt8, blk = (k[n] for n in ("tle", "ugt", "ones", "tle8", "ugt8", "blk"))
    w_raw = [B(f"w_raw{s}", [P, KT, P]) for s in range(2)]
    w_hi = [B(f"w_hi{s}", [P, KT, P], F32R) for s in range(2)]
    w_lo = [B(f"w_lo{s}", [P, KT, P], F32R) for s in range(2)]
    rg_par = B("rg_par", [P, 8, R])
    rg_calc = B("rg_calc", [P, 4, R])
    rg_now = B("rg_now", [P, 4])
    rg_h0 = B("rg_h0", [P, R, NS])
    hist_rg = B("hist_rg", [P, R, NS * HIST])
    hist_g = B("hist_g", [P, QKV, NS * HIST])
    st_rg = B("st_rg", [P, R, (1 + NS) * HIST])
    st_h = B("st_h", [P, R, 1 + NS])
    st_g = B("st_g", [P, QKV, (1 + NS) * HIST])
    conv_w = B("conv_w", [P, QKV, 4])
    alog = B("alog", [P, 2 * H])
    rg_w = B("rg_w", [P, 2, P])
    NSP = MT * H + R
    sp = B("sp", [P, 5, NSP])
    graw = B("graw", [P, MT, 2 * H])
    gblk = B("gblk", [TS, NS, H])
    in_stat = B("in_stat", [P, 2, 2])
    top = B.at
    B = Plan(nc, k["base"])
    xin = [B(f"xin{s}", [P, D]) for s in range(2)]
    xn = [B(f"xn{s}", [P, D]) for s in range(2)]
    gw_raw = B("gw_raw", [P, KT, 2 * H])
    gw_hi = B("gw_hi", [P, KT, 2 * H], F32R)
    gw_lo = B("gw_lo", [P, KT, 2 * H], F32R)
    gt = B("gt", [2 * H, T])
    B = Plan(nc, k["base"])
    rb_x, rb_xc, rb_gy, rb_r, rb_i, rb_t, rb_sq, rb_h = (
        B(f"rb_{n}", [P, W]) for n in ("x", "xc", "gy", "r", "i", "t", "sq", "h"))
    rb_tmp = B("rb_tmp", [P, NS])
    B = Plan(nc, top)
    cb_x = [B(f"cb_x{s}", [P, W]) for s in range(2)]
    cb_y = [B(f"cb_y{s}", [P, W]) for s in range(2)]
    wo_raw = [B(f"wo_raw{s}", [P, D]) for s in range(2)]
    qkv_in = Plan(nc, top)("qkv_in", [P, QKV, P])

    S = nc.alloc_semaphore
    const_in, more_in, x_in = S("const_in"), S("more_in"), [S(f"x_in{s}") for s in range(2)]
    ssq, root, xn_done = S("in_ssq"), S("in_root"), S("xn_done")
    xt_done, ht_hi_done, xt_free = S("xt_done"), S("ht_hi_done"), [S(f"xt_free{s}") for s in range(2)]
    gw_in, gw_hi_done, gw_lo_done = S("gw_in"), S("gw_hi_done"), S("gw_lo_done")
    gate_proj, gate_tok = S("gate_proj"), S("gate_tok")
    graw_done, sp_arg, exp_done = S("graw_done"), S("sp_arg"), S("exp_done")
    chain, g_done, decays = S("dve_chain"), S("g_done"), S("decays")
    w_in, w_hi_done, w_lo_done = [S(f"w_in{s}") for s in range(2)], S("w_hi_done"), S("w_lo_done")
    proj, evac_done = S("proj_done"), S("evac_done")
    rg_init, rg_hist, rg_state = S("rg_init"), S("rg_hist"), S("rg_state")
    rg_conv, rg_w_in, gate_mm, rg_tanh = S("rg_conv"), S("rg_w_in"), S("gate_mm"), S("rg_tanh")
    rg_t, rg_sq, rg_vec, rg_out = S("rg_t"), S("rg_sq"), S("rg_vec"), S("rg_out")
    z_out, wo_in = [S(f"z_out{s}") for s in range(2)], [S(f"wo_in{s}") for s in range(2)]
    wo_hi_done, wo_lo_done = S("wo_hi_done"), S("wo_lo_done")
    cb_init, cb_hist, cb_state = S("cb_init"), S("cb_hist"), S("cb_state")
    cb_conv, cb_silu, cb_out = S("cb_conv"), S("cb_silu"), [S(f"cb_out{s}") for s in range(2)]
    st_out, q_ld = S("st_out"), k["q_ld"]
    first_consts = ((k["expo"][:, :], i["expo"]), (normw[:, :], i["norm1"]), (ident, i["cst"][:, 0]))
    more_consts = ((cst[:, 1:, :], i["cst"][:, 1:]), (cs[:, :], i["cs"]), (rg_par[:, :, :], i["rg_par"]),
                   (rg_h0[:, :, :], i["rg_h0"]), (hist_rg[:, :, :], i["hist_rg"]), (hist_g[:, :, :], i["hist_g"]),
                   (conv_w[:, :, :], i["conv_w"]), (alog[:, :], i["alog"]), (gnw[:, :], i["gnw"]))
    NFIRST, NMORE = 16 * len(first_consts), 16 * len(more_consts)
    VEC = 11
    PAIRS = QKV // 2
    TQ, TZ = 2 * R, 2 * R + QKV

    def bank(s, n):
        return psum[3 * s + n]

    def sample_bank(s):
        a = GROUPS[-1][0]
        return bank(s, 2)[:, SEQ - a:T - a]

    def by_sample(ap):
        return ap.rearrange("p (b l) -> p b l", l=LS)

    with nc.Block() as block:

        @block.sync
        def _(eng):
            eng.dma_start(xin[0][:, :], i["x"][0:P, :]).then_inc(x_in[0], 16)
            for dst, src in first_consts:
                eng.dma_start(dst, src).then_inc(const_in, 16)
            eng.dma_start(xin[1][:, :], i["x"][P:2 * P, :]).then_inc(x_in[1], 16)
            eng.dma_start(gw_raw[:, :, :], i["w_gates"]).then_inc(gw_in, 16)
            for m in range(2, MT):
                eng.wait_ge(xn_done, m - 1)
                n = P if m < NC else TS
                eng.dma_start(xin[m % 2][0:n, :], i["x"][m * P:m * P + n, :]).then_inc(x_in[m % 2], 16)
                if m in (3, 5):
                    s = (m - 3) // 2
                    eng.dma_start(w_raw[s][:, :, :], i["w_in"][s]).then_inc(w_in[s], 16)
            for dst, src in more_consts:
                eng.dma_start(dst, src).then_inc(more_in, 16)

            def load_w(t, s):
                eng.wait_ge(w_hi_done, t + 1)
                eng.wait_ge(w_lo_done, t + 1)
                eng.dma_start(w_raw[s][:, :, :], i["w_in"][bass.ds(t + 2, 1)].squeeze(0)).then_inc(w_in[s], 16)

            def rg_tile(j):
                eng.wait_ge(gate_mm, 6 * j)
                eng.dma_start(rg_w[:, :, :], i["rg_w"][bass.ds(j, 1)].squeeze(0)).then_inc(rg_w_in, 16)
                load_w(2 * j, 0)
                load_w(2 * j + 1, 1)
                eng.wait_ge(rg_vec, VEC * (j + 1))
                eng.dma_start(scratch["rg"][bass.ds(j, 1)].squeeze(0), rb_gy[:, 0:SEQ]).then_inc(rg_out, 16)

            loop(eng, R, rg_tile)
            eng.wait_ge(rg_out, 16 * R)
            def qkv(j):
                for s in range(2):
                    load_w(TQ + 2 * j + s, s)
                for s in range(2):
                    eng.wait_ge(cb_silu, 2 * j + s + 1)
                    eng.dma_start(scratch["qkv"][bass.ds(2 * j + s, 1)].squeeze(0),
                                  cb_y[s][:, 0:SEQ]).then_inc(cb_out[s], 16)

            loop(eng, PAIRS, qkv)
            eng.wait_ge(rg_state, 2 * R)
            eng.wait_ge(rg_vec, VEC * R)
            eng.wait_ge(cb_state, 2 * QKV)
            for name, src in (("st_rg", st_rg), ("st_h", st_h), ("st_g", st_g)):
                eng.dma_start(o[name], src[:, :, :]).then_inc(st_out, 16)

            def z(j, prefetch):
                for s in range(2):
                    for n in range(2):
                        eng.wait_ge(wo_hi_done, 4 * j + 2 * s)
                        eng.wait_ge(wo_lo_done, 4 * j + 2 * s)
                        eng.dma_start(wo_raw[n][:, :],
                                      i["w_out"][bass.ds(4 * j + 2 * s + n, 1)].squeeze(0)).then_inc(wo_in[n], 16)
                    if prefetch:
                        load_w(TZ + 2 * j + s, s)
                for s in range(2):
                    eng.wait_ge(evac_done, TZ + 2 * j + s + 2)
                    eng.dma_start(scratch["z"][bass.ds(2 * j + s, 1)].squeeze(0),
                                  cb_y[s][:, 0:SEQ]).then_inc(z_out[s], 16)

            z(0, True)
            for s in range(2):
                eng.wait_ge(cb_out[s], 16 * PAIRS)
            eng.wait_ge(cb_conv, 4 * QKV)
            eng.dma_start(qkv_in[:, :, :], chunk_of(scratch["qkv"], 0)).then_inc(q_ld, 16)
            z(1, False)
            eng.wait_ge(st_out, 48)
            for s in range(2):
                eng.wait_ge(z_out[s], 16 * H // 2)

        @block.tensor
        def _(eng):
            eng.wait_ge(const_in, NFIRST)

            def transposes(s, n):
                for half in range(2):
                    for kk in range(4):
                        f = 4 * half + kk
                        mm = eng.transpose(bank(s, half)[:, kk * P:kk * P + n],
                                           xn[s][0:n, f * P:(f + 1) * P], ident[0:n, 0:n])
                    mm.then_inc(xt_done, 1)

            def gates(n):
                a, m = GROUPS[n]
                tiles = -(-(a + m) // P)
                eng.wait_ge(xt_free[0], (tiles + 1) // 2)
                eng.wait_ge(xt_free[1], tiles // 2)
                eng.wait_ge(gw_hi_done, 1)
                eng.wait_ge(gw_lo_done, 1)
                for f in range(KT):
                    mm = mm3(eng, psum[5 + n][0:2 * H, 0:m], gw_hi[:, f, :], gw_lo[:, f, :],
                             ht_hi[:, f, a:a + m], ht_lo[:, f, a:a + m], f == 0, f == KT - 1)
                mm.then_inc(gate_proj, 1)

            for m in range(MT):
                eng.wait_ge(xn_done, m + 1)
                eng.wait_ge(xt_free[m % 2], m // 2)
                transposes(m % 2, P if m < NC else TS)
                if m in (4, 7):
                    gates((m - 4) // 3)
            gates(2)
            for s in range(2):
                eng.wait_ge(xt_free[s], NC // 2 + 1 - s)

            def turn_gates():
                eng.wait_ge(evac_done, 1)
                for m in range(MT):
                    n = P if m < NC else TS
                    mm = eng.transpose(psum[6][0:n, m * 2 * H:(m + 1) * 2 * H], gt[:, m * P:m * P + n],
                                       ident[0:2 * H, 0:2 * H])
                mm.then_inc(gate_tok, 1)

            def project(t, s):
                eng.wait_ge(w_hi_done, t + 1)
                eng.wait_ge(w_lo_done, t + 1)
                eng.wait_ge(evac_done, t)
                for n, (a, m) in enumerate(GROUPS):
                    for f in range(KT):
                        mm = mm3(eng, bank(s, n)[:, 0:m], w_hi[s][:, f, :], w_lo[s][:, f, :],
                                 ht_hi[:, f, a:a + m], ht_lo[:, f, a:a + m], f == 0, f == KT - 1)
                    mm.then_inc(proj, 1)

            def rg_tile(j):
                project(2 * j, 0)
                if isinstance(j, int) and j == 0:
                    turn_gates()
                project(2 * j + 1, 1)
                if isinstance(j, int) and j == 0:
                    eng.wait_ge(graw_done, 1)
                eng.wait_ge(rg_conv, 4 * (j + 1))
                eng.wait_ge(rg_w_in, 16 * (j + 1))
                for n, (a, m) in enumerate(GATE_GROUPS):
                    for q in range(2):
                        eng.wait_ge(rg_tanh, 6 * j + max(0, 2 * n + q - 1))
                        eng.matmul(psum[6 + q][:, 0:m], rg_w[:, q, :], rb_xc[:, a:a + m],
                                   start=True, stop=True).then_inc(gate_mm, 1)

            loop(eng, R, rg_tile)
            eng.wait_ge(g_done, 2)
            eng.wait_ge(more_in, NMORE)
            eng.wait_ge(rg_tanh, 6 * R)
            gp = g[:, 0:NC, :].rearrange("p c h -> p (c h)")
            n, full = NC * H, MT * H
            for q, m in enumerate((tle, ugt, ones)):
                eng.matmul(psum[6][:, q * full:q * full + n], m, gp, start=True, stop=True)
            for q, m in enumerate((tle8, ugt8)):
                eng.matmul(psum[6][0:TS, q * full + n:(q + 1) * full], m, g[0:TS, NC, :], start=True, stop=True)
            eng.matmul(psum[7][:, 0:NS * H], ones[0:TS, :], gblk[:, :, :].rearrange("p b h -> p (b h)"),
                       start=True, stop=True).then_inc(decays, 1)
            def two_tiles(first):
                def tiles(j):
                    for s in range(2):
                        project(first + 2 * j + s, s)
                return tiles

            loop(eng, PAIRS, two_tiles(TQ))
            loop(eng, H // 2, two_tiles(TZ))

        @block.scalar
        def _(eng):
            def square(s, load, n):
                eng.wait_ge(x_in[s], 16 * load)
                eng.activation(xn[s][0:n, :], xin[s][0:n, :], ACT.Square, scale=D ** -0.5,
                               accum_out=in_stat[0:n, s, 0:1]).then_inc(ssq, 1)

            def high(m, s, n, toks):
                for half in range(2):
                    eng.wait_ge(xt_done, 2 * m + half + 1)
                    eng.activation(ht_hi[:, 4 * half:4 * half + 4, toks],
                                   bank(s, half)[:, :].rearrange("p (f t) -> p f t", t=P)[:, :, 0:n],
                                   ACT.Copy).then_inc(ht_hi_done, 1)

            def two_tiles(j, then):
                square(1, j + 1, P)
                high(2 * j, 0, P, bass.ds(2 * P * j, P))
                square(0, j + 2, then)
                high(2 * j + 1, 1, P, bass.ds(2 * P * j + P, P))

            square(0, 1, P)
            two_tiles(0, P)
            eng.wait_ge(gw_in, 16)
            eng.activation(gw_hi[:, :, :], gw_raw[:, :, :], ACT.Copy).then_inc(gw_hi_done, 1)
            with eng.Fori(1, NC // 2 - 1) as j:
                two_tiles(j, P)
            eng.wait_ge(w_in[0], 16)
            eng.activation(w_hi[0][:, :, :], w_raw[0][:, :, :], ACT.Copy).then_inc(w_hi_done, 1)
            two_tiles(NC // 2 - 1, TS)
            high(NC, 0, TS, slice(SEQ, T))
            eng.wait_ge(w_in[1], 16)
            eng.activation(w_hi[1][:, :, :], w_raw[1][:, :, :], ACT.Copy).then_inc(w_hi_done, 1)
            for n, (a, m) in enumerate(GROUPS):
                eng.wait_ge(gate_proj, n + 1)
                ins = eng.activation(gt[:, a:a + m], psum[5 + n][0:2 * H, 0:m], ACT.Copy)
            ins.then_inc(evac_done, 1)
            eng.wait_ge(sp_arg, 1)
            eng.wait_ge(more_in, NMORE)
            eng.activation(sp[:, 1, :], sp[:, 1, :], ACT.Exp, scale=-1.0)
            eng.activation(alog[:, 0:H], alog[:, 0:H], ACT.Exp).then_inc(exp_done, 1)
            eng.activation(beta[:, :, :], graw[:, :, 0:H], ACT.Sigmoid)

            def split_next(t, s, load):
                eng.wait_ge(w_in[s], 16 * load)
                eng.activation(w_hi[s][:, :, :], w_raw[s][:, :, :], ACT.Copy).then_inc(w_hi_done, 1)

            eng.wait_ge(rg_init, 1)
            eng.wait_ge(g_done, 2)
            def rg_tile(j):
                eng.wait_ge(rg_conv, 4 * j)
                eng.wait_ge(rg_state, 2 * j)
                for n, (a, m) in enumerate(GROUPS):
                    e = min(a + m, SEQ)
                    eng.wait_ge(proj, 6 * j + n + 1)
                    eng.activation(rb_x[:, HIST + a:HIST + e], bank(0, n)[:, 0:e - a], ACT.Copy)
                eng.activation(sample_rows(rb_x)[:, :, HIST:SROW], by_sample(sample_bank(0)),
                               ACT.Copy).then_inc(evac_done, 1)
                split_next(2 * j, 0, j + 2)
                eng.wait_ge(rg_out, 16 * j)
                eng.wait_ge(rg_vec, VEC * j)
                for n, (a, m) in enumerate(GROUPS):
                    e = min(a + m, SEQ)
                    eng.wait_ge(proj, 6 * j + n + 4)
                    eng.activation(rb_gy[:, a:e], bank(1, n)[:, 0:e - a], ACT.Gelu_apprx_tanh)
                eng.activation(sample_rows(rb_gy)[:, :, 0:LS], by_sample(sample_bank(1)),
                               ACT.Gelu_apprx_tanh).then_inc(evac_done, 1)
                split_next(2 * j + 1, 1, j + 2)
                for n, (a, m) in enumerate(GATE_GROUPS):
                    for q, row in enumerate((rb_r, rb_i)):
                        eng.wait_ge(gate_mm, 6 * j + 2 * n + q + 1)
                        eng.activation(row[:, a:a + m], psum[6 + q][:, 0:m], ACT.Tanh, scale=0.5,
                                       bias=rg_now[:, q:q + 1]).then_inc(rg_tanh, 1)
                eng.wait_ge(rg_tanh, 6 * j + 6)
                eng.activation(rb_t[:, 0:WC], rb_r[:, 0:WC], ACT.Tanh, scale=rg_now[:, 2:3],
                               bias=rg_now[:, 2:3]).then_inc(rg_t, 1)
                eng.wait_ge(rg_t, j + 1)
                eng.activation(rb_r[:, 0:WC], rb_r[:, 0:WC], ACT.Exp, scale=rg_now[:, 3:4], bias=rg_now[:, 3:4])
                eng.activation(rb_sq[:, 0:WC], rb_t[:, 0:WC], ACT.Sqrt, scale=0.25).then_inc(rg_sq, 1)

            loop(eng, R, rg_tile)
            eng.wait_ge(decays, 1)
            n, full = NC * H, MT * H
            eng.activation(edec[:, :, 0:NC, :].rearrange("p q c h -> p q (c h)"),
                           psum[6][:, 0:3 * full].rearrange("p (q n) -> p q n", n=full)[:, :, 0:n], ACT.Exp)
            eng.activation(edec[0:TS, 0:2, NC, :],
                           psum[6][0:TS, 0:2 * full].rearrange("p (q n) -> p q n", n=full)[:, :, n:], ACT.Exp)
            eng.activation(esamp[:, :, :].rearrange("p b h -> p (b h)"), psum[7][:, 0:NS * H], ACT.Exp)
            eng.wait_ge(rg_vec, VEC * R)
            eng.wait_ge(rg_state, 2 * R)
            eng.wait_ge(rg_out, 16 * R)
            def qkv(j):
                for s in range(2):
                    eng.wait_ge(cb_conv, 8 * j + 4 * s)
                    eng.wait_ge(cb_state, 4 * j + 2 * s)
                    for n, (a, m) in enumerate(GROUPS):
                        e = min(a + m, SEQ)
                        eng.wait_ge(proj, 3 * TQ + 6 * j + 3 * s + n + 1)
                        eng.activation(cb_x[s][:, HIST + a:HIST + e], bank(s, n)[:, 0:e - a], ACT.Copy)
                    eng.activation(sample_rows(cb_x[s])[:, :, HIST:SROW], by_sample(sample_bank(s)),
                                   ACT.Copy).then_inc(evac_done, 1)
                    split_next(TQ + 2 * j + s, s, TQ // 2 + j + 2)
                    eng.wait_ge(cb_conv, 8 * j + 4 * (s + 1))
                    eng.activation(by_sample(samp_qkv[:, bass.ds(2 * j + s, 1), :].squeeze(1)),
                                   sample_rows(cb_y[s])[:, :, 0:LS], ACT.Silu)
                    eng.activation(cb_y[s][:, 0:SEQ], cb_y[s][:, 0:SEQ], ACT.Silu).then_inc(cb_silu, 1)

            loop(eng, PAIRS, qkv)

            def z(j, prefetch):
                for s in range(2):
                    for n in range(2):
                        eng.wait_ge(wo_in[n], 16 * (2 * j + s + 1))
                        eng.activation(wo_hi[:, bass.ds(4 * j + 2 * s + n, 1), :].squeeze(1), wo_raw[n][:, :],
                                       ACT.Copy).then_inc(wo_hi_done, 1)
                    if j == 0:
                        eng.wait_ge(cb_out[s], 16 * PAIRS)
                    eng.wait_ge(z_out[s], 16 * j)
                    for n, (a, m) in enumerate(GROUPS):
                        e = min(a + m, SEQ)
                        eng.wait_ge(proj, 3 * TZ + 6 * j + 3 * s + n + 1)
                        eng.activation(cb_y[s][:, a:e], bank(s, n)[:, 0:e - a], ACT.Silu)
                    eng.activation(samp_z[:, bass.ds(2 * j + s, 1), :].squeeze(1), sample_bank(s),
                                   ACT.Silu).then_inc(evac_done, 1)
                    if prefetch:
                        split_next(TZ + 2 * j + s, s, TZ // 2 + j + 2)

            z(0, True)
            z(1, False)

        @block.vector
        def _(eng):
            eng.wait_ge(const_in, NFIRST)

            def norm_tile(m, s, n):
                eng.wait_ge(root, 2 * m + 2)
                eng.scalar_tensor_tensor(out=xn[s][0:n, :], in0=xin[s][0:n, :], scalar=in_stat[0:n, s, 1:2],
                                         in1=normw[0:n, :], op0=ALU.mult, op1=ALU.mult).then_inc(xn_done, 1)

            def low(m, s, n, toks):
                for half in range(2):
                    eng.wait_ge(ht_hi_done, 2 * m + half + 1)
                    ins = eng.tensor_tensor(ht_lo[:, 4 * half:4 * half + 4, toks],
                                            bank(s, half)[:, :].rearrange("p (f t) -> p f t", t=P)[:, :, 0:n],
                                            f32(ht_hi[:, 4 * half:4 * half + 4, toks]), ALU.subtract)
                ins.then_inc(xt_free[s], 1)

            def two_tiles(j, then):
                norm_tile(2 * j + 1, 1, P)
                low(2 * j, 0, P, bass.ds(2 * P * j, P))
                norm_tile(2 * j + 2, 0, then)
                low(2 * j + 1, 1, P, bass.ds(2 * P * j + P, P))

            def split_w(t, s):
                eng.wait_ge(w_hi_done, t + 1)
                eng.tensor_tensor(w_lo[s][:, :, :], w_raw[s][:, :, :], f32(w_hi[s][:, :, :]),
                                  ALU.subtract).then_inc(w_lo_done, 1)

            norm_tile(0, 0, P)
            two_tiles(0, P)
            eng.wait_ge(gw_hi_done, 1)
            eng.tensor_tensor(gw_lo[:, :, :], gw_raw[:, :, :], f32(gw_hi[:, :, :]),
                              ALU.subtract).then_inc(gw_lo_done, 1)
            with eng.Fori(1, NC // 2 - 1) as j:
                two_tiles(j, P)
            split_w(0, 0)
            two_tiles(NC // 2 - 1, TS)
            low(NC, 0, TS, slice(SEQ, T))
            split_w(1, 1)
            count = [0]

            def step(ins):
                ins.then_inc(chain, 1)
                count[0] += 1
                eng.wait_ge(chain, count[0])

            step(eng.memset(graw[TS:P, NC, :], 0.0))
            eng.wait_ge(gate_tok, 1)
            eng.wait_ge(more_in, NMORE)
            eng.tensor_copy(graw[:, 0:NC, :].rearrange("p c h -> p (c h)"), psum[6][:, 0:NC * 2 * H])
            eng.tensor_copy(graw[0:TS, NC, :], psum[6][0:TS, NC * 2 * H:MT * 2 * H]).then_inc(graw_done, 1)
            eng.wait_ge(graw_done, 1)
            n = MT * H
            step(eng.tensor_tensor(sp[:, 0, 0:n].rearrange("p (c h) -> p c h", h=H), graw[:, :, H:2 * H],
                                   alog[:, H:2 * H].unsqueeze(1).to_broadcast([P, MT, H]), ALU.add))
            step(eng.tensor_scalar(sp[:, 0, n:], rg_par[:, 7, :], -1.0, None, ALU.mult))
            eng.scalar_tensor_tensor(out=sp[:, 1, :], in0=sp[:, 0, :], scalar=-1.0, in1=sp[:, 0, :],
                                     op0=ALU.mult, op1=ALU.max).then_inc(sp_arg, 1)
            eng.memset(rb_x[:, 0:HIST], 0.0)
            eng.memset(rb_gy[:, :], 0.0).then_inc(rg_init, 1)
            x, e, z, z2, acc = (sp[:, n, :] for n in range(5))
            eng.wait_ge(exp_done, 1)
            step(eng.tensor_scalar(z2, e, 2.0, None, ALU.add))
            step(eng.reciprocal(z2, z2))
            step(eng.tensor_tensor(z, e, z2, ALU.mult))
            step(eng.tensor_tensor(z2, z, z, ALU.mult))
            step(eng.tensor_scalar(acc, z2, 1 / 15, 1 / 13, ALU.mult, ALU.add))
            for c in (11, 9, 7, 5, 3, 1):
                step(eng.tensor_tensor(acc, acc, z2, ALU.mult))
                step(eng.tensor_scalar(acc, acc, 1 / c, None, ALU.add))
            step(eng.tensor_tensor(acc, acc, z, ALU.mult))
            step(eng.tensor_scalar(z, x, 0.0, None, ALU.max))
            step(eng.scalar_tensor_tensor(out=acc, in0=acc, scalar=2.0, in1=z, op0=ALU.mult, op1=ALU.add))
            n = MT * H
            eng.tensor_scalar(rg_calc[:, 0:2, :], rg_par[:, 5:7, :], 0.5, None, ALU.mult)
            eng.tensor_scalar(rg_calc[:, 2, :], acc[:, n:], 2.0, None, ALU.mult)
            eng.tensor_scalar(rg_calc[:, 3, :], acc[:, n:], -4.0, None, ALU.mult)
            eng.scalar_tensor_tensor(out=g[:, :, :], in0=acc[:, 0:n].rearrange("p (c h) -> p c h", h=H), scalar=-1.0,
                                     in1=alog[:, 0:H].unsqueeze(1).to_broadcast([P, MT, H]),
                                     op0=ALU.mult, op1=ALU.mult).then_inc(g_done, 1)
            eng.wait_ge(g_done, 1)
            eng.tensor_tensor(gblk[:, :, :], g[0:TS, NC, :].unsqueeze(1).to_broadcast([TS, NS, H]),
                              blk.unsqueeze(2).to_broadcast([TS, NS, H]), ALU.mult).then_inc(g_done, 1)

            def conv(dst, src, taps, bias, sem, done):
                if bias is None:
                    eng.tensor_scalar(dst, src[:, 0:WC], taps(0), None, ALU.mult).then_inc(sem, 1)
                else:
                    eng.tensor_scalar(dst, src[:, 0:WC], taps(0), bias, ALU.mult, ALU.add).then_inc(sem, 1)
                for q in range(1, 4):
                    eng.wait_ge(sem, done + q)
                    eng.scalar_tensor_tensor(out=dst, in0=src[:, q:q + WC], scalar=taps(q), in1=dst,
                                             op0=ALU.mult, op1=ALU.add).then_inc(sem, 1)

            def rg_tile(j):
                one = bass.ds(j, 1)
                eng.wait_ge(evac_done, 2 * j + 2)
                eng.wait_ge(rg_hist, j + 1)
                eng.wait_ge(rg_sq, j)
                eng.tensor_copy(rg_now[:, :], rg_calc[:, :, one].squeeze(2))
                conv(rb_xc[:, 0:WC], rb_x, lambda q: rg_par[:, q, one], rg_par[:, 4, one], rg_conv, 4 * j)
                split_w(2 * j + 2, 0)
                split_w(2 * j + 3, 1)
                n = [0]

                def vec(ins, last=False):
                    ins.then_inc(rg_vec, 1)
                    n[0] += 1
                    if not last:
                        eng.wait_ge(rg_vec, VEC * j + n[0])

                u, a_, q_ = rb_xc[:, 0:WC], rb_r[:, 0:WC], rb_i[:, 0:WC]
                eng.wait_ge(rg_sq, j + 1)
                vec(eng.scalar_tensor_tensor(out=q_, in0=q_, scalar=1.0, in1=u, op0=ALU.add, op1=ALU.mult))
                vec(eng.scalar_tensor_tensor(out=rb_sq[:, 0:WC], in0=a_, scalar=1.0, in1=rb_sq[:, 0:WC],
                                             op0=ALU.add, op1=ALU.mult))
                vec(eng.tensor_tensor(u, q_, rb_sq[:, 0:WC], ALU.mult))
                first = lambda row: sample_rows(row)[:, :, 0]
                vec(eng.tensor_tensor(rb_tmp[:, :], first(rb_r), rg_h0[:, one, :].squeeze(1), ALU.mult))
                vec(eng.tensor_tensor(first(rb_xc), first(rb_xc), rb_tmp[:, :], ALU.add))
                vec(eng.memset(first(rb_r), 0.0))
                vec(eng.tensor_tensor_scan(rb_h[:, 0:WC], a_, u, 0.0, ALU.mult, ALU.add))
                vec(eng.tensor_copy(st_h[:, one, 0:1].squeeze(1), rb_h[:, SEQ - 1:SEQ]), True)
                vec(eng.tensor_copy(st_h[:, one, 1:].squeeze(1), sample_rows(rb_h)[:, :, LS - 1]), True)
                vec(eng.tensor_tensor(by_sample(samp_rg[:, one, :].squeeze(1)), sample_rows(rb_gy)[:, :, 0:LS],
                                      sample_rows(rb_h)[:, :, 0:LS], ALU.mult), True)
                vec(eng.tensor_tensor(rb_gy[:, 0:SEQ], rb_gy[:, 0:SEQ], rb_h[:, 0:SEQ], ALU.mult), True)

            loop(eng, R, rg_tile)
            eng.wait_ge(rg_out, 16 * R)
            eng.wait_ge(rg_state, 2 * R)
            for s in range(2):
                eng.memset(cb_x[s][:, 0:HIST], 0.0).then_inc(cb_init, 1)
            def qkv(j):
                for s in range(2):
                    eng.wait_ge(evac_done, TQ + 2 * j + s + 2)
                    eng.wait_ge(cb_hist, 2 * j + s + 1)
                    eng.wait_ge(cb_out[s], 16 * j)
                    eng.wait_ge(cb_silu, 2 * j)
                    row = bass.ds(2 * j + s, 1)
                    conv(cb_y[s][:, 0:WC], cb_x[s], lambda q: conv_w[:, row, q], None, cb_conv, 8 * j + 4 * s)
                    split_w(TQ + 2 * j + s + 2, s)

            loop(eng, PAIRS, qkv)

            def z(j, prefetch):
                for s in range(2):
                    for n in range(2):
                        eng.wait_ge(wo_hi_done, 4 * j + 2 * s + n + 1)
                        eng.tensor_tensor(wo_lo[:, bass.ds(4 * j + 2 * s + n, 1), :].squeeze(1), wo_raw[n][:, :],
                                          f32(wo_hi[:, bass.ds(4 * j + 2 * s + n, 1), :].squeeze(1)),
                                          ALU.subtract).then_inc(wo_lo_done, 1)
                    if prefetch:
                        split_w(TZ + 2 * j + s + 2, s)

            z(0, True)
            z(1, False)

        @block.gpsimd
        def _(eng):
            eng.wait_ge(const_in, NFIRST)

            def norm_tile(m, s, n):
                ms, root_ms = in_stat[0:n, s, 0:1], in_stat[0:n, s, 1:2]
                eng.wait_ge(ssq, m + 1)
                eng.tensor_tensor(ms, ms, eps_col[0:n, :], ALU.add).then_inc(root, 1)
                eng.wait_ge(root, 2 * m + 1)
                eng.tensor_tensor(root_ms, ms, minus_half[0:n, :], ALU.pow).then_inc(root, 1)

            def two_tiles(j):
                for s in range(2):
                    norm_tile(2 * j + s, s, P)

            loop(eng, NC // 2, two_tiles)
            norm_tile(NC, 0, TS)
            eng.wait_ge(more_in, NMORE)

            def rows(buf, hist, state, t, ev, hist_done, state_done, free):
                for sem, v in free:
                    eng.wait_ge(sem, v)
                eng.tensor_copy(sample_rows(buf)[:, :, 0:HIST],
                                hist[:, bass.ds(t, 1), :].squeeze(1).rearrange("p (b r) -> p b r", r=HIST)
                                ).then_inc(hist_done, 1)
                eng.wait_ge(evac_done, ev)
                out = state[:, bass.ds(t, 1), :].squeeze(1)
                eng.tensor_copy(out[:, 0:HIST], buf[:, SEQ:SEQ + HIST]).then_inc(state_done, 1)
                eng.tensor_copy(out[:, HIST:].rearrange("p (b r) -> p b r", r=HIST),
                                sample_rows(buf)[:, :, LS:SROW]).then_inc(state_done, 1)

            eng.wait_ge(rg_init, 1)
            def rg_tile(j):
                rows(rb_x, hist_rg, st_rg, j, 2 * j + 2, rg_hist, rg_state, [(rg_conv, 4 * j)])

            loop(eng, R, rg_tile)
            eng.wait_ge(cb_init, 2)
            def two_rows(j):
                for s in range(2):
                    rows(cb_x[s], hist_g, st_g, 2 * j + s, TQ + 2 * j + s + 2, cb_hist, cb_state,
                         [(cb_conv, 8 * j)])

            loop(eng, PAIRS, two_rows)
    return qkv_in, top


def mixer_block(nc, i, o, scratch, psum, B, k):
    cst, ident, ht_hi, ht_lo, stat, normw = (k[n] for n in ("cst", "ident", "ht_hi", "ht_lo", "stat", "normw"))
    wo_hi, wo_lo, samp_qkv, samp_z, samp_rg = (k[n] for n in ("wo_hi", "wo_lo", "samp_qkv", "samp_z", "samp_rg"))
    beta, g, edec, esamp, expo, gnw = (k[n] for n in ("beta", "g", "edec", "esamp", "expo", "gnw"))
    minus_half, eps_col = k["minus_half"], k["eps_col"]
    tle, ugt, strict, ones, tle8, ugt8, strict8, blk, mlow = (
        k[n] for n in ("tle", "ugt", "strict", "ones", "tle8", "ugt8", "strict8", "blk", "mlow"))
    q_ld, gu_first_in, gu_first_done = k["q_ld"], k["gu_first_in"], k["gu_first_done"]
    four = lambda name: B(name, [P, H, P])
    x_in = B("x_in", [P, D])
    xn = B("xn2", [P, D])
    sq = xn[:, :].rearrange("p (t n) -> p t n", n=P)
    mix_hi, mix_lo = B("mix_hi", [P, KT, P], F32R), B("mix_lo", [P, KT, P], F32R)
    sums = B("sums", [P, 2 * H])
    rn = B("rn", [P, 2 * H])
    epsq = B("epsq", [P, H])
    fac = B("fac", [P, 3, H])
    o_, on, st = four("o"), four("on"), four("state")
    v_tok, kn, kg, ktail = four("v_tok"), four("kn"), four("kg"), four("ktail")
    assert B.at <= k["qkv_at"]
    at = k["qkv_at"]
    B = Plan(nc, at)
    s_states = [B(f"s_state{s}", [P, NS, P]) for s in range(3)]
    v_exp = xn[0:TS, :].rearrange("p (b d) -> p b d", d=P)
    gu_first_raw = Plan(nc, at + 4 * D)("gu_first_raw", [P, 2, KT, P])
    B = Plan(nc, at)
    qkv_in, B.at = k["qkv_in"], at + 4 * QKV * P
    q_in, rg_in, z_in = four("q_in"), four("rg_in"), four("z_in")
    gu_at = B.at
    kt, e_, u_, mq = four("kt"), four("decay"), four("u"), four("mq")
    pp, y_, x_ = four("pp"), four("inv_t"), four("inv")
    B = Plan(nc, gu_at)
    gu_first_hi, gu_first_lo = (B(f"gu_first_{n}", [P, 2, KT, P], F32R) for n in ("hi", "lo"))
    vnew, nw, gr = kn, kt, kg

    S = nc.alloc_semaphore
    names = ("init_done qo_ld z_ld rg_ld x_ld n2_ld sq_done k_tr v_tr ss_mm rn_raw rn_done kn_done v_done "
             "kt_tr kt_done gr_done d_mm e_done e2_done ml_done kg_done ktail_done kk_mm qk_mm u1_done mq_done u_done "
             "ut_tr pp_done y_tr y_done x_done p_mm y_mm x_mm w_mm nw_done v_mm o1_mm vnew_done o2_mm ds_mm s_done "
             "t1_done o_done osq_done so_done fac_done on_done on_tr mix_done mixhi_done mixlo_done "
             "rghi_done rglo_done wo_mm x1_done ssq2 root2 xn_done hx_tr hhi_done hlo_done x1_out "
             "ss_ld0 ss_ld1 ss_ld2 qs_mm spread_zero spread_done vh_mm samp_new dss_mm "
             "samp_state ss_out0 ss_out1 ss_out2 sp_out").split()
    m_ = {n: S(f"mx_{n}") for n in names}
    NL = len(LEVELS)

    class Tile:

        def __init__(self, c):
            self.c = c
            self.samples = isinstance(c, int) and c == NC
            self.n = TS if self.samples else P
            self.levels = SAMPLE_LEVELS if self.samples else NL
            if self.samples:
                self.qkv, self.z, self.rg = samp_qkv, samp_z, samp_rg
                self.tle, self.ugt, self.strict = tle8, ugt8, strict8
            else:
                self.qkv, self.z, self.rg = qkv_in, z_in, rg_in
                self.tle, self.ugt, self.strict = tle, ugt, strict
            self.tok = slice(SEQ, T) if self.samples else bass.ds(P * c, P)

            self.q_o = samp_qkv if self.samples else q_in

        def col(self, t):
            return t[0:self.n, bass.ds(self.c, 1), :].squeeze(1)

    def spread(ap, n, m=P):
        return ap.unsqueeze(2).to_broadcast([n, H, m])

    def over(ap, n):
        return ap.unsqueeze(1).to_broadcast([n, H, ap.shape[1]])

    def b4(q, n=P, m=P):
        return psum[q][0:n, :].rearrange("p (h m) -> p h m", m=P)[:, :, 0:m]

    def token_rows(a, t):
        return a[SEQ:T, :] if t.samples else a[0:SEQ, :].rearrange("(c p) d -> c p d", p=P)[bass.ds(t.c, 1)].squeeze(0)

    P_BANK, Y_BANK, X_BANK = (5, 2), (6, 3), (7, 4)

    w_spread, q_spread = (on, u_), (e_, kt)

    def flat(buf):
        return buf[:, :, :].rearrange("p h m -> p (h m)")

    def by_token(buf, b):
        return flat(buf)[:, b * TS:(b + 1) * TS]

    def mlow2(q, n):
        return over(mlow[q][0:n, 0:n], n)[:, 0:2]

    def pair_of(ap, n, r, m=P):
        return ap[0:n, 2 * r:2 * r + 2, 0:m]

    with nc.Block() as block:

        @block.sync
        def _(eng):
            eng.dma_start(normw[:, :], i["norm2"]).then_inc(m_["n2_ld"], 16)

            def load_qkv(c):
                eng.dma_start(qkv_in[:, :, :], chunk_of(scratch["qkv"], c)).then_inc(q_ld, 16)

            def chunk(c, more):
                eng.wait_ge(m_["o1_mm"], c)
                eng.dma_start(q_in[:, :, :], chunk_of(scratch["qkv"][0:H], c)).then_inc(m_["qo_ld"], 16)
                eng.wait_ge(m_["mix_done"], c)
                eng.dma_start(z_in[:, :, :], chunk_of(scratch["z"], c)).then_inc(m_["z_ld"], 16)
                eng.wait_ge(m_["rghi_done"], c)
                eng.wait_ge(m_["rglo_done"], c)
                eng.dma_start(rg_in[:, :, :], chunk_of(scratch["rg"], c)).then_inc(m_["rg_ld"], 16)
                if more:
                    eng.wait_ge(m_["qk_mm"], c + 1)
                    load_qkv(c + 1)

            def residual(c, stored):
                t = Tile(c)
                if stored:
                    store_x1(Tile(c - 1))
                eng.wait_ge(m_["x1_out"], 16 * c)
                eng.wait_ge(m_["xn_done"], c)
                eng.dma_start(x_in[0:t.n, :], token_rows(i["x"], t)).then_inc(m_["x_ld"], 16)

            def store_x1(t):
                eng.wait_ge(m_["x1_done"], 2 * (t.c + 1))
                eng.dma_start(token_rows(scratch["x1"], t), x_in[0:t.n, :]).then_inc(m_["x1_out"], 16)

            chunk(0, True)
            residual(0, False)
            with eng.Fori(1, NC - 1) as c:
                chunk(c, True)
                residual(c, True)
            chunk(NC - 1, False)
            residual(NC - 1, True)

            def load_states(h):
                eng.dma_start(s_states[h % 3][:, :, :], i["state_S"][h]).then_inc(m_[f"ss_ld{h % 3}"], 16)

            eng.wait_ge(m_["qk_mm"], NC)
            load_states(0)
            eng.wait_ge(m_["s_done"], NC)
            eng.dma_start(o["S_prompt"], st[:, :, :]).then_inc(m_["sp_out"], 16)
            eng.wait_ge(m_["o1_mm"], NC)
            load_states(1)
            eng.wait_ge(m_["mix_done"], NC)
            eng.wait_ge(m_["rghi_done"], NC)
            eng.wait_ge(m_["rglo_done"], NC)
            load_states(2)
            residual(NC, True)
            for h in range(H):
                if h == H - 1:
                    eng.wait_ge(m_["ss_out1"], 16)
                    eng.wait_ge(m_["ss_out2"], 16)
                    for q, name in enumerate(("w_gate", "w_up")):
                        eng.dma_start(gu_first_raw[:, q], i[name][0]).then_inc(gu_first_in, 16)
                eng.wait_ge(m_["samp_state"], 2 * h + 2)
                eng.dma_start(o["S_sample"][h], s_states[h % 3][:, :, :]).then_inc(m_[f"ss_out{h % 3}"], 16)
                if h + 3 < H:
                    eng.wait_ge(m_[f"ss_out{h % 3}"], 16 * (h // 3 + 1))
                    load_states(h + 3)
            store_x1(Tile(NC))
            eng.wait_ge(m_["ss_out0"], 32)
            eng.wait_ge(m_["sp_out"], 16)
            eng.wait_ge(m_["x1_out"], 16 * MT)

        @block.tensor
        def _(eng):

            def turn_o(t):
                eng.wait_ge(m_["on_done"], t.c + 1)
                for h in range(H):
                    mm = eng.transpose(psum[6][:, h * P:h * P + t.n], on[0:t.n, h, :], ident[0:t.n, 0:t.n])
                mm.then_inc(m_["on_tr"], 1)

            def project(t, steps):
                for half, f in steps:
                    if (half, f) == (0, 0):
                        eng.wait_ge(m_["hlo_done"], 2 * t.c)
                        eng.wait_ge(m_["rglo_done"], t.c + 1)
                    if (half, f) == (0, R):
                        eng.wait_ge(m_["mixlo_done"], t.c + 1)
                    cols = slice(half * BANK, (half + 1) * BANK)
                    mm = mm3(eng, psum[half][0:t.n, :], mix_hi[:, f, 0:t.n], mix_lo[:, f, 0:t.n],
                             wo_hi[:, f, cols], wo_lo[:, f, cols], f == 0, f == KT - 1)
                    if f == KT - 1:
                        mm.then_inc(m_["wo_mm"], 1)

            def turn_x(t, half):
                eng.wait_ge(m_["xn_done"], t.c + 1)
                for kk in range(4):
                    f = 4 * half + kk
                    mm = eng.transpose(psum[half][:, kk * P:kk * P + t.n], xn[0:t.n, f * P:(f + 1) * P],
                                       ident[0:t.n, 0:t.n])
                mm.then_inc(m_["hx_tr"], 1)

            rg_steps = [(half, f) for half in range(2) for f in range(R)]
            o_steps = [(half, f) for half in range(2) for f in range(R, KT)]

            def chunk(c, tail):
                t = Tile(c)
                n = t.n
                if not t.samples:
                    eng.wait_ge(q_ld, 16 * (c + 1))
                eng.wait_ge(m_["vnew_done"], c)
                eng.wait_ge(m_["t1_done"], c)
                for q, off, sem in ((2, H, "k_tr"), (3, 2 * H, "v_tr")):
                    for h in range(H):
                        mm = eng.transpose(psum[q][0:n, h * P:(h + 1) * P], t.qkv[:, off + h, 0:n], ident)
                    mm.then_inc(m_[sem], 1)
                eng.wait_ge(m_["sq_done"], c + 1)
                eng.wait_ge(m_["s_done"], c)
                for h in range(2 * H):
                    mm = eng.matmul(psum[7][0:n, h:h + 1], sq[:, h, 0:n], ones[:, 0:1], start=True, stop=True)
                mm.then_inc(m_["ss_mm"], 1)
                eng.wait_ge(m_["gr_done"], c + 1)
                eng.wait_ge(m_["o_done"], c)
                eng.matmul(b4(5, n, n), t.ugt, gr[0:n, :, 0:n], start=True, stop=True).then_inc(m_["d_mm"], 1)
                if tail:
                    project(tail, rg_steps[0:3])
                eng.wait_ge(m_["kn_done"], c + 1)
                eng.wait_ge(m_["nw_done"], c)
                for h in range(H):
                    mm = eng.transpose(psum[4][:, h * P:h * P + n], kn[0:n, h, :], ident[0:n, 0:n])
                mm.then_inc(m_["kt_tr"], 1)
                if tail:
                    project(tail, rg_steps[3:5])
                eng.wait_ge(m_["kt_done"], c + 1)
                for h in range(H):
                    mm = eng.matmul(psum[2][0:n, h * P:h * P + n], kt[:, h, 0:n], kt[:, h, 0:n], start=True, stop=True)
                mm.then_inc(m_["kk_mm"], 1)
                eng.wait_ge(m_["v_done"], c + 1)
                for h in range(H):
                    mm = eng.matmul(psum[3][0:n, h * P:h * P + n], kt[:, h, 0:n], t.qkv[:, h, 0:n],
                                    start=True, stop=True)
                mm.then_inc(m_["qk_mm"], 1)
                if tail:
                    turn_o(tail)
                eng.wait_ge(m_["u_done"], c + 1)
                for h in range(H):
                    mm = eng.transpose(psum[4][0:n, h * P:h * P + n], u_[0:n, h, 0:n], ident[0:n, 0:n])
                mm.then_inc(m_["ut_tr"], 1)
                if tail:
                    project(tail, rg_steps[5:])
                eng.wait_ge(m_["mix_done"], c)
                eng.wait_ge(m_["mq_done"], c + 1)
                for r in range(2):
                    eng.wait_ge(m_["pp_done"], 2 * NL * c + r + 1)
                    for h in (2 * r, 2 * r + 1):
                        mm = eng.transpose(psum[Y_BANK[r]][0:n, h * P:h * P + n], pp[0:n, h, 0:n], ident[0:n, 0:n])
                    mm.then_inc(m_["y_tr"], 1)
                per_slot = 2 if t.samples else 1
                for q in range(1, t.levels):
                    last = q == t.levels - 1
                    slots = [o_steps[(2 * (q - 1) + s) * per_slot:(2 * (q - 1) + s + 1) * per_slot] for s in range(2)]
                    for r in range(2):
                        eng.wait_ge(m_["x_done"], 2 * (NL - 1) * c + 2 * (q - 1) + r + 1)
                        for h in (2 * r, 2 * r + 1):
                            mm = eng.matmul(psum[P_BANK[r]][0:n, h * P:h * P + n], u_[0:n, h, 0:n], x_[0:n, h, 0:n],
                                            start=True, stop=True)
                        mm.then_inc(m_["p_mm"], 1)
                    if tail:
                        project(tail, slots[0])
                    for r in range(2):
                        eng.wait_ge(m_["y_done"], 2 * NL * c + 2 * (q - 1) + r + 1)
                        eng.wait_ge(m_["pp_done"], 2 * NL * c + 2 * q + r + 1)
                        for h in (2 * r, 2 * r + 1):
                            mm = eng.matmul(psum[Y_BANK[r]][0:n, h * P:h * P + n], pp[0:n, h, 0:n], y_[0:n, h, 0:n],
                                            start=True, stop=True)
                        mm.then_inc(m_["y_mm"], 1)
                        if not last:
                            for h in (2 * r, 2 * r + 1):
                                mm = eng.matmul(psum[X_BANK[r]][0:n, h * P:h * P + n], y_[0:n, h, 0:n],
                                                pp[0:n, h, 0:n], start=True, stop=True)
                            mm.then_inc(m_["x_mm"], 1)
                    if tail:
                        project(tail, slots[1])
                if tail and not t.samples:
                    turn_x(tail, 0)
                eng.wait_ge(m_["y_done"], 2 * NL * c + 2 * t.levels)
                eng.wait_ge(m_["kg_done"], c + 1)
                for h in range(H):
                    mm = eng.matmul(psum[4][:, h * P:h * P + n], kg[0:n, h, :], y_[0:n, h, 0:n], start=True, stop=True)
                mm.then_inc(m_["w_mm"], 1)
                if tail:
                    if t.samples:
                        turn_x(tail, 0)
                    turn_x(tail, 1)
                if t.samples:
                    samples_states(t)
                else:
                    eng.wait_ge(m_["nw_done"], c + 1)
                    eng.wait_ge(m_["s_done"], c)
                    eng.wait_ge(m_["init_done"], 1)
                    for h in range(H):
                        eng.matmul(psum[2][:, h * P:(h + 1) * P], y_[:, h, :], v_tok[:, h, :], start=True, stop=False)
                        mm = eng.matmul(psum[2][:, h * P:(h + 1) * P], nw[:, h, :], st[:, h, :],
                                        start=False, stop=True)
                    mm.then_inc(m_["v_mm"], 1)
                    eng.wait_ge(m_["mq_done"], c + 1)
                    eng.wait_ge(m_["qo_ld"], 16 * (c + 1))
                    for h in range(H):
                        mm = eng.matmul(psum[3][:, h * P:(h + 1) * P], q_in[:, h, :], st[:, h, :],
                                        start=True, stop=True)
                    mm.then_inc(m_["o1_mm"], 1)
                    eng.wait_ge(m_["vnew_done"], c + 1)
                    eng.wait_ge(m_["ktail_done"], c + 1)
                    for h in range(H):
                        mm = eng.matmul(psum[7][:, h * P:(h + 1) * P], ktail[:, h, :], vnew[:, h, :],
                                        start=True, stop=True)
                    mm.then_inc(m_["ds_mm"], 1)
                for h in range(H):
                    mm = eng.matmul(psum[5][0:n, h * P:(h + 1) * P], mq[0:n, h, 0:n], vnew[0:n, h, :],
                                    start=True, stop=True)
                mm.then_inc(m_["o2_mm"], 1)

            def samples_states(t):
                for h in range(H):
                    hs = slice(h * P, (h + 1) * P)
                    eng.wait_ge(m_[f"ss_ld{h % 3}"], 16 * (h // 3 + 1))
                    eng.wait_ge(m_["spread_done"], 2 * (h + 1))
                    eng.wait_ge(m_["samp_new"], 2 * h)
                    eng.matmul(psum[2][0:TS, hs], y_[0:TS, h, 0:TS], v_tok[0:TS, h, :], start=True, stop=False)
                    for b in range(NS):
                        mm = eng.matmul(psum[2][0:TS, hs], by_token(w_spread[h % 2], b), s_states[h % 3][:, b, :],
                                        start=False, stop=b == NS - 1)
                    mm.then_inc(m_["vh_mm"], 1)
                    eng.wait_ge(m_["mq_done"], NC + 1)
                    for b in range(NS):
                        mm = eng.matmul(psum[3][0:TS, hs], by_token(q_spread[h % 2], b), s_states[h % 3][:, b, :],
                                        start=b == 0, stop=b == NS - 1)
                    mm.then_inc(m_["qs_mm"], 1)
                    eng.wait_ge(m_["samp_new"], 2 * h + 2)
                    eng.wait_ge(m_["ktail_done"], NC + 1)
                    eng.wait_ge(m_["samp_state"], 2 * h)
                    for q in range(2):
                        mm = eng.matmul(psum[6 + q][:, :], ktail[0:TS, h, :],
                                        v_exp[:, 4 * q:4 * q + 4, :].rearrange("p b d -> p (b d)"),
                                        start=True, stop=True)
                    mm.then_inc(m_["dss_mm"], 1)
                eng.wait_ge(m_["samp_state"], 2 * H)

            chunk(0, None)
            with eng.Fori(1, NC) as c:
                chunk(c, Tile(c - 1))
            chunk(NC, Tile(NC - 1))
            end = Tile(NC)
            turn_o(end)
            project(end, rg_steps + o_steps)
            eng.wait_ge(gu_first_done, 2)
            eng.wait_ge(m_["o_done"], MT)
            eng.wait_ge(m_["hlo_done"], 2 * NC)
            m = GROUPS[0][1]
            for q in range(2):
                for f in range(KT):
                    mm = mm3(eng, psum[2 + q][:, 0:m], gu_first_hi[:, q, f, :], gu_first_lo[:, q, f, :],
                             ht_hi[:, f, 0:m], ht_lo[:, f, 0:m], f == 0, f == KT - 1)
                mm.then_inc(k["gu_mm"], 1)
            for half in range(2):
                turn_x(end, half)

        @block.scalar
        def _(eng):

            def square_o(t):
                eng.wait_ge(m_["o_done"], t.c + 1)
                eng.activation(on[0:t.n, :, :], o_[0:t.n, :, :], ACT.Square, scale=1.0 / P).then_inc(m_["osq_done"], 1)

            def mix(t):
                eng.wait_ge(m_["mix_done"], t.c + 1)
                eng.activation(mix_hi[:, R:KT, 0:t.n], o_[:, :, 0:t.n], ACT.Copy).then_inc(m_["mixhi_done"], 1)

            def square_x(t):
                eng.wait_ge(m_["x1_done"], 2 * (t.c + 1))
                eng.activation(xn[0:t.n, :], x_in[0:t.n, :], ACT.Square, scale=D ** -0.5,
                               accum_out=stat[0:t.n, 0:1]).then_inc(m_["ssq2"], 1)

            def split_x(t, half):
                eng.wait_ge(m_["hx_tr"], 2 * t.c + half + 1)
                eng.activation(ht_hi[:, 4 * half:4 * half + 4, t.tok], b4(half, P, t.n),
                               ACT.Copy).then_inc(m_["hhi_done"], 1)

            def chunk(c, tail):
                t = Tile(c)
                n = t.n
                if not t.samples:
                    eng.wait_ge(q_ld, 16 * (c + 1))
                eng.wait_ge(m_["v_mm"], c)
                eng.activation(sq[:, :, 0:n], t.qkv[:, 0:2 * H, 0:n], ACT.Square).then_inc(m_["sq_done"], 1)
                if tail:
                    square_o(tail)
                eng.wait_ge(m_["v_tr"], c + 1)
                eng.activation(v_tok[0:n, :, :], b4(3, n), ACT.Copy).then_inc(m_["v_done"], 1)
                eng.wait_ge(m_["d_mm"], c + 1)
                eng.activation(e_[0:n, :, 0:n], b4(5, n, n), ACT.Exp).then_inc(m_["e_done"], 1)
                eng.wait_ge(m_["kt_tr"], c + 1)
                eng.activation(kt[:, :, 0:n], b4(4, P, n), ACT.Copy).then_inc(m_["kt_done"], 1)
                if tail:
                    mix(tail)
                    square_x(tail)
                eng.wait_ge(m_["w_mm"], c + 1)
                if not t.samples:
                    eng.activation(nw[:, :, 0:n], b4(4, P, n), ACT.Copy, scale=-1.0).then_inc(m_["nw_done"], 1)
                else:
                    for h in range(2):
                        spread_samples(h)
                if not t.samples:
                    eng.wait_ge(m_["rg_ld"], 16 * (c + 1))
                eng.wait_ge(m_["wo_mm"], 2 * c)
                eng.activation(mix_hi[:, 0:R, 0:n], t.rg[:, :, 0:n], ACT.Copy).then_inc(m_["rghi_done"], 1)
                if tail:
                    for half in range(2):
                        split_x(tail, half)
                if t.samples:
                    for h in range(2, H):
                        spread_samples(h)

            def spread_samples(h):
                if h < 2:
                    eng.wait_ge(m_["spread_zero"], 4)
                else:
                    eng.wait_ge(m_["vh_mm"], h - 1)
                    eng.wait_ge(m_["qs_mm"], h - 1)
                for dst, src, scale in ((w_spread[h % 2], b4(4)[:, h, 0:TS], -1.0),
                                        (q_spread[h % 2], samp_qkv[:, h, :], 1.0)):
                    src = src.rearrange("p (b l) -> p b l", l=LS)
                    step = TS + LS
                    eng.activation(flat(dst)[:, 0:(NS - 1) * step].rearrange("p (b r) -> p b r", r=step)[:, :, 0:LS],
                                   src[:, 0:NS - 1, :], ACT.Copy, scale=scale)
                    eng.activation(flat(dst)[:, (NS - 1) * step:], src[:, NS - 1, :],
                                   ACT.Copy, scale=scale).then_inc(m_["spread_done"], 1)

            chunk(0, None)
            with eng.Fori(1, NC) as c:
                chunk(c, Tile(c - 1))
            chunk(NC, Tile(NC - 1))
            end = Tile(NC)
            square_o(end)
            eng.wait_ge(gu_first_in, 32)
            eng.wait_ge(m_["o2_mm"], MT)
            eng.activation(gu_first_hi[:, :, :, :], gu_first_raw[:, :, :, :], ACT.Copy).then_inc(gu_first_done, 1)
            mix(end)
            square_x(end)
            for half in range(2):
                split_x(end, half)

        @block.vector
        def _(eng):
            eng.tensor_scalar(fac[:, 2, 0:1], gnw[:, :], P ** -0.5, None, ALU.mult)
            eng.memset(st[:, :, :], 0.0).then_inc(m_["init_done"], 1)

            def sum_o(t):
                eng.wait_ge(m_["osq_done"], t.c + 1)
                eng.tensor_reduce(fac[0:t.n, 0, :], on[0:t.n, :, :], AX, ALU.add).then_inc(m_["so_done"], 1)

            def norm_o(t):
                eng.wait_ge(m_["fac_done"], 2 * t.c + 2)
                eng.tensor_tensor(on[0:t.n, :, :], o_[0:t.n, :, :], spread(fac[0:t.n, 1, :], t.n),
                                  ALU.mult).then_inc(m_["on_done"], 1)

            def mix(t):
                eng.wait_ge(m_["on_tr"], t.c + 1)
                if not t.samples:
                    eng.wait_ge(m_["z_ld"], 16 * (t.c + 1))
                eng.wait_ge(m_["init_done"], 1)
                eng.scalar_tensor_tensor(out=o_[:, :, 0:t.n], in0=b4(6, P, t.n), scalar=fac[:, 2, 0:1],
                                         in1=t.z[:, :, 0:t.n], op0=ALU.mult, op1=ALU.mult).then_inc(m_["mix_done"], 1)

            def mix_low(t):
                eng.wait_ge(m_["mixhi_done"], t.c + 1)
                eng.tensor_tensor(mix_lo[:, R:KT, 0:t.n], o_[:, :, 0:t.n], f32(mix_hi[:, R:KT, 0:t.n]),
                                  ALU.subtract).then_inc(m_["mixlo_done"], 1)

            def add_x(t, half):
                part = x_in[0:t.n, half * BANK:(half + 1) * BANK]
                eng.wait_ge(m_["x_ld"], 16 * (t.c + 1))
                eng.wait_ge(m_["wo_mm"], 2 * t.c + half + 1)
                eng.tensor_tensor(part, part, psum[half][0:t.n, :], ALU.add).then_inc(m_["x1_done"], 1)

            def norm_x(t):
                eng.wait_ge(m_["n2_ld"], 16)
                eng.wait_ge(m_["root2"], 2 * t.c + 2)
                eng.scalar_tensor_tensor(out=xn[0:t.n, :], in0=x_in[0:t.n, :], scalar=stat[0:t.n, 1:2],
                                         in1=normw[0:t.n, :], op0=ALU.mult, op1=ALU.mult).then_inc(m_["xn_done"], 1)

            def split_x(t, half):
                eng.wait_ge(m_["hhi_done"], 2 * t.c + half + 1)
                eng.tensor_tensor(ht_lo[:, 4 * half:4 * half + 4, t.tok], b4(half, P, t.n),
                                  f32(ht_hi[:, 4 * half:4 * half + 4, t.tok]),
                                  ALU.subtract).then_inc(m_["hlo_done"], 1)

            def chunk(c, tail):
                t = Tile(c)
                n = t.n
                eng.wait_ge(m_["ss_mm"], c + 1)
                eng.wait_ge(m_["kg_done"], c)
                eng.tensor_scalar(sums[0:n, :], psum[7][0:n, 0:2 * H], EPS, None, ALU.add).then_inc(m_["rn_raw"], 1)
                eng.wait_ge(m_["k_tr"], c + 1)
                eng.wait_ge(m_["rn_done"], c + 1)
                eng.tensor_tensor(kn[0:n, :, :], b4(2, n), spread(rn[0:n, H:], n),
                                  ALU.mult).then_inc(m_["kn_done"], 1)
                if tail:
                    sum_o(tail)
                    norm_o(tail)
                eng.wait_ge(m_["kk_mm"], c + 1)
                eng.wait_ge(m_["e2_done"], c + 1)
                eng.tensor_tensor(u_[0:n, :, 0:n], b4(2, n, n), e_[0:n, :, 0:n], ALU.mult).then_inc(m_["u1_done"], 1)
                eng.wait_ge(m_["u1_done"], c + 1)
                eng.wait_ge(m_["ml_done"], c + 1)
                eng.tensor_tensor(u_[0:n, :, 0:n], u_[0:n, :, 0:n], x_[0:n, :, 0:n], ALU.mult).then_inc(m_["u_done"], 1)
                eng.wait_ge(m_["qk_mm"], c + 1)
                eng.tensor_tensor(mq[0:n, :, 0:n], b4(3, n, n), e_[0:n, :, 0:n], ALU.mult).then_inc(m_["mq_done"], 1)
                eng.wait_ge(m_["ut_tr"], c + 1)
                eye = over(ident[0:n, 0:n], n)
                for r in range(2):
                    eng.tensor_tensor(pair_of(pp, n, r, n), pair_of(b4(4), n, r, n), mlow2(0, n),
                                      ALU.mult).then_inc(m_["pp_done"], 1)
                if tail:
                    mix(tail)
                for r in range(2):
                    eng.wait_ge(m_["pp_done"], 2 * NL * c + r + 1)
                    eng.tensor_tensor(pair_of(x_, n, r, n), eye[:, 0:2], pair_of(pp, n, r, n),
                                      ALU.subtract).then_inc(m_["x_done"], 1)
                for r in range(2):
                    eng.wait_ge(m_["y_tr"], 2 * c + r + 1)
                    eng.tensor_tensor(pair_of(y_, n, r, n), eye[:, 0:2], pair_of(b4(Y_BANK[r]), n, r, n),
                                      ALU.subtract).then_inc(m_["y_done"], 1)
                if tail:
                    mix_low(tail)
                for q in range(1, t.levels):
                    last = q == t.levels - 1
                    for r in range(2):
                        eng.wait_ge(m_["p_mm"], 2 * (NL - 1) * c + 2 * (q - 1) + r + 1)
                        eng.tensor_tensor(pair_of(pp, n, r, n), pair_of(b4(P_BANK[r]), n, r, n), mlow2(q, n),
                                          ALU.mult).then_inc(m_["pp_done"], 1)
                    if tail and not t.samples:
                        if q in (3, 5):
                            add_x(tail, (q - 3) // 2)
                        if q == 6:
                            norm_x(tail)
                    if tail and t.samples and q == 2:
                        add_x(tail, 0)
                    for r in range(2):
                        eng.wait_ge(m_["y_mm"], 2 * (NL - 1) * c + 2 * (q - 1) + r + 1)
                        if not last:
                            eng.wait_ge(m_["x_mm"], 2 * (NL - 2) * c + 2 * (q - 1) + r + 1)
                        eng.tensor_tensor(pair_of(y_, n, r, n), pair_of(y_, n, r, n), pair_of(b4(Y_BANK[r]), n, r, n),
                                          ALU.subtract).then_inc(m_["y_done"], 1)
                        if not last:
                            eng.tensor_tensor(pair_of(x_, n, r, n), pair_of(x_, n, r, n),
                                              pair_of(b4(X_BANK[r]), n, r, n), ALU.subtract).then_inc(m_["x_done"], 1)
                if tail and t.samples:
                    add_x(tail, 1)
                    norm_x(tail)
                if t.samples:
                    for half in range(2):
                        split_x(tail, half)
                    samples_states(n)
                else:
                    eng.wait_ge(m_["v_mm"], c + 1)
                    eng.wait_ge(m_["kg_done"], c + 1)
                    eng.wait_ge(m_["ktail_done"], c + 1)
                    eng.tensor_tensor(vnew[:, :, :], b4(2), spread(t.col(beta), n),
                                      ALU.mult).then_inc(m_["vnew_done"], 1)
                    eng.wait_ge(m_["o1_mm"], c + 1)
                if tail:
                    eng.wait_ge(m_["mixlo_done"], c)
                eng.tensor_tensor(o_[0:n, :, :], b4(3, n), spread(edec[0:n, 0, bass.ds(c, 1), :].squeeze(1), n),
                                  ALU.mult).then_inc(m_["t1_done"], 1)
                if tail and not t.samples:
                    split_x(tail, 0)
                if not t.samples:
                    eng.wait_ge(m_["ds_mm"], c + 1)
                    for h in range(H):
                        ins = eng.scalar_tensor_tensor(out=st[:, h, :], in0=st[:, h, :],
                                                       scalar=edec[:, 2, bass.ds(c, 1), h], in1=b4(7)[:, h, :],
                                                       op0=ALU.mult, op1=ALU.add)
                    ins.then_inc(m_["s_done"], 1)
                eng.wait_ge(m_["o2_mm"], c + 1)
                eng.wait_ge(m_["t1_done"], c + 1)
                eng.tensor_tensor(o_[0:n, :, :], o_[0:n, :, :], b4(5, n), ALU.add).then_inc(m_["o_done"], 1)
                if tail and not t.samples:
                    split_x(tail, 1)

            def samples_states(n):
                for h in range(H):
                    state = s_states[h % 3]
                    eng.wait_ge(m_["kg_done"], NC + 1)
                    eng.wait_ge(m_["ktail_done"], NC + 1)
                    eng.wait_ge(m_["vh_mm"], h + 1)
                    eng.tensor_scalar(vnew[0:n, h, :], psum[2][0:n, h * P:(h + 1) * P],
                                      beta[0:n, NC, h:h + 1], None, ALU.mult).then_inc(m_["samp_new"], 1)
                    eng.wait_ge(m_["samp_new"], 2 * h + 1)
                    eng.wait_ge(m_["hx_tr"], 2 * NC)
                    eng.tensor_tensor(v_exp[:, :, :], vnew[0:n, h, :].unsqueeze(1).to_broadcast([n, NS, P]),
                                      blk.unsqueeze(2).to_broadcast([n, NS, P]),
                                      ALU.mult).then_inc(m_["samp_new"], 1)
                    eng.wait_ge(m_["vh_mm"], h + 1)
                    eng.wait_ge(m_["qs_mm"], h + 1)
                    eng.tensor_tensor(state[:, :, :], state[:, :, :],
                                      esamp[:, :, h:h + 1].to_broadcast([P, NS, P]),
                                      ALU.mult).then_inc(m_["samp_state"], 1)
                    eng.wait_ge(m_["samp_state"], 2 * h + 1)
                    eng.wait_ge(m_["dss_mm"], h + 1)
                    for q in range(2):
                        part = state[:, 4 * q:4 * q + 4, :]
                        ins = eng.tensor_tensor(part, part, b4(6 + q), ALU.add)
                    ins.then_inc(m_["samp_state"], 1)

            chunk(0, None)
            with eng.Fori(1, NC) as c:
                chunk(c, Tile(c - 1))
            chunk(NC, Tile(NC - 1))
            end = Tile(NC)
            sum_o(end)
            norm_o(end)
            mix(end)
            mix_low(end)
            eng.wait_ge(gu_first_done, 1)
            eng.tensor_tensor(gu_first_lo[:, :, :, :], gu_first_raw[:, :, :, :], f32(gu_first_hi[:, :, :, :]),
                              ALU.subtract).then_inc(gu_first_done, 1)
            for half in range(2):
                add_x(end, half)
            norm_x(end)
            for half in range(2):
                split_x(end, half)

        @block.gpsimd
        def _(eng):

            def scale_o(t):
                so, f = fac[0:t.n, 0, :], fac[0:t.n, 1, :]
                eng.wait_ge(m_["so_done"], t.c + 1)
                eng.tensor_tensor(so, so, epsq[0:t.n, :], ALU.add).then_inc(m_["fac_done"], 1)
                eng.wait_ge(m_["on_done"], t.c)
                eng.wait_ge(m_["fac_done"], 2 * t.c + 1)
                eng.tensor_tensor(f, so, expo[0:t.n, 0:H], ALU.pow).then_inc(m_["fac_done"], 1)

            def root_x(t):
                eng.wait_ge(m_["ssq2"], t.c + 1)
                eng.tensor_tensor(stat[0:t.n, 0:1], stat[0:t.n, 0:1], eps_col[0:t.n, :],
                                  ALU.add).then_inc(m_["root2"], 1)
                eng.wait_ge(m_["root2"], 2 * t.c + 1)
                eng.tensor_tensor(stat[0:t.n, 1:2], stat[0:t.n, 0:1], minus_half[0:t.n, :],
                                  ALU.pow).then_inc(m_["root2"], 1)

            def chunk(c, tail):
                t = Tile(c)
                n = t.n
                eng.wait_ge(m_["w_mm"], c)
                eng.tensor_tensor(gr[0:n, :, 0:n], over(t.tle, n), spread(t.col(g), n, n),
                                  ALU.mult).then_inc(m_["gr_done"], 1)
                eng.wait_ge(m_["rn_raw"], c + 1)
                eng.tensor_tensor(rn[0:n, :], sums[0:n, :], expo[0:n, 0:2 * H], ALU.pow).then_inc(m_["rn_done"], 1)
                eng.wait_ge(m_["w_mm"], c)
                eng.tensor_tensor(x_[0:n, :, 0:n], over(t.strict, n), spread(t.col(beta), n, n),
                                  ALU.mult).then_inc(m_["ml_done"], 1)
                eng.wait_ge(m_["e_done"], c + 1)
                eng.tensor_tensor(e_[0:n, :, 0:n], e_[0:n, :, 0:n], over(t.tle, n), ALU.mult).then_inc(m_["e2_done"], 1)
                if tail:
                    scale_o(tail)
                eng.wait_ge(m_["rn_raw"], c + 1)
                eng.tensor_tensor(epsq[0:n, :], sums[0:n, 0:H], expo[0:n, 2 * H:], ALU.mult)
                eng.wait_ge(m_["kn_done"], c + 1)
                eng.tensor_tensor(kg[0:n, :, :], kn[0:n, :, :], spread(edec[0:n, 0, bass.ds(c, 1), :].squeeze(1), n),
                                  ALU.mult).then_inc(m_["kg_done"], 1)
                eng.tensor_tensor(ktail[0:n, :, :], kn[0:n, :, :], spread(edec[0:n, 1, bass.ds(c, 1), :].squeeze(1), n),
                                  ALU.mult).then_inc(m_["ktail_done"], 1)
                if t.samples:
                    zero_spreads()
                if tail:
                    root_x(tail)
                eng.wait_ge(m_["rghi_done"], c + 1)
                eng.tensor_tensor(mix_lo[:, 0:R, 0:n], t.rg[:, :, 0:n], f32(mix_hi[:, 0:R, 0:n]),
                                  ALU.subtract).then_inc(m_["rglo_done"], 1)

            def zero_spreads():
                for buf, sem, v in ((e_, "mq_done", NC + 1), (kt, "qk_mm", NC + 1), (on, "on_tr", NC),
                                    (u_, "w_mm", NC + 1)):
                    eng.wait_ge(m_[sem], v)
                    eng.memset(flat(buf), 0.0).then_inc(m_["spread_zero"], 1)

            chunk(0, None)
            with eng.Fori(1, NC) as c:
                chunk(c, Tile(c - 1))
            chunk(NC, Tile(NC - 1))
            scale_o(Tile(NC))
            root_x(Tile(NC))
    return (gu_first_raw, gu_first_hi, gu_first_lo), (k["after_wo"], at)



def ffn_block(nc, i, o, scratch, psum, B, k):
    ht_hi, ht_lo, normw, minus_half, eps_col = (k[n] for n in ("ht_hi", "ht_lo", "normw", "minus_half", "eps_col"))
    acc = B("acc", [P, MT, D])
    h_hi = B("h_hi", [P, 2, T], F32R)
    h_lo = B("h_lo", [P, 2, T], F32R)
    dn_hi = B("dn_hi", [P, 2, D], F32R)
    dn_lo = B("dn_lo", [P, 2, D], F32R)
    most = max(m for _, m in GROUPS)
    sg = [B(f"sg{s}", [P, most]) for s in range(2)]
    hf = [B(f"hf{s}", [P, most]) for s in range(2)]
    fstat = B("fstat", [P, MT, 2])
    first_raw, first_hi, first_lo = k["gu_first"]
    after_wo, raw_at = k["rest"]
    B = Plan(nc, max(B.at, after_wo))
    gu_raw = [first_raw, B("gu_raw1", [P, 2, KT, P])]
    gu_hi = [first_hi, B("gu_hi1", [P, 2, KT, P], F32R)]
    gu_lo = [first_lo, B("gu_lo1", [P, 2, KT, P], F32R)]
    dn_raw = [B("dn_raw0", [P, D]), Plan(nc, raw_at)("dn_raw1", [P, D])]
    assert B.at <= raw_at
    B = Plan(nc, raw_at + 4 * D)
    y_out = [B(f"y_out{s}", [P, D]) for s in range(2)]

    S = nc.alloc_semaphore
    x1_in, n3_in = S("ff_x1_in"), S("ff_n3_in")
    gu_in, dn_in = [S(f"gu_in{s}") for s in range(2)], S("dn_in")
    gu_hi_done, gu_lo_done, dn_hi_done, dn_lo_done = S("gu_hi_done"), S("gu_lo_done"), S("dn_hi_done"), S("dn_lo_done")
    gu_mm = k["gu_mm"]
    sg_done, hf_done, h_hi_done, h_lo_done = S("sg_done"), S("hf_done"), S("h_hi_done"), S("h_lo_done")
    dn_mm, acc_done = S("dn_mm"), S("acc_done")
    ssq, root, y_done, y_dma = S("ff_ssq"), S("ff_root"), S("ff_y_done"), [S(f"y_dma{s}") for s in range(2)]
    NG = len(GROUPS)
    PAIR = 2 * NG
    SUMS = 2 * MT
    NP = FT // 2

    def group_of(m):
        last = min((m + 1) * P, T) - 1
        return next(n for n, (a, ln) in enumerate(GROUPS) if last < a + ln)

    def first(n):
        return isinstance(n, int) and n < 2

    with nc.Block() as block:

        @block.sync
        def _(eng):
            def load_gu(j, s):
                t = 2 * j + s
                for q, name in enumerate(("w_gate", "w_up")):
                    eng.dma_start(gu_raw[s][:, q], i[name][bass.ds(t, 1)].squeeze(0)).then_inc(gu_in[s], 16)

            def load_dn(j):
                for s in range(2):
                    eng.dma_start(dn_raw[s][:, :], i["w_down"][bass.ds(2 * j + s, 1)].squeeze(0)).then_inc(dn_in, 16)

            load_gu(0, 1)
            load_dn(0)
            eng.dma_start(acc[:, 0:NC, :],
                          scratch["x1"][0:SEQ, :].rearrange("(c p) d -> p c d", p=P)).then_inc(x1_in, 16)
            eng.dma_start(acc[0:TS, NC, :], scratch["x1"][SEQ:T, :]).then_inc(x1_in, 16)
            eng.dma_start(normw[:, :], i["norm3"]).then_inc(n3_in, 16)

            def pair(j):
                for s in range(2):
                    eng.wait_ge(gu_hi_done, 2 * j + s)
                    eng.wait_ge(gu_lo_done, 2 * j + s)
                    load_gu(j + 1, s)
                eng.wait_ge(dn_hi_done, 2 * j + 2)
                eng.wait_ge(dn_lo_done, 2 * j + 2)
                load_dn(j + 1)

            loop(eng, NP - 1, pair)
            for m in range(MT):
                n = P if m < NC else TS
                eng.wait_ge(y_done, m + 1)
                eng.dma_start(o["y"][m * P:m * P + n, :], y_out[m % 2][0:n, :]).then_inc(y_dma[m % 2], 16)
            eng.wait_ge(y_dma[0], 16 * (MT // 2 + 1))
            eng.wait_ge(y_dma[1], 16 * (MT // 2))

        @block.tensor
        def _(eng):
            def pair(j):
                for s in range(2):
                    eng.wait_ge(gu_hi_done, 2 * j + s)
                    eng.wait_ge(gu_lo_done, 2 * j + s)
                    for g, (a, m) in enumerate(GROUPS):
                        n = PAIR * j + NG * s + g
                        b = 2 * ((NG * s + g + 1) % 2)
                        if isinstance(j, int) and j == s == g == 0:
                            continue
                        if not first(n):
                            eng.wait_ge(hf_done, n - 1)
                        for q in range(2):
                            for f in range(KT):
                                mm = mm3(eng, psum[b + q][:, 0:m], gu_hi[s][:, q, f, :], gu_lo[s][:, q, f, :],
                                         ht_hi[:, f, a:a + m], ht_lo[:, f, a:a + m], f == 0, f == KT - 1)
                            mm.then_inc(gu_mm, 1)
                eng.wait_ge(dn_hi_done, 2 * j + 2)
                eng.wait_ge(dn_lo_done, 2 * j + 2)
                for m in range(MT):
                    n = P if m < NC else TS
                    toks = slice(m * P, m * P + n)
                    if m == 0 or group_of(m) != group_of(m - 1):
                        eng.wait_ge(h_lo_done, PAIR * j + NG + group_of(m) + 1)
                    for half in range(2):
                        cols = slice(half * BANK, (half + 1) * BANK)
                        eng.wait_ge(acc_done, SUMS * j + (2 * (m - 2) + half + 1 if m >= 2 else 0))
                        for s in range(2):
                            mm = mm3(eng, psum[4 + 2 * (m % 2) + half][0:n, :], h_hi[:, s, toks], h_lo[:, s, toks],
                                     dn_hi[:, s, cols], dn_lo[:, s, cols], s == 0, s == 1)
                        mm.then_inc(dn_mm, 1)

            loop(eng, NP, pair)

        @block.scalar
        def _(eng):
            def split_gu(j, s):
                eng.wait_ge(gu_in[s], 32 * (j + s))
                eng.wait_ge(gu_mm, 2 * PAIR * (j - 1) + 2 * NG * (s + 1))
                eng.activation(gu_hi[s][:, :, :, :], gu_raw[s][:, :, :, :], ACT.Copy).then_inc(gu_hi_done, 1)

            def split_dn(j):
                eng.wait_ge(dn_in, 32 * (j + 1))
                eng.wait_ge(dn_mm, SUMS * j)
                for s in range(2):
                    eng.activation(dn_hi[:, s, :], dn_raw[s][:, :], ACT.Copy).then_inc(dn_hi_done, 1)

            def pair(j, more):
                for s in range(2):
                    for g, (a, m) in enumerate(GROUPS):
                        n = PAIR * j + NG * s + g
                        b = (NG * s + g + 1) % 2
                        eng.wait_ge(gu_mm, 2 * n + 1)
                        if not first(n):
                            eng.wait_ge(hf_done, n - 1)
                        eng.activation(sg[b][:, 0:m], psum[2 * b][:, 0:m], ACT.Silu).then_inc(sg_done, 1)
                        eng.wait_ge(hf_done, n + 1)
                        eng.activation(h_hi[:, s, a:a + m], hf[b][:, 0:m], ACT.Copy).then_inc(h_hi_done, 1)
                        if s == 0 and g == 0:
                            if isinstance(j, int) and j == 0:
                                eng.wait_ge(gu_in[1], 32)
                                eng.activation(gu_hi[1][:, :, :, :], gu_raw[1][:, :, :, :],
                                               ACT.Copy).then_inc(gu_hi_done, 1)
                        if s == 0 and g == 1:
                            split_dn(j)
                    if more:
                        split_gu(j + 1, s)

            loop(eng, NP - 1, lambda j: pair(j, True))
            pair(NP - 1, False)
            for m in range(MT):
                n = P if m < NC else TS
                eng.wait_ge(acc_done, SUMS * (NP - 1) + 2 * m + 2)
                if m >= 2:
                    eng.wait_ge(y_dma[m % 2], 16 * (m // 2))
                eng.activation(y_out[m % 2][0:n, :], acc[0:n, m, :], ACT.Square, scale=D ** -0.5,
                               accum_out=fstat[0:n, m, 0:1]).then_inc(ssq, 1)

        @block.vector
        def _(eng):
            def split_gu(j, s):
                eng.wait_ge(gu_hi_done, 2 * j + s)
                eng.tensor_tensor(gu_lo[s][:, :, :, :], gu_raw[s][:, :, :, :], f32(gu_hi[s][:, :, :, :]),
                                  ALU.subtract).then_inc(gu_lo_done, 1)

            def norm_tile(m):
                n = P if m < NC else TS
                eng.wait_ge(n3_in, 16)
                eng.wait_ge(root, 2 * m + 2)
                eng.scalar_tensor_tensor(out=y_out[m % 2][0:n, :], in0=acc[0:n, m, :], scalar=fstat[0:n, m, 1:2],
                                         in1=normw[0:n, :], op0=ALU.mult, op1=ALU.mult).then_inc(y_done, 1)

            def pair(j, more):
                for s in range(2):
                    for g, (a, m) in enumerate(GROUPS):
                        n = PAIR * j + NG * s + g
                        b = (NG * s + g + 1) % 2
                        eng.wait_ge(gu_mm, 2 * n + 2)
                        eng.wait_ge(sg_done, n + 1)
                        if not first(n):
                            eng.wait_ge(h_lo_done, n - 1)
                        eng.tensor_tensor(hf[b][:, 0:m], sg[b][:, 0:m], psum[2 * b + 1][:, 0:m],
                                          ALU.mult).then_inc(hf_done, 1)
                        eng.wait_ge(h_hi_done, n + 1)
                        eng.tensor_tensor(h_lo[:, s, a:a + m], hf[b][:, 0:m], f32(h_hi[:, s, a:a + m]),
                                          ALU.subtract).then_inc(h_lo_done, 1)
                        if s == 0 and g == 0:
                            if isinstance(j, int) and j == 0:
                                split_gu(0, 1)
                        if s == 0 and g == 1:
                            for d in range(2):
                                eng.wait_ge(dn_hi_done, 2 * j + d + 1)
                                eng.tensor_tensor(dn_lo[:, d, :], dn_raw[d][:, :], f32(dn_hi[:, d, :]),
                                                  ALU.subtract).then_inc(dn_lo_done, 1)
                    if more:
                        split_gu(j + 1, s)
                if isinstance(j, int) and j == 0:
                    eng.wait_ge(x1_in, 32)
                for m in range(MT):
                    n = P if m < NC else TS
                    if not more and m >= 2:
                        norm_tile(m - 2)
                    for half in range(2):
                        part = acc[0:n, m, half * BANK:(half + 1) * BANK]
                        eng.wait_ge(dn_mm, SUMS * j + 2 * m + half + 1)
                        eng.tensor_tensor(part, part, psum[4 + 2 * (m % 2) + half][0:n, :],
                                          ALU.add).then_inc(acc_done, 1)

            loop(eng, NP - 1, lambda j: pair(j, True))
            pair(NP - 1, False)
            norm_tile(MT - 2)
            norm_tile(MT - 1)

        @block.gpsimd
        def _(eng):
            for m in range(MT):
                n = P if m < NC else TS
                eng.wait_ge(ssq, m + 1)
                eng.tensor_tensor(fstat[0:n, m, 0:1], fstat[0:n, m, 0:1], eps_col[0:n, :], ALU.add).then_inc(root, 1)
                eng.wait_ge(root, 2 * m + 1)
                eng.tensor_tensor(fstat[0:n, m, 1:2], fstat[0:n, m, 0:1], minus_half[0:n, :], ALU.pow).then_inc(root, 1)



def lay_out(v):
    f = lambda n: np.asarray(v[n], np.float32)
    c = np.ascontiguousarray
    tiles = lambda w: w.reshape(w.shape[0], -1, P)
    win = f("w_in")[0]
    dr = R * P
    cols = []
    for t in range(R):
        cols += [np.arange(t * P, (t + 1) * P), np.arange(dr + t * P, dr + (t + 1) * P)]
    z0 = 2 * dr + QKV * P
    cols += [np.arange(2 * dr + t * P, 2 * dr + (t + 1) * P) for t in range(QKV + H)]
    w4 = win.reshape(KT, P, -1)
    i = {"x": np.concatenate([f("x_prompt")[0], f("x_sample").reshape(TS, D)])}
    i["w_in"] = c(np.stack([w4[:, :, cc].transpose(1, 0, 2) for cc in cols]))
    i["w_gates"] = c(w4[:, :, z0 + H * P:].transpose(1, 0, 2))
    i["w_out"] = f("w_out")[0].reshape(KT, P, D)
    for n, s in (("norm1", f("norm1")[0]), ("norm2", f("norm2")[0]), ("norm3", f("final_norm"))):
        i[n] = c(np.broadcast_to(s, (P, D)))
    feat = lambda a: c(a.reshape(a.shape[:-1] + (-1, P)))
    i["rg_par"] = c(np.stack([*feat(f("rg_conv_w")[0]), feat(f("rg_conv_b")[0]), feat(f("rg_ba")[0]),
                              feat(f("rg_bi")[0]), feat(f("rg_lambda")[0])]).transpose(2, 0, 1))
    i["rg_h0"] = c(feat(f("state_rglru_h")[0]).transpose(2, 1, 0))
    i["hist_rg"] = c(feat(f("state_rglru_conv")[0]).transpose(3, 2, 0, 1).reshape(P, R, NS * HIST))
    i["hist_g"] = c(feat(f("state_gdn_conv")[0]).transpose(3, 2, 0, 1).reshape(P, QKV, NS * HIST))
    i["conv_w"] = c(feat(f("gdn_conv_w")[0]).transpose(2, 1, 0))
    i["alog"] = c(np.broadcast_to(np.concatenate([f("gdn_A_log")[0], f("gdn_dt_bias")[0]]), (P, 2 * H)))
    rw = np.zeros((R, P, 2, P), np.float32)
    half = P // 2
    for q, n in enumerate(("rg_wa", "rg_wi")):
        for b in range(2 * R):
            s = b % 2 * half
            rw[b // 2, s:s + half, q, s:s + half] = f(n)[0][b]
    i["rg_w"] = rw
    i["gnw"] = c(f("gdn_norm_w")[0][:, None])
    i["state_S"] = c(f("state_gdn_S")[0].transpose(1, 2, 0, 3))
    i["w_gate"] = c(f("w_gate")[0].reshape(KT, P, FT, P).transpose(2, 1, 0, 3))
    i["w_up"] = c(f("w_up")[0].reshape(KT, P, FT, P).transpose(2, 1, 0, 3))
    i["w_down"] = f("w_down")[0].reshape(FT, P, D)
    i["expo"] = c(np.broadcast_to(np.array([-0.5] * 2 * H + [EPS] * H, np.float32), (P, 3 * H)))
    a, b = np.arange(P)[:, None], np.arange(P)[None, :]
    masks = [a == b, a <= b, a > b, a < b, a >= 0 * b]
    masks += [(a // (2 * n) == b // (2 * n)) & (a // n % 2 == 1) & (b // n % 2 == 0) for n in LEVELS]
    i["cst"] = c(np.stack([np.broadcast_to(m, (P, P)) for m in masks], 1).astype(np.float32))
    same = (a // LS == b // LS)[:TS, :TS]
    sm = [m[:TS, :TS] & same for m in masks[1:4]] + [(a // LS == b)[:TS, :NS]]
    i["cs"] = c(np.concatenate(sm, 1).astype(np.float32))
    return i


_OUTS = {"y": (T, D), "st_rg": (P, R, (1 + NS) * HIST), "st_h": (P, R, 1 + NS), "st_g": (P, QKV, (1 + NS) * HIST),
         "S_prompt": (P, H, P), "S_sample": (H, P, NS, P)}
_SCRATCH = {"rg": (R, P, SEQ), "z": (H, P, SEQ), "qkv": (QKV, P, SEQ), "x1": (T, D)}


def kernel(**inputs):
    import concourse.bacc as bacc
    from concourse.bass_utils import run_bass_kernel_spmd

    nc = bacc.Bacc("TRN2", target_bir_lowering=False, num_devices=1)
    arrays = {f"in_{n}": a for n, a in lay_out(inputs).items()}
    i = {n[3:]: nc.dram_tensor(n, a.shape, F32, kind="ExternalInput").ap() for n, a in arrays.items()}
    o = {n: nc.dram_tensor(f"out_{n}", s, F32, kind="ExternalOutput").ap() for n, s in _OUTS.items()}
    scratch = {n: nc.dram_tensor(f"scratch_{n}", s, F32, kind="Internal").ap() for n, s in _SCRATCH.items()}
    build(nc, i, o, scratch)
    r = run_bass_kernel_spmd(nc, [arrays], core_ids=[0]).results[0]
    y, rg, h, gd, sp, ss = (r[f"out_{n}"] for n in _OUTS)
    c = np.ascontiguousarray

    def rows(a):
        return c(a.reshape(P, -1, 1 + NS, HIST).transpose(2, 3, 1, 0).reshape(1, 1 + NS, HIST, -1))

    rc, gc = rows(rg), rows(gd)
    hh = c(h.transpose(2, 1, 0).reshape(1, 1 + NS, -1))
    return (c(y[:SEQ].reshape(1, SEQ, D)), c(y[SEQ:].reshape(NS, LS, D)),
            c(rc[:, :1]), c(hh[:, :1]), c(gc[:, :1]), c(sp.transpose(1, 0, 2)[None, None]),
            c(rc[:, 1:]), c(hh[:, 1:]), c(gc[:, 1:]), c(ss.transpose(2, 0, 1, 3)[None]))
```
